# Optimizing a Trainium2 kernel written in Bass

```python
import math
import jax, jax.numpy as jnp
from jax import lax
import numpy as np

D_MODEL = 1024
BATCH = 1
SEQ = 256
DEPTH = 2

HEAD_DIM = 64
ROPE_DIM = HEAD_DIM // 4
ROPE_THETA = 500000.0
Q_BLOCK = 128
LN_EPS = 1e-5
DIFF_HEADS = 4
NSA_HEADS = 8
NSA_KV_HEADS = 2
NSA_CMP_LEN = 32
NSA_CMP_STRIDE = 16
NSA_CMP_HIDDEN = 256
NSA_SEL_LEN = 64
NSA_TOPK = 8
NSA_WINDOW = 512
NSA_Q_BLOCK = 64
NSA_N_BRANCH = 3
NSA_BIG = 1e4
NEG = -1e30
FOX_HEADS = D_MODEL // HEAD_DIM
FOX_WIDTH = FOX_HEADS * HEAD_DIM
D_FF = 4 * D_MODEL
ALPHA = (2 * DEPTH) ** 0.25
BETA = (8 * DEPTH) ** -0.25
N_EVEN = (DEPTH + 1) // 2
N_ODD = DEPTH // 2

DIFF_QK = DIFF_HEADS * 2 * HEAD_DIM
DIFF_V = DIFF_HEADS * 2 * HEAD_DIM
NSA_Q = NSA_HEADS * HEAD_DIM
NSA_KV = NSA_KV_HEADS * HEAD_DIM
EVEN_SPLITS = (DIFF_QK, DIFF_QK, DIFF_V, NSA_Q, NSA_KV, NSA_KV, NSA_KV, NSA_KV, NSA_KV, NSA_KV, NSA_HEADS * NSA_N_BRANCH)
EVEN_COLS = sum(EVEN_SPLITS)
EVEN_MIX = DIFF_V + NSA_Q
ODD_SPLITS = (FOX_WIDTH, FOX_WIDTH, FOX_WIDTH, FOX_HEADS)
ODD_COLS = sum(ODD_SPLITS)


def _split(h, sizes):
    offsets = [int(o) for o in np.cumsum(sizes)[:-1]]
    return jnp.split(h, offsets, axis=-1)

def layer_norm(x, g, b):
    xf = x.astype(jnp.float32)
    mu = jnp.mean(xf, axis=-1, keepdims=True)
    var = jnp.mean(jnp.square(xf - mu), axis=-1, keepdims=True)
    return ((xf - mu) * lax.rsqrt(var + LN_EPS) * g.astype(jnp.float32) + b.astype(jnp.float32)).astype(x.dtype)

def rms_norm(x, g):
    xf = x.astype(jnp.float32)
    return xf * lax.rsqrt(jnp.mean(jnp.square(xf), axis=-1, keepdims=True) + LN_EPS) * g.astype(jnp.float32)

def partial_rope(x, pos):
    half = ROPE_DIM // 2
    inv = ROPE_THETA ** (-jnp.arange(half, dtype=jnp.float32) / half)
    ang = pos.astype(jnp.float32)[:, None] * inv[None, :]
    shape = (pos.shape[0],) + (1,) * (x.ndim - 3) + (half,)
    cos = jnp.cos(ang).reshape(shape)
    sin = jnp.sin(ang).reshape(shape)
    xf = x.astype(jnp.float32)
    x1 = xf[..., :half]
    x2 = xf[..., half:ROPE_DIM]
    return jnp.concatenate([x1 * cos - x2 * sin, x2 * cos + x1 * sin, xf[..., ROPE_DIM:]], axis=-1)

def _sweep(fn, seq_len, block):
    out = lax.map(fn, jnp.arange(seq_len // block))
    out = jnp.moveaxis(out, 0, 1)
    return out.reshape((out.shape[0], seq_len) + out.shape[3:])

def diff_attention(q, k, v, lam_params, subln_g, layer_idx):
    B, S = q.shape[:2]
    pos = jnp.arange(S)
    scale = HEAD_DIM ** -0.5
    qr = partial_rope(q, pos) * scale
    kr = partial_rope(k, pos)
    vf = v.astype(jnp.float32)
    lam_init = 0.8 - 0.6 * math.exp(-0.3 * layer_idx)
    lp = lam_params.astype(jnp.float32)
    lam = jnp.exp(jnp.sum(lp[0] * lp[1])) - jnp.exp(jnp.sum(lp[2] * lp[3])) + lam_init

    def blk(i):
        q0 = i * Q_BLOCK
        qb = lax.dynamic_slice_in_dim(qr, q0, Q_BLOCK, axis=1)
        tq = q0 + jnp.arange(Q_BLOCK)
        mask = pos[None, :] <= tq[:, None]
        s = jnp.einsum('bqhcd,bshcd->bhcqs', qb, kr)
        p = jax.nn.softmax(jnp.where(mask, s, -jnp.inf), axis=-1)
        pd = p[:, :, 0] - lam * p[:, :, 1]
        return jnp.einsum('bhqs,bshe->bqhe', pd, vf)

    o = _sweep(blk, S, Q_BLOCK)
    o = rms_norm(o, subln_g) * (1.0 - lam_init)
    return o.reshape(B, S, -1).astype(v.dtype)

def nsa_attention(q, k_cmp, v_cmp, k_slc, v_slc, k_win, v_win, gate_logits, pe, w1, b1, w2):
    B, S, H, d = q.shape
    G = NSA_KV_HEADS
    HPG = H // G
    W = NSA_WINDOW
    pos = jnp.arange(S)
    scale = HEAD_DIM ** -0.5
    qr = (partial_rope(q, pos) * scale).reshape(B, S, G, HPG, d)

    n_cmp = (S - NSA_CMP_LEN) // NSA_CMP_STRIDE + 1
    cmp_start = jnp.arange(n_cmp) * NSA_CMP_STRIDE
    cmp_end = cmp_start + NSA_CMP_LEN - 1
    cmp_idx = cmp_start[:, None] + jnp.arange(NSA_CMP_LEN)[None, :]

    def compress(t, j):
        blocks = t[:, cmp_idx] + pe[j][None, None, :, None, :]
        blocks = jnp.moveaxis(blocks, 3, 2).reshape(B, n_cmp, G, NSA_CMP_LEN * d)
        h = jax.nn.gelu(blocks @ w1[j] + b1[j])
        return h @ w2[j]

    kc = partial_rope(compress(k_cmp, 0), cmp_end)
    vc = compress(v_cmp, 1).astype(jnp.float32)

    n_sel = S // NSA_SEL_LEN
    topk = min(NSA_TOPK, n_sel)
    ks = partial_rope(k_slc, pos)
    ks_blk = ks.reshape(B, n_sel, NSA_SEL_LEN, G, d).transpose(0, 3, 1, 2, 4)
    vs_blk = v_slc.astype(jnp.float32).reshape(B, n_sel, NSA_SEL_LEN, G, d).transpose(0, 3, 1, 2, 4)
    sel_start = jnp.arange(n_sel) * NSA_SEL_LEN
    overlap = ((cmp_start[:, None] <= sel_start[None, :] + NSA_SEL_LEN - 1)
               & (cmp_end[:, None] >= sel_start[None, :])).astype(jnp.float32)
    bi = jnp.arange(B)[:, None, None, None]
    gi = jnp.arange(G)[None, :, None, None]
    jb = jnp.arange(n_sel)

    kw_pad = jnp.pad(partial_rope(k_win, pos), ((0, 0), (W, 0), (0, 0), (0, 0)))
    vw_pad = jnp.pad(v_win.astype(jnp.float32), ((0, 0), (W, 0), (0, 0), (0, 0)))

    gate = jax.nn.sigmoid(gate_logits.astype(jnp.float32)).reshape(B, S, G, HPG, NSA_N_BRANCH)

    def blk(i):
        q0 = i * NSA_Q_BLOCK
        qb = lax.dynamic_slice_in_dim(qr, q0, NSA_Q_BLOCK, axis=1)
        tq = q0 + jnp.arange(NSA_Q_BLOCK)
        valid_c = cmp_end[None, :] <= tq[:, None]
        sc = jnp.einsum('bqghd,bngd->bghqn', qb, kc)
        pc = jax.nn.softmax(jnp.where(valid_c, sc, NEG), axis=-1) * valid_c
        o_c = jnp.einsum('bghqn,bngd->bqghd', pc, vc)
        imp = jnp.einsum('bghqn,nj->bgqj', pc, overlap)
        cur = tq // NSA_SEL_LEN
        forced = (jb[None, :] == 0) | (jb[None, :] == cur[:, None]) | (jb[None, :] == cur[:, None] - 1)
        future = jb[None, :] > cur[:, None]
        imp = jnp.where(forced, NSA_BIG, jnp.where(future, -NSA_BIG, imp))
        _, idx = lax.top_k(imp, topk)
        kg = ks_blk[bi, gi, idx]
        vg = vs_blk[bi, gi, idx]
        tok = idx[..., None] * NSA_SEL_LEN + jnp.arange(NSA_SEL_LEN)
        valid_s = (tok <= tq[None, None, :, None, None])[:, :, None]
        ss = jnp.where(valid_s, jnp.einsum('bqghd,bgqkld->bghqkl', qb, kg), -jnp.inf)
        ps = jax.nn.softmax(ss.reshape(ss.shape[:4] + (-1,)), axis=-1).reshape(ss.shape)
        o_s = jnp.einsum('bghqkl,bgqkld->bqghd', ps, vg)
        kwb = lax.dynamic_slice_in_dim(kw_pad, q0, W + NSA_Q_BLOCK, axis=1)
        vwb = lax.dynamic_slice_in_dim(vw_pad, q0, W + NSA_Q_BLOCK, axis=1)
        sk = q0 - W + jnp.arange(W + NSA_Q_BLOCK)
        valid_w = (sk[None, :] <= tq[:, None]) & (sk[None, :] > tq[:, None] - W) & (sk[None, :] >= 0)
        sw = jnp.einsum('bqghd,bsgd->bghqs', qb, kwb)
        pw = jax.nn.softmax(jnp.where(valid_w, sw, -jnp.inf), axis=-1)
        o_w = jnp.einsum('bghqs,bsgd->bqghd', pw, vwb)
        gb = lax.dynamic_slice_in_dim(gate, q0, NSA_Q_BLOCK, axis=1)
        return gb[..., 0:1] * o_c + gb[..., 1:2] * o_s + gb[..., 2:3] * o_w

    o = _sweep(blk, S, NSA_Q_BLOCK)
    return o.reshape(B, S, H * d).astype(q.dtype)

def forgetting_attention(q, k, v, f_logit, f_bias):
    B, S, H, d = q.shape
    pos = jnp.arange(S)
    qf = q.astype(jnp.float32) * (HEAD_DIM ** -0.5)
    kf = k.astype(jnp.float32)
    vf = v.astype(jnp.float32)
    log_f = jax.nn.log_sigmoid(f_logit.astype(jnp.float32) + f_bias.astype(jnp.float32))
    c = jnp.cumsum(log_f, axis=1).transpose(0, 2, 1)

    def blk(i):
        q0 = i * Q_BLOCK
        qb = lax.dynamic_slice_in_dim(qf, q0, Q_BLOCK, axis=1)
        cq = lax.dynamic_slice_in_dim(c, q0, Q_BLOCK, axis=2)
        tq = q0 + jnp.arange(Q_BLOCK)
        mask = pos[None, :] <= tq[:, None]
        s = jnp.einsum('bqhd,bshd->bhqs', qb, kf) + cq[..., None] - c[:, :, None, :]
        p = jax.nn.softmax(jnp.where(mask, s, -jnp.inf), axis=-1)
        return jnp.einsum('bhqs,bshd->bqhd', p, vf)

    o = _sweep(blk, S, Q_BLOCK)
    return o.reshape(B, S, H * d).astype(q.dtype)

def sqrelu_mlp(x, w_up, w_down):
    return jnp.square(jax.nn.relu(x @ w_up)) @ w_down

def first_inputs(seed: int = 0) -> dict:
    key = jax.random.key(seed)
    ks = jax.random.split(key, 16)

    def nrm(k, shape, scale):
        return jax.random.normal(k, shape, jnp.float32) * scale

    return {
        'x': nrm(ks[0], (BATCH, SEQ, D_MODEL), 1.0),
        'ln_gain': 1.0 + nrm(ks[1], (DEPTH, 2, D_MODEL), 0.02),
        'ln_bias': nrm(ks[2], (DEPTH, 2, D_MODEL), 0.02),
        'mlp_w_up': nrm(ks[3], (DEPTH, D_MODEL, D_FF), D_MODEL ** -0.5),
        'mlp_w_down': nrm(ks[4], (DEPTH, D_FF, D_MODEL), BETA * D_FF ** -0.5),
        'w_in_even': nrm(ks[5], (N_EVEN, D_MODEL, EVEN_COLS), D_MODEL ** -0.5),
        'w_out_even': nrm(ks[6], (N_EVEN, EVEN_MIX, D_MODEL), BETA * EVEN_MIX ** -0.5),
        'diff_lambda': nrm(ks[7], (N_EVEN, 4, HEAD_DIM), 0.1),
        'diff_subln': 1.0 + nrm(ks[8], (N_EVEN, 2 * HEAD_DIM), 0.02),
        'nsa_pe': nrm(ks[9], (N_EVEN, 2, NSA_CMP_LEN, HEAD_DIM), 0.1),
        'nsa_cmp_w1': nrm(ks[10], (N_EVEN, 2, NSA_CMP_LEN * HEAD_DIM, NSA_CMP_HIDDEN), (NSA_CMP_LEN * HEAD_DIM) ** -0.5),
        'nsa_cmp_b1': nrm(ks[11], (N_EVEN, 2, NSA_CMP_HIDDEN), 0.02),
        'nsa_cmp_w2': nrm(ks[12], (N_EVEN, 2, NSA_CMP_HIDDEN, HEAD_DIM), NSA_CMP_HIDDEN ** -0.5),
        'w_in_odd': nrm(ks[13], (N_ODD, D_MODEL, ODD_COLS), D_MODEL ** -0.5),
        'fox_f_bias': jnp.linspace(1.0, 6.0, FOX_HEADS, dtype=jnp.float32)[None, :] + nrm(ks[14], (N_ODD, FOX_HEADS), 0.1),
        'w_out_odd': nrm(ks[15], (N_ODD, FOX_WIDTH, D_MODEL), BETA * FOX_WIDTH ** -0.5),
    }

def first_block(x, ln_gain, ln_bias, mlp_w_up, mlp_w_down, w_in_even, w_out_even, diff_lambda, diff_subln,
              nsa_pe, nsa_cmp_w1, nsa_cmp_b1, nsa_cmp_w2, w_in_odd, fox_f_bias, w_out_odd):
    B, S, _ = x.shape
    for layer in range(DEPTH):
        li = layer // 2
        if layer % 2 == 0:
            h = x @ w_in_even[li]
            qa, ka, va, qn, kc, vc, ksl, vsl, kw, vw, g = _split(h, EVEN_SPLITS)
            o_a = diff_attention(qa.reshape(B, S, DIFF_HEADS, 2, HEAD_DIM),
                                 ka.reshape(B, S, DIFF_HEADS, 2, HEAD_DIM),
                                 va.reshape(B, S, DIFF_HEADS, 2 * HEAD_DIM),
                                 diff_lambda[li], diff_subln[li], layer)
            kv = lambda t: t.reshape(B, S, NSA_KV_HEADS, HEAD_DIM)
            o_b = nsa_attention(qn.reshape(B, S, NSA_HEADS, HEAD_DIM), kv(kc), kv(vc), kv(ksl), kv(vsl),
                                kv(kw), kv(vw), g, nsa_pe[li], nsa_cmp_w1[li], nsa_cmp_b1[li], nsa_cmp_w2[li])
            mix = jnp.concatenate([o_a, o_b], axis=-1) @ w_out_even[li]
        else:
            h = x @ w_in_odd[li]
            qf, kf, vf, fl = _split(h, ODD_SPLITS)
            hd = lambda t: t.reshape(B, S, FOX_HEADS, HEAD_DIM)
            mix = forgetting_attention(hd(qf), hd(kf), hd(vf), fl, fox_f_bias[li]) @ w_out_odd[li]
        x = layer_norm(ALPHA * x + mix, ln_gain[layer, 0], ln_bias[layer, 0])
        x = layer_norm(ALPHA * x + sqrelu_mlp(x, mlp_w_up[layer], mlp_w_down[layer]), ln_gain[layer, 1], ln_bias[layer, 1])
    return x


DEPTH_2 = 1

GRID_W = 64
CTX_LEN = 256
N_HEADS = 8
N_KV_HEADS = 2
KV_GROUP = N_HEADS // N_KV_HEADS
ATTN_WIDTH = N_HEADS * HEAD_DIM
KV_WIDTH = N_KV_HEADS * HEAD_DIM
WINDOW = 128
BLOCK = 128
ROPE_THETA_2 = 10000.0
POOL_WINDOWS = (2, 4, 8, 16)
N_POOL_GROUPS = 4
POOL_WIDTH = D_MODEL - ATTN_WIDTH
POOL_GROUP_DIM = POOL_WIDTH // N_POOL_GROUPS
MIX_WIDTH = ATTN_WIDTH + POOL_WIDTH
IN_COLS = ATTN_WIDTH + 2 * KV_WIDTH + POOL_WIDTH
N_EXPERTS = 64
TOP_K = 8
N_EXPERT_GROUPS = 8
EXPERTS_PER_GROUP = N_EXPERTS // N_EXPERT_GROUPS
TOPK_GROUPS = 4
D_EXPERT = 256
D_SHARED = 256
ROUTED_SCALE = 2.5
EXPERT_BLOCK = 128
EPS = 1e-6


F32 = jnp.float32

def rmsnorm(x, g):
    x32 = x.astype(F32)
    y = x32 * lax.rsqrt(jnp.mean(x32 * x32, axis=-1, keepdims=True) + EPS)
    return (y * g.astype(F32)).astype(x.dtype)

def modulate(h, shift, scale):
    return h * (1 + scale) + shift

def axial_rope_tables(n_tokens):
    rows = n_tokens // GRID_W
    row = jnp.repeat(jnp.arange(rows), GRID_W).astype(F32)
    col = jnp.tile(jnp.arange(GRID_W), rows).astype(F32)
    n_freq = HEAD_DIM // 4
    inv_freq = ROPE_THETA_2 ** (-jnp.arange(n_freq, dtype=F32) / n_freq)
    ang_r = row[:, None] * inv_freq[None, :]
    ang_c = col[:, None] * inv_freq[None, :]
    return jnp.cos(ang_r), jnp.sin(ang_r), jnp.cos(ang_c), jnp.sin(ang_c)

def _rope_half(x, cos, sin):
    x1, x2 = jnp.split(x, 2, axis=-1)
    cos = cos[:, None, :]
    sin = sin[:, None, :]
    return jnp.concatenate([x1 * cos - x2 * sin, x1 * sin + x2 * cos], axis=-1)

def apply_axial_rope(x, tables):
    cos_r, sin_r, cos_c, sin_c = tables
    xr, xc = jnp.split(x.astype(F32), 2, axis=-1)
    return jnp.concatenate([_rope_half(xr, cos_r, sin_r), _rope_half(xc, cos_c, sin_c)], axis=-1).astype(x.dtype)

def split_projection(z):
    B, L = z.shape[:2]
    q = z[..., :ATTN_WIDTH].reshape(B, L, N_HEADS, HEAD_DIM)
    k = z[..., ATTN_WIDTH:ATTN_WIDTH + KV_WIDTH].reshape(B, L, N_KV_HEADS, HEAD_DIM)
    v = z[..., ATTN_WIDTH + KV_WIDTH:ATTN_WIDTH + 2 * KV_WIDTH].reshape(B, L, N_KV_HEADS, HEAD_DIM)
    p = z[..., ATTN_WIDTH + 2 * KV_WIDTH:]
    return q, k, v, p

def split_kv(z):
    B, L = z.shape[:2]
    k = z[..., :KV_WIDTH].reshape(B, L, N_KV_HEADS, HEAD_DIM)
    v = z[..., KV_WIDTH:].reshape(B, L, N_KV_HEADS, HEAD_DIM)
    return k, v

def latent_window_attention(q, k, v, k_ctx, v_ctx, sink):
    B, S = q.shape[:2]
    nb = S // BLOCK
    scale = HEAD_DIM ** -0.5
    qb = q.reshape(B, nb, BLOCK, N_KV_HEADS, KV_GROUP, HEAD_DIM)

    def band(t):
        tp = jnp.pad(t, ((0, 0), (BLOCK, BLOCK), (0, 0), (0, 0))).reshape(B, nb + 2, BLOCK, N_KV_HEADS, HEAD_DIM)
        return jnp.concatenate([tp[:, :-2], tp[:, 1:-1], tp[:, 2:]], axis=2)

    kb, vb = band(k), band(v)
    s_loc = jnp.einsum('bnqkgd,bnjkd->bnkgqj', qb, kb, preferred_element_type=F32) * scale
    s_ctx = jnp.einsum('bnqkgd,bckd->bnkgqc', qb, k_ctx, preferred_element_type=F32) * scale
    q_pos = jnp.arange(nb)[:, None, None] * BLOCK + jnp.arange(BLOCK)[None, :, None]
    k_pos = jnp.arange(nb)[:, None, None] * BLOCK - BLOCK + jnp.arange(3 * BLOCK)[None, None, :]
    allowed = (jnp.abs(q_pos - k_pos) <= WINDOW) & (k_pos >= 0) & (k_pos < S)
    s_loc = jnp.where(allowed[None, :, None, None], s_loc, -jnp.inf)
    sink_l = sink.astype(F32).reshape(1, 1, N_KV_HEADS, KV_GROUP, 1, 1)
    m = jnp.maximum(jnp.maximum(s_loc.max(-1, keepdims=True), s_ctx.max(-1, keepdims=True)), sink_l)
    p_loc = jnp.exp(s_loc - m)
    p_ctx = jnp.exp(s_ctx - m)
    denom = p_loc.sum(-1, keepdims=True) + p_ctx.sum(-1, keepdims=True) + jnp.exp(sink_l - m)
    o = (jnp.einsum('bnkgqj,bnjkd->bnkgqd', p_loc, vb.astype(F32))
         + jnp.einsum('bnkgqc,bckd->bnkgqd', p_ctx, v_ctx.astype(F32))) / denom
    o = o.transpose(0, 1, 4, 2, 3, 5).reshape(B, S, ATTN_WIDTH)
    return o.astype(q.dtype)

def context_attention(q, k, v, sink):
    B, C = q.shape[:2]
    scale = HEAD_DIM ** -0.5
    qc = q.reshape(B, C, N_KV_HEADS, KV_GROUP, HEAD_DIM)
    s = jnp.einsum('bqkgd,bckd->bkgqc', qc, k, preferred_element_type=F32) * scale
    sink_l = sink.astype(F32).reshape(1, N_KV_HEADS, KV_GROUP, 1, 1)
    m = jnp.maximum(s.max(-1, keepdims=True), sink_l)
    p = jnp.exp(s - m)
    denom = p.sum(-1, keepdims=True) + jnp.exp(sink_l - m)
    o = jnp.einsum('bkgqc,bckd->bkgqd', p, v.astype(F32)) / denom
    return o.transpose(0, 3, 1, 2, 4).reshape(B, C, ATTN_WIDTH).astype(q.dtype)

def multiscale_pool(p, pool_w, pool_scale):
    B, L, _ = p.shape
    p32 = p.astype(F32)
    cs = jnp.concatenate([jnp.zeros((B, 1, POOL_WIDTH), F32), jnp.cumsum(p32, axis=1)], axis=1)
    t = jnp.arange(L)
    outs = []
    for g, w in enumerate(POOL_WINDOWS):
        lo = jnp.clip(t - w // 2, 0, L)
        hi = jnp.clip(t - w // 2 + w, 0, L)
        sl = slice(g * POOL_GROUP_DIM, (g + 1) * POOL_GROUP_DIM)
        csg = cs[:, :, sl]
        mean = (csg[:, hi] - csg[:, lo]) / (hi - lo).astype(F32)[None, :, None]
        outs.append(mean - p32[:, :, sl])
    d = jnp.stack(outs, axis=2)
    y = jnp.einsum('blgc,gcd->blgd', d, pool_w.astype(F32)).reshape(B, L, POOL_WIDTH)
    return (y * pool_scale.astype(F32)).astype(p.dtype)

def routed_experts(h, idx, gate, w_gate, w_up, w_down):
    T, D = h.shape
    TK = T * TOP_K
    flat_e = idx.reshape(TK)
    flat_w = gate.reshape(TK)
    order = jnp.argsort(flat_e)
    e_sorted = flat_e[order]
    sizes = jnp.bincount(flat_e, length=N_EXPERTS)
    padded = (sizes + EXPERT_BLOCK - 1) // EXPERT_BLOCK * EXPERT_BLOCK
    pad_end = jnp.cumsum(padded)
    pad_start = pad_end - padded
    start = jnp.cumsum(sizes) - sizes
    dest = pad_start[e_sorted] + (jnp.arange(TK) - start[e_sorted])
    n_rows = -(-(TK + N_EXPERTS * (EXPERT_BLOCK - 1)) // EXPERT_BLOCK) * EXPERT_BLOCK
    n_blocks = n_rows // EXPERT_BLOCK
    row_tok = jnp.zeros((n_rows,), jnp.int32).at[dest].set((order // TOP_K).astype(jnp.int32))
    row_w = jnp.zeros((n_rows,), F32).at[dest].set(flat_w[order])
    block_e = jnp.minimum(jnp.searchsorted(pad_end, jnp.arange(n_blocks) * EXPERT_BLOCK, side='right'),
                          N_EXPERTS - 1)

    def expert_block(args):
        tok_b, w_b, e = args
        xb = h[tok_b]
        y = (jax.nn.silu(xb @ w_gate[e]) * (xb @ w_up[e])) @ w_down[e]
        return y.astype(F32) * w_b[:, None]

    y_rows = lax.map(expert_block, (row_tok.reshape(n_blocks, EXPERT_BLOCK),
                                    row_w.reshape(n_blocks, EXPERT_BLOCK), block_e))
    return jnp.zeros((T, D), F32).at[row_tok].add(y_rows.reshape(n_rows, D))

def moe_ffn(h, w_router, router_bias, w_gate, w_up, w_down, ws_gate, ws_up, ws_down):
    T = h.shape[0]
    scores = jax.nn.sigmoid(jnp.dot(h, w_router, preferred_element_type=F32))
    biased = scores + router_bias.astype(F32)
    grp_score = lax.top_k(biased.reshape(T, N_EXPERT_GROUPS, EXPERTS_PER_GROUP), 2)[0].sum(-1)
    _, top_grp = lax.top_k(grp_score, TOPK_GROUPS)
    grp_mask = jnp.any(top_grp[:, :, None] == jnp.arange(N_EXPERT_GROUPS)[None, None, :], axis=1)
    expert_mask = jnp.repeat(grp_mask, EXPERTS_PER_GROUP, axis=1)
    _, idx = lax.top_k(jnp.where(expert_mask, biased, -jnp.inf), TOP_K)
    gate = jnp.take_along_axis(scores, idx, axis=1)
    gate = gate / jnp.sum(gate, axis=-1, keepdims=True) * ROUTED_SCALE
    routed = routed_experts(h, idx, gate, w_gate, w_up, w_down)
    shared = (jax.nn.silu(h @ ws_gate) * (h @ ws_up)) @ ws_down
    return (routed + shared.astype(F32)).astype(h.dtype)

def second_inputs(seed: int = 0) -> dict:
    key = jax.random.key(seed)
    ks = jax.random.split(key, 24)
    D, L = D_MODEL, DEPTH_2

    def nrm(k, shape, scale):
        return jax.random.normal(k, shape, F32) * scale

    return {
        "x": nrm(ks[0], (BATCH, SEQ, D), 1.0),
        "c": nrm(ks[1], (BATCH, D), 1.0),
        "ctx": nrm(ks[2], (BATCH, CTX_LEN, D), 1.0),
        "c_ctx": nrm(ks[3], (D,), 1.0),
        "w_ada": nrm(ks[4], (L, D, 6 * D), 0.5 * D ** -0.5),
        "b_ada": nrm(ks[5], (L, 6 * D), 0.02),
        "norm1_g": 1.0 + nrm(ks[6], (L, D), 0.05),
        "norm2_g": 1.0 + nrm(ks[7], (L, D), 0.05),
        "w_in": nrm(ks[8], (L, D, IN_COLS), D ** -0.5),
        "attn_sink": nrm(ks[9], (L, N_HEADS), 0.5),
        "pool_w": nrm(ks[10], (L, N_POOL_GROUPS, POOL_GROUP_DIM, POOL_GROUP_DIM), POOL_GROUP_DIM ** -0.5),
        "pool_scale": 1.0 + nrm(ks[11], (L, POOL_WIDTH), 0.1),
        "w_out": nrm(ks[12], (L, MIX_WIDTH, D), MIX_WIDTH ** -0.5),
        "w_router": nrm(ks[13], (L, D, N_EXPERTS), D ** -0.5),
        "router_bias": nrm(ks[14], (L, N_EXPERTS), 0.01),
        "w_gate": nrm(ks[15], (L, N_EXPERTS, D, D_EXPERT), D ** -0.5),
        "w_up": nrm(ks[16], (L, N_EXPERTS, D, D_EXPERT), D ** -0.5),
        "w_down": nrm(ks[17], (L, N_EXPERTS, D_EXPERT, D), D_EXPERT ** -0.5),
        "ws_gate": nrm(ks[18], (L, D, D_SHARED), D ** -0.5),
        "ws_up": nrm(ks[19], (L, D, D_SHARED), D ** -0.5),
        "ws_down": nrm(ks[20], (L, D_SHARED, D), D_SHARED ** -0.5),
        "final_g": 1.0 + nrm(ks[21], (D,), 0.05),
    }

def second_block(x, c, ctx, c_ctx, w_ada, b_ada, norm1_g, norm2_g, w_in, attn_sink, pool_w, pool_scale,
              w_out, w_router, router_bias, w_gate, w_up, w_down, ws_gate, ws_up, ws_down, final_g):
    B, S, D = x.shape
    rope = axial_rope_tables(S)
    silu_c = jax.nn.silu(c)
    silu_cc = jax.nn.silu(c_ctx)
    for l in range(DEPTH_2):
        last = l == DEPTH_2 - 1
        mod = silu_c @ w_ada[l] + b_ada[l]
        mod_c = silu_cc @ w_ada[l] + b_ada[l]
        sh1, sc1, g1, sh2, sc2, g2 = jnp.split(mod[:, None, :], 6, axis=-1)
        sh1c, sc1c, g1c, sh2c, sc2c, g2c = jnp.split(mod_c, 6)

        hx = modulate(rmsnorm(x, norm1_g[l]), sh1, sc1)
        hc = modulate(rmsnorm(ctx, norm1_g[l]), sh1c, sc1c)
        qx, kx, vx, px = split_projection(hx @ w_in[l])
        qx = apply_axial_rope(qx, rope)
        kx = apply_axial_rope(kx, rope)
        if last:
            kc, vc = split_kv(hc @ w_in[l][:, ATTN_WIDTH:ATTN_WIDTH + 2 * KV_WIDTH])
        else:
            qc, kc, vc, pc = split_projection(hc @ w_in[l])
        attn_x = latent_window_attention(qx, kx, vx, kc, vc, attn_sink[l])
        pool_x = multiscale_pool(px, pool_w[l], pool_scale[l])
        x = x + g1 * (jnp.concatenate([attn_x, pool_x], axis=-1) @ w_out[l])
        if not last:
            attn_c = context_attention(qc, kc, vc, attn_sink[l])
            pool_c = multiscale_pool(pc, pool_w[l], pool_scale[l])
            ctx = ctx + g1c * (jnp.concatenate([attn_c, pool_c], axis=-1) @ w_out[l])

        hx2 = modulate(rmsnorm(x, norm2_g[l]), sh2, sc2)
        ffn_x = moe_ffn(hx2.reshape(B * S, D), w_router[l], router_bias[l], w_gate[l], w_up[l], w_down[l],
                        ws_gate[l], ws_up[l], ws_down[l]).reshape(B, S, D)
        x = x + g2 * ffn_x
        if not last:
            Cn = ctx.shape[1]
            hc2 = modulate(rmsnorm(ctx, norm2_g[l]), sh2c, sc2c)
            ffn_c = moe_ffn(hc2.reshape(B * Cn, D), w_router[l], router_bias[l], w_gate[l], w_up[l], w_down[l],
                            ws_gate[l], ws_up[l], ws_down[l]).reshape(B, Cn, D)
            ctx = ctx + g2c * ffn_c
    return rmsnorm(x, final_g)


def setup_inputs(seed=0):
    out = dict(first_inputs(seed))
    for name, value in second_inputs(seed + 1).items():
        if name != "x":
            out[name + "_2"] = value
    return out


def reference(
    x, ln_gain, ln_bias, mlp_w_up, mlp_w_down, w_in_even, w_out_even, diff_lambda, diff_subln,
    nsa_pe, nsa_cmp_w1, nsa_cmp_b1, nsa_cmp_w2, w_in_odd, fox_f_bias, w_out_odd, c_2, ctx_2,
    c_ctx_2, w_ada_2, b_ada_2, norm1_g_2, norm2_g_2, w_in_2, attn_sink_2, pool_w_2,
    pool_scale_2, w_out_2, w_router_2, router_bias_2, w_gate_2, w_up_2, w_down_2, ws_gate_2,
    ws_up_2, ws_down_2, final_g_2,
):
    x = first_block(
        x, ln_gain, ln_bias, mlp_w_up, mlp_w_down, w_in_even, w_out_even, diff_lambda,
        diff_subln, nsa_pe, nsa_cmp_w1, nsa_cmp_b1, nsa_cmp_w2, w_in_odd, fox_f_bias, w_out_odd,
    )
    return second_block(
        x, c_2, ctx_2, c_ctx_2, w_ada_2, b_ada_2, norm1_g_2, norm2_g_2, w_in_2, attn_sink_2,
        pool_w_2, pool_scale_2, w_out_2, w_router_2, router_bias_2, w_gate_2, w_up_2, w_down_2,
        ws_gate_2, ws_up_2, ws_down_2, final_g_2,
    )


_drawn_inputs = setup_inputs


def setup_inputs(seed=0):
    import zlib

    import numpy as np

    out = dict(_drawn_inputs(seed))
    spreads = {}
    factors = {'diff_subln': 3.785,
     'nsa_pe': 3.171,
     'nsa_cmp_b1': 5.353,
     'norm1_g_2': 2.817,
     'attn_sink_2': 64.0}
    for name, (base, spread) in spreads.items():
        noise = np.random.default_rng([zlib.crc32(name.encode()), seed]).standard_normal(out[name].shape)
        drawn = base * np.exp(spread * noise) if base else spread * noise
        out[name] = __import__('jax').numpy.asarray(drawn.astype(out[name].dtype))
    for name, factor in factors.items():
        out[name] = (out[name] * factor).astype(out[name].dtype)
    return out
```

```python
from contextlib import ExitStack
import math

import numpy as np

import concourse.bass as bass
from concourse import mybir

F32 = mybir.dt.float32
U32 = mybir.dt.uint32
ALU = mybir.AluOpType
ACT = mybir.ActivationFunctionType
AX = mybir.AxisListType.X

P = 128
D = 1024
T = 256
TT = T // P
KT = D // P
HD = 64
FF = 4096
SLOT = 2048
RING = 8
BIG = -1e30
LN_EPS = 1e-5
RMS_EPS = 1e-6
ALPHA = 4.0 ** 0.25
LAM_INIT = 0.8 - 0.6 * math.exp(-0.3 * 0)
NCMP = (T - 32) // 16 + 1
NEXP = 64
ROUTED_SCALE = 2.5
POOL_WINDOWS = (2, 4, 8, 16)
SCALE = HD ** -0.5

MLP_STEPS = 4
EARLY = 1
SECTIONS = [
    ("in_even", 11), ("cmp", 4), ("out_even", 4), ("mlp0", 8 * MLP_STEPS),
    ("in_odd", 12), ("out_odd", 4), ("mlp1", 8 * MLP_STEPS),
    ("ada", 24), ("in_2", 5), ("out_2", 4), ("moe", 3 * (NEXP + 1)),
]
FIRST = {}
_n = 0
for _name, _count in SECTIONS:
    FIRST[_name] = _n
    _n += _count
CHUNKS = _n

PARAMS = [
    ("pe", 32), ("b1", 4), ("w2k", 256), ("w2v", 128), ("wgate", 192), ("wforget", 128),
    ("router", 512), ("rbias", 64), ("poolw", 512), ("poolscale", 4), ("cvec", 16), ("bada", 48),
    ("norm1", 8), ("norm2", 8), ("sink", 8), ("lam", 256), ("subln", 128), ("fbias", 1),
]
CONSTS = [
    ("ident", 128), ("rot1", 128), ("rot2", 128), ("cos1", 256), ("sin1", 256), ("cos2", 256), ("sin2", 256),
    ("cosc", 2 * NCMP), ("sinc", 2 * NCMP), ("causal", 512), ("local", 1024), ("cmpmask", 2 * NCMP),
    ("rowvalid", 2), ("iota8", 8),
]


def columns(blocks):
    at, n = {}, 0
    for name, width in blocks:
        at[name] = (n, width)
        n += width
    return at, n


PARAM_AT, NPARAM = columns(PARAMS)
CONST_AT, NCONST = columns(CONSTS)
TURNS = ["x0", "mix0", "ln0", "ln1", "mix1", "ln2", "rms1", "ctx", "mix2", "rms2"]
TURN_AT = {name: 4 * i for i, name in enumerate(TURNS)}


def attention_units():
    units = []
    group = 0
    for qt in range(TT):
        for h0 in (0, 4):
            for c in range(4):
                units.append(("diff", qt, h0 + c, P * (qt + 1), c * 128, 128, group))
            group += 1
    for kind in ("slc", "win", "cmp"):
        for qt in range(TT):
            for h in range(8):
                units.append((kind, qt, h, NCMP if kind == "cmp" else P * (qt + 1), h * HD, HD, group))
            group += 1
    for qt in range(TT):
        for h0 in (0, 8):
            for h in range(8):
                units.append(("fox", qt, h0 + h, P * (qt + 1), h * HD, HD, group))
            group += 1
    for qt in range(TT):
        for h in range(8):
            units.append(("loc", qt, h, 2 * T, h * HD, HD, group))
        group += 1
    return units


UNITS = attention_units()
INSTANCES = {"a0": (0, 64), "a1": (64, 96), "a2": (96, 112)}


def group_units(g):
    return [u for u, unit in enumerate(UNITS) if unit[6] == g]


def build(nc, d_stream, d_params, d_consts, d_pool, d_x, d_ctx, d_gain, d_bias, d_badarow, d_final, d_out):
    with ExitStack() as ctx:
        def sb(name, shape, dt=F32):
            return ctx.enter_context(nc.sbuf_tensor(name, shape, dt))

        def sem(name):
            return ctx.enter_context(nc.semaphore(name))

        ring = sb("ring", [P, RING, SLOT])
        par = sb("par", [P, NPARAM])
        con = sb("con", [P, NCONST])
        x = sb("x_rows", [P, TT, D])
        y = sb("y_rows", [P, TT, D])
        mix = sb("mix_rows", [P, TT, D])
        xT = sb("xT", [P, KT, T])
        qk = sb("qk_tiles", [P, 32, T])
        v = sb("v_rows", [P, TT, D])
        masked = sb("masked", [P, 4, 512])
        prob = sb("prob", [P, 3, 512])
        probT = sb("probT", [P, 2, 512])
        vec = sb("vec_rows", [P, 4, D])
        negmax = sb("negmax", [P, len(UNITS)])
        esum = sb("esum", [P, len(UNITS)])
        small = sb("small", [P, 160])
        gate3 = sb("gate3", [P, TT, 24])
        vcmp = sb("vcmp", [P, 2, HD])
        negsink = sb("negsink", [P, 8])
        csil = sb("csil", [P, KT, 2])
        modT = sb("modT", [P, 32, 2])
        amod = sb("amod", [P, 48])
        score = sb("score", [P, TT, NEXP])
        biased = sb("biased", [P, TT, NEXP])
        chosen = sb("chosen", [P, TT, NEXP])
        weight = sb("weight", [P, TT, NEXP + 8])
        ps = ctx.enter_context(nc.psum_tensor("ps", [P, 8, 512], F32))

        s_full = [sem(f"slot_full{i}") for i in range(RING)]
        s_used = sem("chunks_used")
        s_const = sem("consts_loaded")
        s_x = sem("x_loaded")
        s_ctx = sem("ctx_loaded")
        s_poolmat = sem("poolmat_loaded")
        s_vecA = sem("vecA_loaded")
        s_vecB = sem("vecB_loaded")
        s_out = sem("out_stored")
        s_rows = sem("rows_ready")
        s_turn = sem("turned_psum")
        s_xT = sem("xT_by_act")
        s_xTv = sem("xT_by_dve")
        s_gates = sem("gates_psum")
        s_projsb = sem("proj_sbuf")
        s_rot = sem("rotated_psum")
        s_roped = sem("roped")
        s_blk = sem("cmp_blocks")
        s_hidsb = sem("cmp_hidden_sbuf")
        s_cmp = sem("cmp_kv_psum")
        s_cmpsb = sem("cmp_kv_sbuf")
        s_crot = sem("cmp_rotated")
        s_ckey = sem("cmp_keys_ready")
        s_sc = sem("scores_psum")
        s_mask = sem("masked_ready")
        s_exp = sem("exp_ready")
        s_pT = sem("probT_psum")
        s_pTsb = sem("probT_sbuf")
        s_o = sem("outs_psum")
        s_odone = sem("outs_taken")
        s_restaken = sem("residual_taken")
        s_var = sem("variance_ready")
        s_std = sem("std_ready")
        s_normed = sem("norms_done")
        s_relu = sem("mlp_relu")
        s_hT = sem("mlp_hidden")
        s_acc = sem("mlp_added")
        s_f = sem("forget_psum")
        s_fact = sem("forget_act")
        s_fdve = sem("forget_dve")
        s_caug = sem("forget_rows_placed")
        s_csil = sem("c_silu")
        s_cb = sem("c_rows_ready")
        s_mod = sem("mod_ready")
        s_ss = sem("square_sums")
        s_dps = sem("pool_psum")
        s_dsb = sem("pool_sbuf")
        s_esink = sem("sink_exp")
        s_sinkin = sem("sink_shifted")
        s_lam = sem("lambda_sums")
        s_lexp = sem("lambda_exps")
        s_rps = sem("router_psum")
        s_score = sem("router_scores")
        s_msilu = sem("moe_silu")
        s_mact = sem("moe_act")
        s_macc = sem("moe_added")
        s_dve = sem("dve_chain")
        s_act = sem("act_chain")
        s_pool = sem("pool_chain")

        def windows(tiles, g):
            row = tiles[:, g, :]
            return bass.AP(row.tensor, row.offset, [row.ap[0], (2, 16), (16, NCMP)])

        def C(name, p=P):
            a, w = CONST_AT[name]
            return con[0:p, a:a + w]

        def R(name, p=P):
            a, w = PARAM_AT[name]
            return par[0:p, a:a + w]

        ident = C("ident")
        raw = masked[:].rearrange("p a b -> p (a b)").rearrange("p (s t c) -> p s t c", s=2, t=4)
        lamc = small[:, 0:1]
        var2 = small[:, 2:4]
        std2 = small[:, 4:6]
        rstd = small[:, 6:8]
        nwt = small[:, 8:10]
        mv = small[:, 10:14].rearrange("p (t s) -> p t s", t=2)
        bn = small[:, 16:40].rearrange("p (a s) -> p a s", a=4)
        ss = small[:, 40:42]
        lsum = small[:, 42:44]
        lexp = small[:, 44:46]
        coef = small[:, 48:56]
        dms = small[:, 56:58]
        top8 = small[:, 64:80].rearrange("p (t k) -> p t k", t=2)
        esink = small[:, 80:88]
        sinksh = small[:, 88:96]
        gsc = small[:, 96:112].rearrange("p (t k) -> p t k", t=2)
        gmask = small[:, 112:128].rearrange("p (t k) -> p t k", t=2)
        wsum = small[:, 128:130]
        var_c = small[:, 130:132]
        top8b = small[:, 136:152].rearrange("p (t k) -> p t k", t=2)
        drms = small[:, 152:154]
        dstd = small[:, 154:156]
        drs = small[:, 156:158]
        dnw = small[:, 158:160]
        gidx = sb("gidx", [P, TT, 8], U32)
        gidxf = sb("gidxf", [P, TT, 8])

        hT = qk[:, 0:8, :]
        XS = lambda j: qk[:, 20 + 2 * j:22 + 2 * j, :]
        cmpin = qk[:, 24:28, :].rearrange("p a b -> p (a b)")[:, 0:2 * 16 * 2 * NCMP].rearrange(
            "p (j m g n) -> p j m g n", j=2, m=16, g=2)
        kcraw = qk[:, 28, 0:2 * NCMP]
        kcd = qk[:, 28, 32:32 + 2 * NCMP]
        hidT = qk[:, 29, 0:4 * 2 * NCMP].rearrange("p (j t n) -> p j t n", j=2, t=2)
        kctmp = qk[:, 28, 64:64 + 2 * NCMP]
        foxq = qk[0:66, 0:16, :]
        foxk = qk[0:66, 16:32, :]
        ctxr = qk[:, 24:32, :].rearrange("p a b -> p (a b)").rearrange("p (t f) -> p t f", t=2)
        cT = qk[:, 16:24, :]
        poolmat = y[:].rearrange("p t f -> p (t f)").rearrange("p (g t c) -> p g t c", g=4, t=2)
        dT = qk[:, 9:13, :]
        cb = masked[:, 0:2, :].rearrange("p a b -> p (a b)").rearrange("p (k c) -> p k c", k=KT)
        actT = masked[:].rearrange("p a b -> p (a b)").rearrange("p (s t c) -> p s t c", s=4, t=2)
        sg = prob[:, 0:2, :]

        causal = C("causal").rearrange("p (q k) -> p q k", q=2)
        local = C("local").rearrange("p (q k) -> p q k", q=2)
        cmpmask = C("cmpmask").rearrange("p (q k) -> p q k", q=2)

        def unit_operands(u):
            kind, qt, h, nk, _, w, _ = UNITS[u]
            qs = slice(qt * P, (qt + 1) * P)
            lo = HD * (h % 2)
            half = slice(lo, lo + HD)
            g = h // 4
            tiles = range(qt + 1)
            if kind == "diff":
                return (qk[half, h // 2, qs], [(qk[half, 4 + h // 2, 0:nk], 0)], causal[:, qt, 0:nk],
                        [v[:, t, (h // 2) * P:(h // 2 + 1) * P] for t in tiles])
            if kind == "slc":
                return (qk[half, 8 + h // 2, qs], [(qk[half, 12 + g, 0:nk], 0)], causal[:, qt, 0:nk],
                        [v[:, t, 512 + g * HD:512 + (g + 1) * HD] for t in tiles])
            if kind == "win":
                return (qk[half, 8 + h // 2, qs], [(qk[half, 14 + g, 0:nk], 0)], causal[:, qt, 0:nk],
                        [v[:, t, 640 + g * HD:640 + (g + 1) * HD] for t in tiles])
            if kind == "cmp":
                return (qk[half, 8 + h // 2, qs], [(kcd[half, g * NCMP:(g + 1) * NCMP], 0)], cmpmask[:, qt, :],
                        [vcmp[0:NCMP, g, :]])
            if kind == "fox":
                return (foxq[:, h, qs], [(foxk[:, h, 0:nk], 0)], causal[:, qt, 0:nk],
                        [v[:, t, h * HD:(h + 1) * HD] for t in tiles])
            return (qk[half, h // 2, qs], [(qk[half, 5 + g, :], 0), (qk[half, 7 + g, :], T)], local[:, qt, :],
                    [v[:, t, g * HD:(g + 1) * HD] for t in range(2)]
                    + [v[:, t, 128 + g * HD:128 + (g + 1) * HD] for t in range(2)])

        block = ctx.enter_context(nc.Block())

        @block.sync
        def _(sp):
            for s in range(RING):
                sp.dma_start(ring[:, s, :], d_stream[s]).then_inc(s_full[s], 16)
                if s == 1:
                    sp.dma_start(par[:], d_params).then_inc(s_const, 16)
            with sp.Fori(1, CHUNKS // RING) as it:
                for s in range(RING):
                    sp.wait_ge(s_used, it * RING + (s - RING + 1))
                    sp.dma_start(ring[:, s, :], d_stream[bass.ds(it * RING + s, 1)].rearrange("o p c -> (o p) c")
                                 ).then_inc(s_full[s], 16)
            for n in range(CHUNKS // RING * RING, CHUNKS):
                sp.wait_ge(s_used, n - RING + 1)
                sp.dma_start(ring[:, n % RING, :], d_stream[n]).then_inc(s_full[n % RING], 16)
            for t in range(TT):
                sp.wait_ge(s_normed, 5 + t)
                sp.dma_start(d_out[t * P:(t + 1) * P, :], x[:, t, :]).then_inc(s_out, 16)
            sp.wait_ge(s_out, 16 * TT)

        @block.tensor
        def _(pe):
            def chunk(n, per=0, it=0):
                pe.wait_ge(s_full[n % RING], it * (16 * per) + 16 * (n // RING + 1) if per else 16 * (n // RING + 1))
                return ring[:, n % RING, :]

            def turn(src, name, tiles=KT):
                for t in range(TT):
                    pe.wait_ge(s_rows, TT * TURNS.index(name) + t + 1)
                    for half in range(tiles // 4):
                        for j in range(4):
                            f = (4 * half + j) * P
                            mm = pe.transpose(ps[:, 4 + 2 * t + half, j * P:(j + 1) * P], src[:, t, f:f + P], ident)
                        mm.then_inc(s_turn, 4 // (tiles // 4) // 2)

            def wait_xT(name):
                pe.wait_ge(s_xT, 2 * (TURNS.index(name) + 1))
                pe.wait_ge(s_xTv, 2 * (TURNS.index(name) + 1))

            def panel(n0, started, jobs, k_per=4):
                width = SLOT // k_per
                for c in range(KT // k_per):
                    w = chunk(n0 + c).rearrange("p (k n) -> p k n", k=k_per)
                    for kind, src, col, n, bank, off in jobs:
                        for kk in range(k_per):
                            k = c * k_per + kk
                            if kind == "ws":
                                mm = pe.matmul(ps[0:n, bank, off:off + T], w[:, kk, col:col + n], src[:, k, :],
                                               start=bank not in started, stop=k == KT - 1, skip_group_check=True)
                                started.add(bank)
                            else:
                                t = kind
                                mm = pe.matmul(ps[:, bank, off:off + n], src[:, k, t * P:(t + 1) * P],
                                               w[:, kk, col:col + n], start=bank not in started, stop=k == KT - 1,
                                               skip_group_check=True)
                                started.add(bank)
                    mm.then_inc(s_used, 1)
                return mm

            def rotate(rot, src, bank, n):
                return pe.matmul(ps[:, bank, 0:n], rot, src, start=True, stop=True)

            def attention(name):
                a, b = INSTANCES[name]
                for i in range(a, b + 3):
                    if i < b:
                        lhs, keys, _, _ = unit_operands(i)
                        if UNITS[i][0] == "cmp" and UNITS[i - 1][0] != "cmp":
                            pe.wait_ge(s_ckey, 2)
                        if i >= 2:
                            pe.wait_ge(s_mask, i - 1)
                        for key, col in keys:
                            mm = pe.matmul(ps[:, i % 2, col:col + key.shape[1]], lhs, key, start=True, stop=True)
                        mm.then_inc(s_sc, 1)
                    u = i - 2
                    if a <= u < b:
                        nk = UNITS[u][3]
                        pe.wait_ge(s_exp, u + 1)
                        if u >= 2:
                            pe.wait_ge(s_pTsb, u - 1)
                        for t in range((nk + P - 1) // P):
                            n = min(P, nk - t * P)
                            mm = pe.transpose(ps[0:n, 2 + u % 2, t * P:(t + 1) * P], prob[:, u % 3, t * P:t * P + n], ident)
                        mm.then_inc(s_pT, 1)
                    u = i - 3
                    if a <= u < b:
                        _, _, _, vals = unit_operands(u)
                        _, _, _, nk, col, w, g = UNITS[u]
                        pe.wait_ge(s_pTsb, u + 1)
                        if u == group_units(g)[0] and g >= 2:
                            pe.wait_ge(s_odone, g - 1)
                        for t, val in enumerate(vals):
                            n = min(P, nk - t * P)
                            mm = pe.matmul(ps[:, 4 + g % 2, col:col + w], probT[0:n, u % 2, t * P:(t + 1) * P], val,
                                           start=t == 0, stop=t == len(vals) - 1)
                        if u == group_units(g)[-1]:
                            mm.then_inc(s_o, 1)

            def out_projection(n0):
                for c in range(4):
                    w = chunk(n0 + c).rearrange("p (k n) -> p k n", k=2)
                    for kk in range(2):
                        k = 2 * c + kk
                        for t in range(TT):
                            for half in range(2):
                                mm = pe.matmul(ps[:, 2 * t + half, :], xT[:, k, t * P:(t + 1) * P],
                                               w[:, kk, half * 512:(half + 1) * 512], start=k == 0, stop=k == KT - 1)
                    mm.then_inc(s_used, 1)

            def mlp(layer):
                n0 = FIRST[f"mlp{layer}"]
                pe_done = layer * 2 * MLP_STEPS
                with pe.Fori(0, MLP_STEPS) as it:
                    for j in range(2):
                        pe.wait_ge(s_relu, it * 2 + (pe_done + EARLY))
                        started = set()
                        for c in range(2):
                            w = chunk(n0 + 2 * j + c, 1, it).rearrange("p (k n) -> p k n", k=4)
                            for m in range(4):
                                bank = 4 + 2 * j + m // 2
                                for kk in range(4):
                                    k = 4 * c + kk
                                    mm = pe.matmul(ps[:, bank, (m % 2) * T:(m % 2 + 1) * T], w[:, kk, m * P:(m + 1) * P],
                                                   xT[:, k, :], start=bank not in started, stop=k == KT - 1,
                                                   skip_group_check=True)
                                    started.add(bank)
                            mm.then_inc(s_used, 1)
                    for c in range(4):
                        w = chunk(n0 + 4 + c, 1, it).rearrange("p (k n) -> p k n", k=2)
                        if c % 2 == 0:
                            pe.wait_ge(s_hT, it * 2 + (pe_done + c // 2 + 1))
                        if c == 0:
                            pe.wait_ge(s_acc, it + (layer * MLP_STEPS + EARLY))
                        for kk in range(2):
                            k = 2 * c + kk
                            for t in range(TT):
                                for half in range(2):
                                    mm = pe.matmul(ps[:, 2 * t + half, :], hT[:, k, t * P:(t + 1) * P],
                                                   w[:, kk, half * 512:(half + 1) * 512], start=k == 0, stop=k == 7)
                        mm.then_inc(s_used, 1)

            pe.wait_ge(s_const, 32)
            pe.wait_ge(s_x, 16)
            turn(x, "x0")
            wait_xT("x0")
            n0 = FIRST["in_even"]

            def ws4(bank, src=xT):
                return [("ws", src, m * P, P, bank + m // 2, (m % 2) * T) for m in range(4)]

            panel(n0, set(), ws4(0))
            panel(n0 + 2, set(), ws4(2))
            for m in range(2):
                pe.wait_ge(s_projsb, 1)
                mm = rotate(C("rot1"), raw[:, 0, 2 * m:2 * m + 2, :], 6 + m, 512)
            mm.then_inc(s_rot, 1)
            panel(n0 + 4, set(), [(t, xT, 0, 512, 4 + t, 0) for t in range(TT)])
            pe.wait_ge(s_roped, 1)
            pe.wait_ge(s_projsb, 2)
            for m in range(2):
                mm = rotate(C("rot1"), raw[:, 1, 2 * m:2 * m + 2, :], 6 + m, 512)
            mm.then_inc(s_rot, 1)
            panel(n0 + 6, set(), ws4(0))
            started = set()
            panel(n0 + 8, started, [("ws", xT, 0, P, 2, 0), ("ws", xT, P, P, 2, T), ("ws", xT, 2 * P, P, 3, 0),
                                    (0, xT, 3 * P, P, 3, T), (1, xT, 3 * P, P, 3, T + P)])
            pe.wait_ge(s_roped, 2)
            pe.wait_ge(s_projsb, 4)
            for m in range(2):
                mm = rotate(C("rot1"), raw[:, 0, 2 * m:2 * m + 2, :], 6 + m, 512)
            mm.then_inc(s_rot, 1)
            pe.wait_ge(s_projsb, 3)
            started = set()
            mm = panel(n0 + 10, started, [("ws", xT, 0, P, 4, 0), (0, xT, P, P, 4, T), (1, xT, P, P, 4, T + P)], 8)
            for t in range(TT):
                for k in range(KT):
                    mm = pe.matmul(ps[:, 5, t * 24:(t + 1) * 24], xT[:, k, t * P:(t + 1) * P],
                                   R("wgate")[:, k * 24:(k + 1) * 24], start=k == 0, stop=k == KT - 1)
            mm.then_inc(s_gates, 1)
            pe.wait_ge(s_roped, 3)
            pe.wait_ge(s_projsb, 6)
            rotate(C("rot1"), raw[:, 1, 0:2, :], 6, 512).then_inc(s_rot, 1)
            n0 = FIRST["cmp"]
            pe.wait_ge(s_blk, 4)
            for j in range(2):
                for c in range(2):
                    w = chunk(n0 + 2 * j + c).rearrange("p (m n) -> p m n", m=8)
                    for nt in range(2):
                        for mi in range(8):
                            m = 8 * c + mi
                            mm = pe.matmul(ps[:, 7, (2 * j + nt) * 32:(2 * j + nt) * 32 + 2 * NCMP],
                                           w[:, mi, nt * P:(nt + 1) * P],
                                           cmpin[:, j, m, :, :].rearrange("p g n -> p (g n)"),
                                           start=j == 0 and m == 0 and nt == 0, stop=m == 15, skip_group_check=True)
                    mm.then_inc(s_used, 1)
            pe.wait_ge(s_hidsb, 1)
            pe.wait_ge(s_roped, 4)
            for nt in range(2):
                mm = pe.matmul(ps[:, 6, 0:2 * NCMP], R("w2k")[:, nt * P:(nt + 1) * P], hidT[:, 0, nt, :],
                               start=nt == 0, stop=nt == 1)
            for g in range(2):
                for nt in range(2):
                    mm = pe.matmul(ps[0:NCMP, 6, 64 + g * HD:64 + (g + 1) * HD], hidT[:, 1, nt, g * NCMP:(g + 1) * NCMP],
                                   R("w2v")[:, nt * HD:(nt + 1) * HD], start=nt == 0, stop=nt == 1)
            mm.then_inc(s_cmp, 1)
            pe.wait_ge(s_cmpsb, 1)
            rotate(C("rot1"), kcraw, 7, 2 * NCMP).then_inc(s_crot, 1)
            attention("a0")
            turn(mix, "mix0")
            wait_xT("mix0")
            out_projection(FIRST["out_even"])
            turn(x, "ln0")
            wait_xT("ln0")
            mlp(0)
            turn(x, "ln1")
            wait_xT("ln1")
            n0 = FIRST["in_odd"]
            for j in range(4):
                if j >= 3:
                    pe.wait_ge(s_projsb, 6 + j - 2)
                panel(n0 + 2 * j, set(), ws4(2 * (j % 3)))
                if j == 0:
                    for k in range(KT):
                        mm = pe.matmul(ps[0:16, 7, 0:T], R("wforget")[:, k * 16:(k + 1) * 16], xT[:, k, :],
                                       start=k == 0, stop=k == KT - 1)
                    mm.then_inc(s_f, 1)
            for j in range(4, 6):
                pe.wait_ge(s_projsb, 6 + j - 2)
                b = 2 * (j % 3)
                panel(n0 + 2 * j, set(), [(t, xT, 0, 512, b + t, 0) for t in range(TT)])
            pe.wait_ge(s_projsb, 12)
            pe.wait_ge(s_caug, 32)
            attention("a1")
            turn(mix, "mix1")
            wait_xT("mix1")
            out_projection(FIRST["out_odd"])
            turn(x, "ln2")
            wait_xT("ln2")
            mlp(1)
            pe.wait_ge(s_cb, 1)
            pe.wait_ge(s_relu, 4 * MLP_STEPS + EARLY)
            pe.wait_ge(s_acc, 2 * MLP_STEPS + EARLY)
            n0 = FIRST["ada"]
            started = set()
            for i, what in enumerate(("sh1", "sc1", "g1", "sh2", "sc2", "g2")):
                for half in range(2):
                    for c in range(2):
                        w = chunk(n0 + 4 * i + 2 * half + c).rearrange("p (k n) -> p k n", k=4)
                        if what in ("g1", "g2"):
                            bank = (0 if what == "g1" else 2) + half
                            for kk in range(4):
                                k = 4 * c + kk
                                mm = pe.matmul(ps[:, bank, :], cb[:, k, :], w[:, kk, :], start=k == 0, stop=k == KT - 1)
                        else:
                            col = {"sh1": 0, "sc1": 8, "sh2": 16, "sc2": 24}[what] + 4 * half
                            for m in range(4):
                                for kk in range(4):
                                    k = 4 * c + kk
                                    mm = pe.matmul(ps[:, 6, 2 * (col + m):2 * (col + m) + 2], w[:, kk, m * P:(m + 1) * P],
                                                   csil[:, k, :], start=6 not in started, stop=k == KT - 1,
                                                   skip_group_check=True)
                                    started.add(6)
                        mm.then_inc(s_used, 1)
            pe.wait_ge(s_mod, 1)
            turn(y, "rms1")
            wait_xT("rms1")
            turn(ctxr, "ctx")
            wait_xT("ctx")
            n0 = FIRST["in_2"]
            pe.wait_ge(s_mod, 3)
            panel(n0, set(), ws4(0))
            jobs = [("ws", xT, 0, P, 2, 0), ("ws", cT, 0, P, 2, T)]
            jobs += [(t, xT, P, P, 3, t * P) for t in range(TT)] + [(t, cT, P, P, 3, T + t * P) for t in range(TT)]
            panel(n0 + 2, set(), jobs, 8)
            pe.wait_ge(s_projsb, 13)
            for m in range(2):
                mm = rotate(C("rot2"), raw[:, 0, 2 * m:2 * m + 2, :], 6 + m, 512)
            mm.then_inc(s_rot, 1)
            panel(n0 + 3, set(), [(t, xT, 0, 512, 4 + t, 0) for t in range(TT)])
            pe.wait_ge(s_projsb, 14)
            rotate(C("rot2"), raw[:, 1, 0, :], 0, T).then_inc(s_rot, 1)
            pe.wait_ge(s_projsb, 15)
            pe.wait_ge(s_poolmat, 16)
            for g in range(4):
                for t in range(TT):
                    mm = pe.matmul(ps[:, 4 + g // 2, (g % 2) * T:(g % 2 + 1) * T],
                                   v[:, t, 512 + g * P:512 + (g + 1) * P], poolmat[:, g, t, :], start=t == 0, stop=t == 1)
            mm.then_inc(s_dps, 1)
            pe.wait_ge(s_dsb, 1)
            pe.wait_ge(s_roped, 5)
            for g in range(4):
                mm = pe.matmul(ps[:, 6 + g // 2, (g % 2) * T:(g % 2 + 1) * T], R("poolw")[:, g * P:(g + 1) * P],
                               dT[:, g, :], start=True, stop=True)
            mm.then_inc(s_dps, 1)
            pe.wait_ge(s_roped, 6)
            pe.wait_ge(s_dsb, 2)
            attention("a2")
            turn(mix, "mix2", 4)
            wait_xT("mix2")
            out_projection(FIRST["out_2"])
            turn(y, "rms2")
            wait_xT("rms2")
            for t in range(TT):
                for k in range(KT):
                    mm = pe.matmul(ps[:, 0, t * NEXP:(t + 1) * NEXP], xT[:, k, t * P:(t + 1) * P],
                                   R("router")[:, k * NEXP:(k + 1) * NEXP], start=k == 0, stop=k == KT - 1)
            mm.then_inc(s_rps, 1)

            def expert_up(n, odd, per=0, it=0):
                started = set()
                for c in range(2):
                    w = chunk(n + c, per, it).rearrange("p (k n) -> p k n", k=4)
                    for m in range(4):
                        bank = 4 + 2 * odd + m // 2
                        for kk in range(4):
                            k = 4 * c + kk
                            mm = pe.matmul(ps[:, bank, (m % 2) * T:(m % 2 + 1) * T], w[:, kk, m * P:(m + 1) * P],
                                           xT[:, k, :], start=bank not in started, stop=k == KT - 1, skip_group_check=True)
                            started.add(bank)
                    mm.then_inc(s_used, 1)

            def expert_down(n, odd, per=0, it=0):
                w = chunk(n, per, it).rearrange("p (k n) -> p k n", k=2)
                for k in range(2):
                    for t in range(TT):
                        for half in range(2):
                            mm = pe.matmul(ps[:, 2 * t + half, :], actT[:, 2 * odd + k // 2, k, t * P:(t + 1) * P],
                                           w[:, k, half * 512:(half + 1) * 512], start=k == 0, stop=k == 1)
                mm.then_inc(s_used, 1)

            n0 = FIRST["moe"]
            expert_up(n0, 0)
            pe.wait_ge(s_score, 1)
            with pe.Fori(0, NEXP // 8) as it:
                for j in range(8):
                    pe.wait_ge(s_mact, it * 8 + (j + EARLY))
                    expert_up(n0 + 2 + 3 * j, (j + 1) % 2, 3, it)
                    pe.wait_ge(s_mact, it * 8 + (j + 1 + EARLY))
                    pe.wait_ge(s_macc, it * 8 + (j + EARLY))
                    expert_down(n0 + 4 + 3 * j, j % 2, 3, it)
            pe.wait_ge(s_mact, NEXP + 1 + EARLY)
            pe.wait_ge(s_macc, NEXP + EARLY)
            expert_down(n0 + 2 + 3 * NEXP, 0)

        @block.scalar
        def _(act):
            chain = [0]

            def link(ins):
                chain[0] += 1
                ins.then_inc(s_act, 1)
                act.wait_ge(s_act, chain[0])

            def panel_done(section, n):
                act.wait_ge(s_used, FIRST[section] + n)

            def take_turn(name, dst, tiles=KT):
                for t in range(TT):
                    act.wait_ge(s_turn, TURN_AT[name] + 2 * t + (1 if tiles == KT else 2))
                    act.activation(dst[:, 0:4, t * P:(t + 1) * P], ps[:, 4 + 2 * t, :].rearrange("p (j c) -> p j c", j=4),
                                   ACT.Copy).then_inc(s_xT, 1)

            def take_turn_mod(name, dst, a, b):
                for t in range(TT):
                    act.wait_ge(s_turn, TURN_AT[name] + 2 * t + 1)
                    for j in range(4):
                        i = act.activation(dst[:, j, t * P:(t + 1) * P], ps[:, 4 + 2 * t, j * P:(j + 1) * P],
                                           ACT.Identity, scale=a[:, j:j + 1], bias=b[:, j:j + 1])
                    i.then_inc(s_xT, 1)

            def copy(dst, src, **kw):
                return act.activation(dst, src, ACT.Copy, **kw)

            def copy_panel(dst, bank):
                for m in range(2):
                    i = copy(dst[:, 2 * m:2 * m + 2, :], ps[:, bank + m, :].rearrange("p (a c) -> p a c", a=2))
                return i

            def exps(name):
                a, b = INSTANCES[name]
                for u in range(a, b + 5):
                    if u < b:
                        nk = UNITS[u][3]
                        act.wait_ge(s_mask, u + 1)
                        if u >= 3:
                            act.wait_ge(s_pT, u - 2)
                        act.activation(prob[:, u % 3, 0:nk], masked[:, u % 3, 0:nk], ACT.Exp, bias=negmax[:, u:u + 1],
                                       scale=-1.0, accum_out=esum[:, u:u + 1]).then_inc(s_exp, 1)
                    if a <= u - 4 < b and group_units(UNITS[u - 4][6])[-1] == u - 4:
                        kind, qt, _, _, _, _, g = UNITS[u - 4]
                        if kind == "loc":
                            act.wait_ge(s_sinkin, qt + 1)
                            act.activation(esink, sinksh, ACT.Exp).then_inc(s_esink, 1)
                        if kind == "diff":
                            act.wait_ge(s_var, g + 1)
                            act.activation(dstd, drms, ACT.Sqrt).then_inc(s_std, 1)


            def std(k):
                act.wait_ge(s_var, k)
                act.activation(std2, var2, ACT.Sqrt).then_inc(s_std, 1)

            act.dma_start(x[:], d_x.rearrange("(t p) f -> p t f", p=P)).then_inc(s_x, 16)
            act.dma_start(con[:], d_consts).then_inc(s_const, 16)
            take_turn("x0", xT)
            act.wait_ge(s_lam, 1)
            act.activation(lexp, lsum, ACT.Exp).then_inc(s_lexp, 1)
            panel_done("in_even", 2)
            copy_panel(raw[:, 0], 0).then_inc(s_projsb, 1)
            panel_done("in_even", 4)
            copy_panel(raw[:, 1], 2).then_inc(s_projsb, 1)
            panel_done("in_even", 6)
            for t in range(TT):
                i = copy(v[:, t, 0:512], ps[:, 4 + t, :])
            i.then_inc(s_projsb, 1)
            panel_done("in_even", 8)
            act.wait_ge(s_roped, 1)
            copy_panel(raw[:, 0], 0).then_inc(s_projsb, 1)
            panel_done("in_even", 10)
            act.wait_ge(s_roped, 2)
            for j in range(2):
                for g in range(2):
                    rows = slice(g * HD, (g + 1) * HD)
                    copy(XS(j)[0:HD, g, :], ps[rows, 2, j * T:(j + 1) * T])
                    i = copy(XS(j)[HD:P, g, 0:T - 1], ps[rows, 2, j * T + 1:(j + 1) * T])
            copy(raw[:, 1, 0, :], ps[:, 3, 0:T])
            for t in range(TT):
                i = copy(v[:, t, 512:640], ps[:, 3, T + t * P:T + (t + 1) * P])
            i.then_inc(s_projsb, 1)
            act.wait_ge(s_gates, 1)
            copy(raw[:, 1, 1, :], ps[:, 4, 0:T])
            for t in range(TT):
                copy(v[:, t, 640:768], ps[:, 4, T + t * P:T + (t + 1) * P])
            act.activation(gate3[:], ps[:, 5, 0:48].rearrange("p (t c) -> p t c", t=2), ACT.Sigmoid).then_inc(s_projsb, 1)
            panel_done("cmp", 4)
            for j in range(2):
                for nt in range(2):
                    i = act.activation(hidT[:, j, nt, :], ps[:, 7, (2 * j + nt) * 32:(2 * j + nt) * 32 + 2 * NCMP],
                                       ACT.Gelu_apprx_tanh, bias=R("b1")[:, 2 * j + nt:2 * j + nt + 1])
            i.then_inc(s_hidsb, 1)
            act.wait_ge(s_cmp, 1)
            copy(vcmp[0:NCMP, :, :], ps[0:NCMP, 6, 64:64 + 2 * HD].rearrange("p (g d) -> p g d", g=2)).then_inc(s_ckey, 1)
            copy(kcraw, ps[:, 6, 0:2 * NCMP]).then_inc(s_cmpsb, 1)
            exps("a0")
            take_turn("mix0", xT)
            std(5)
            take_turn("ln0", xT)

            def mlp(layer):
                with act.Fori(0, MLP_STEPS) as it:
                    for j in range(2):
                        base = layer * 2 * MLP_STEPS
                        act.wait_ge(s_used, it * 8 + (FIRST[f"mlp{layer}"] + 2 * j + 2))
                        for m in range(2):
                            i = act.activation(hT[:, 4 * j + 2 * m:4 * j + 2 * m + 2, :],
                                               ps[:, 4 + 2 * j + m, :].rearrange("p (a c) -> p a c", a=2), ACT.Relu)
                        i.then_inc(s_relu, 1)

            mlp(0)
            std(6)
            take_turn("ln1", xT)
            for j in range(6):
                panel_done("in_odd", 2 * j + 2)
                b = 2 * (j % 3)
                if j < 4:
                    dst = foxq if j < 2 else foxk
                    for m in range(4):
                        h = 8 * (j % 2) + 2 * m
                        for o in range(2):
                            i = copy(dst[0:HD, h + o, :], ps[o * HD:(o + 1) * HD, b + m // 2, (m % 2) * T:(m % 2 + 1) * T],
                                     scale=SCALE if j < 2 else 1.0)
                else:
                    for t in range(TT):
                        i = copy(v[:, t, 512 * (j - 4):512 * (j - 3)], ps[:, b + t, :])
                i.then_inc(s_projsb, 1)
                if j == 0:
                    act.wait_ge(s_fdve, 1)
                    link(act.activation(mix[0:16, 0, 256:512], mix[0:16, 0, 256:512], ACT.Exp, scale=-1.0))
                    act.activation(mix[0:16, 0, 256:512], mix[0:16, 0, 256:512], ACT.Ln, bias=1.0).then_inc(s_fact, 1)
            exps("a1")
            take_turn("mix1", xT)
            std(7)
            take_turn("ln2", xT)
            act.activation(csil[:].rearrange("p k c -> p (k c)"), R("cvec"), ACT.Silu).then_inc(s_csil, 1)
            mlp(1)
            std(8)
            act.wait_ge(s_ctx, 16)
            for t in range(TT):
                i = act.activation(mix[:, t, :], ctxr[:, t, :], ACT.Square, accum_out=var_c[:, t:t + 1])
            i.then_inc(s_ss, 1)
            act.wait_ge(s_ss, 1)
            act.wait_ge(s_normed, 4)
            for t in range(TT):
                i = act.activation(mix[:, t, :], x[:, t, :], ACT.Square, accum_out=ss[:, t:t + 1])
            i.then_inc(s_ss, 1)
            act.wait_ge(s_var, 9)
            act.activation(std2, var2, ACT.Sqrt).then_inc(s_std, 1)
            act.wait_ge(s_var, 10)
            act.activation(std2, var2, ACT.Sqrt).then_inc(s_std, 1)
            act.wait_ge(s_mod, 2)
            take_turn_mod("rms1", xT, amod[:, 0:8], modT[:, 0:8, 0])
            take_turn_mod("ctx", cT, amod[:, 8:16], modT[:, 0:8, 1])
            panel_done("in_2", 2)
            copy_panel(raw[:, 0], 0).then_inc(s_projsb, 1)
            panel_done("in_2", 3)
            copy(raw[:, 1, 0, :], ps[:, 2, 0:T])
            for g in range(2):
                for o in range(2):
                    copy(qk[o * HD:(o + 1) * HD, 7 + g, :], ps[g * HD:(g + 1) * HD, 2, T:2 * T])
            for t in range(TT):
                copy(v[:, t, 0:128], ps[:, 3, t * P:(t + 1) * P])
                i = copy(v[:, t, 128:256], ps[:, 3, T + t * P:T + (t + 1) * P])
            i.then_inc(s_projsb, 1)
            panel_done("in_2", 5)
            for t in range(TT):
                i = copy(v[:, t, 512:1024], ps[:, 4 + t, :])
            i.then_inc(s_projsb, 1)
            act.wait_ge(s_dps, 1)
            copy_panel(dT, 4).then_inc(s_dsb, 1)
            act.wait_ge(s_dps, 2)
            for g in range(4):
                i = act.activation(xT[:, 4 + g, :], ps[:, 6 + g // 2, (g % 2) * T:(g % 2 + 1) * T],
                                   ACT.Identity, scale=R("poolscale")[:, g:g + 1])
            i.then_inc(s_dsb, 1)
            exps("a2")
            take_turn("mix2", xT, 4)
            act.wait_ge(s_restaken, 3)
            for t in range(TT):
                i = act.activation(mix[:, t, :], x[:, t, :], ACT.Square, accum_out=ss[:, t:t + 1])
            i.then_inc(s_ss, 1)
            std(11)
            take_turn_mod("rms2", xT, amod[:, 16:24], modT[:, 16:24, 0])
            act.wait_ge(s_rps, 1)
            act.activation(score[:], ps[:, 0, 0:2 * NEXP].rearrange("p (t e) -> p t e", t=2), ACT.Sigmoid).then_inc(s_score, 1)
            act.wait_ge(s_used, FIRST["moe"] + 2)
            act.activation(sg[:, 0, :], ps[:, 4, :], ACT.Silu).then_inc(s_msilu, 1)
            with act.Fori(0, NEXP // 8) as it:
                for j in range(8):
                    odd = (j + 1) % 2
                    act.wait_ge(s_used, it * 24 + (FIRST["moe"] + 3 * j + 4))
                    act.wait_ge(s_mact, it * 8 + (j + EARLY))
                    act.activation(sg[:, odd, :], ps[:, 4 + 2 * odd, :], ACT.Silu).then_inc(s_msilu, 1)
            act.wait_ge(s_macc, NEXP + 2 + EARLY)
            for t in range(TT):
                i = act.activation(mix[:, t, :], x[:, t, :], ACT.Square, accum_out=ss[:, t:t + 1])
            i.then_inc(s_ss, 1)
            std(12)

        @block.vector
        def _(dve):
            chain = [0]

            def link(ins):
                chain[0] += 1
                ins.then_inc(s_dve, 1)
                dve.wait_ge(s_dve, chain[0])

            def take_turn(name, dst, tiles=KT):
                for t in range(TT):
                    dve.wait_ge(s_turn, TURN_AT[name] + 2 * t + 2)
                    if tiles == KT:
                        dve.tensor_copy(dst[:, 4:8, t * P:(t + 1) * P],
                                        ps[:, 5 + 2 * t, :].rearrange("p (j c) -> p j c", j=4)).then_inc(s_xTv, 1)

            def take_turn_mod(name, dst, a, b):
                for t in range(TT):
                    dve.wait_ge(s_turn, TURN_AT[name] + 2 * t + 2)
                    for j in range(4):
                        i = dve.tensor_scalar(dst[:, 4 + j, t * P:(t + 1) * P], ps[:, 5 + 2 * t, j * P:(j + 1) * P],
                                              a[:, 4 + j:5 + j], b[:, 4 + j:5 + j], ALU.mult, ALU.add)
                    i.then_inc(s_xTv, 1)

            def rope(out, src, banks, cos, sin, tiles):
                for m in range((tiles + 1) // 2):
                    n = min(2, tiles - 2 * m)
                    s3 = [P, n, T]
                    o, i0 = out[:, 2 * m:2 * m + n, :], src[:, 2 * m:2 * m + n, :]
                    rot = ps[:, banks + m, 0:n * T].rearrange("p (a c) -> p a c", a=n)
                    part = probT[:, 0, 0:n * T].rearrange("p (a c) -> p a c", a=n)
                    dve.tensor_tensor(o, i0, cos.unsqueeze(1).to_broadcast(s3), ALU.mult)
                    link(dve.tensor_tensor(part, rot, sin.unsqueeze(1).to_broadcast(s3), ALU.mult))
                    i = dve.tensor_tensor(o, o, part, ALU.add)
                    if 2 * m + n < tiles:
                        link(i)
                return i

            def inv_sqrt(out, var, std, tmp):
                link(dve.reciprocal(out, std))
                link(dve.tensor_tensor(tmp, out, out, ALU.mult))
                link(dve.tensor_tensor(tmp, tmp, var, ALU.mult))
                link(dve.tensor_scalar(tmp, tmp, -0.5, 1.5, ALU.mult, ALU.add))
                link(dve.tensor_tensor(out, out, tmp, ALU.mult))

            def take_group(g):
                units = group_units(g)
                kind, qt, h0 = UNITS[units[0]][:3]
                a, n = units[0], len(units)
                bank = 4 + g % 2
                dve.wait_ge(s_o, g + 1)
                if kind == "loc":
                    dve.tensor_tensor(sinksh, R("sink"), negmax[:, a:a + n], ALU.add).then_inc(s_sinkin, 1)
                    dve.wait_ge(s_esink, qt + 1)
                    link(dve.tensor_tensor(esum[:, a:a + n], esum[:, a:a + n], esink, ALU.add))
                link(dve.reciprocal(coef[:, 0:n], esum[:, a:a + n]))
                if kind == "diff":
                    o4 = y[:, 0, 0:512].rearrange("p (c w) -> p c w", c=4)
                    link(dve.tensor_tensor(o4, ps[:, bank, :].rearrange("p (c w) -> p c w", c=4),
                                           coef[:, 0:4].unsqueeze(2).to_broadcast([P, 4, P]), ALU.mult))
                    o2 = y[:, 0, 0:512].rearrange("p (h c w) -> p h c w", h=2, c=2)
                    dif = y[:, 1, 0:256].rearrange("p (h w) -> p h w", h=2)
                    sq = y[:, 1, 256:512].rearrange("p (h w) -> p h w", h=2)
                    for h in range(2):
                        i = dve.scalar_tensor_tensor(out=dif[:, h, :], in0=o2[:, h, 1, :], scalar=lamc, in1=o2[:, h, 0, :],
                                                     op0=ALU.mult, op1=ALU.add)
                    link(i)
                    link(dve.tensor_tensor(sq, dif, dif, ALU.mult))
                    link(dve.tensor_reduce(dms, sq, AX, ALU.add))
                    dve.tensor_scalar(drms, dms, 1.0 / P, LN_EPS, ALU.mult, ALU.add).then_inc(s_var, 1)
                    dve.wait_ge(s_std, g + 1)
                    inv_sqrt(drs, drms, dstd, dnw)
                    link(dve.tensor_tensor(dif, dif, drs.unsqueeze(2).to_broadcast([P, 2, P]), ALU.mult))
                    out = mix[:, qt, (h0 // 2) * P:(h0 // 2 + 2) * P].rearrange("p (h w) -> p h w", h=2)
                    link(dve.tensor_tensor(out, dif, R("subln").unsqueeze(1).to_broadcast([P, 2, P]), ALU.mult))
                    dve.tensor_scalar(out, out, 1.0 - LAM_INIT, None, ALU.mult).then_inc(s_odone, 1)
                    dve.wait_ge(s_odone, g + 1)
                    return
                if kind in ("slc", "win", "cmp"):
                    b = {"cmp": 0, "slc": 1, "win": 2}[kind]
                    gates = gate3[:, qt, :].rearrange("p (h b) -> p h b", b=3)[:, :, b]
                    link(dve.tensor_tensor(coef, coef, gates, ALU.mult))
                    if kind == "cmp":
                        link(dve.tensor_scalar(coef, coef, C("rowvalid")[:, qt:qt + 1], None, ALU.mult))
                    out = mix[:, qt, 512:1024]
                else:
                    out = mix[:, qt, h0 * HD:(h0 + 8) * HD]
                out3 = out.rearrange("p (h w) -> p h w", h=8)
                o3 = ps[:, bank, :].rearrange("p (h w) -> p h w", h=8)
                c3 = coef.unsqueeze(2).to_broadcast([P, 8, HD])
                if kind in ("win", "cmp"):
                    tmp = y[:, 0, 0:512].rearrange("p (h w) -> p h w", h=8)
                    link(dve.tensor_tensor(tmp, o3, c3, ALU.mult))
                    i = dve.tensor_tensor(out3, out3, tmp, ALU.add)
                else:
                    i = dve.tensor_tensor(out3, o3, c3, ALU.mult)
                i.then_inc(s_odone, 1)
                dve.wait_ge(s_odone, g + 1)

            def attention(name):
                a, b = INSTANCES[name]
                taken = 0
                for i in range(a, b + 5):
                    if i < b:
                        kind, qt, h, nk, _, _, _ = UNITS[i]
                        _, _, mask, _ = unit_operands(i)
                        dve.wait_ge(s_sc, i + 1)
                        if i >= 3:
                            dve.wait_ge(s_exp, i - 2)
                        first = negsink[:, h:h + 1] if kind == "loc" else 1e38
                        dve.tensor_tensor_reduce(out=masked[:, i % 3, 0:nk], in0=ps[:, i % 2, 0:nk], in1=mask,
                                                 scale=-1.0 if kind == "fox" else -SCALE, scalar=first,
                                                 op0=ALU.add, op1=ALU.min, accum_out=negmax[:, i:i + 1]).then_inc(s_mask, 1)
                    u = i - 2
                    if a <= u < b:
                        nk = UNITS[u][3]
                        n = P if nk >= P else nk
                        w = P * ((nk + P - 1) // P)
                        dve.wait_ge(s_pT, u + 1)
                        dve.tensor_copy(probT[0:n, u % 2, 0:w], ps[0:n, 2 + u % 2, 0:w]).then_inc(s_pTsb, 1)
                    u = i - 4
                    if a <= u < b and u == group_units(UNITS[u][6])[-1]:
                        take_group(UNITS[u][6])

            def stats(k, g_row, b_row, s_vec, v_vec, turned=True):
                for t in range(TT):
                    for half in range(2):
                        i = dve.bn_stats(bn[:, 2 * t + half, :], y[:, t, half * 512:(half + 1) * 512])
                link(i)
                for t in range(TT):
                    i = dve.bn_aggr(mv[:, t, :], bn[:, 2 * t:2 * t + 2, :])
                link(i)
                dve.tensor_scalar(var2, mv[:, :, 1], LN_EPS, None, ALU.add).then_inc(s_var, 1)
                dve.wait_ge(s_std, k)
                inv_sqrt(rstd, var2, std2, nwt)
                dve.wait_ge(s_vec, v_vec)
                for t in range(TT):
                    link(dve.scalar_tensor_tensor(out=y[:, t, :], in0=y[:, t, :], scalar=mv[:, t, 0:1], in1=g_row,
                                                  op0=ALU.subtract, op1=ALU.mult))
                    i = dve.scalar_tensor_tensor(out=x[:, t, :], in0=y[:, t, :], scalar=rstd[:, t:t + 1], in1=b_row,
                                                 op0=ALU.mult, op1=ALU.add)
                    if turned:
                        i.then_inc(s_rows, 1)
                if turned:
                    rows[0] += TT
                    dve.wait_ge(s_rows, rows[0])
                else:
                    link(i)

            rows = [0]

            def rows_ready(n=1):
                rows[0] += n
                dve.engine_nop().then_inc(s_rows, n)

            def normed():
                dve.engine_nop().then_inc(s_normed, 1)

            def residual(k):
                dve.wait_ge(s_used, FIRST[k] + 4)
                for t in range(TT):
                    for half in range(2):
                        cols = slice(half * 512, (half + 1) * 512)
                        i = dve.scalar_tensor_tensor(out=y[:, t, cols], in0=x[:, t, cols], scalar=ALPHA,
                                                     in1=ps[:, 2 * t + half, :], op0=ALU.mult, op1=ALU.add)
                link(i)
                dve.engine_nop().then_inc(s_restaken, 1)

            def mlp(layer):
                link(dve.tensor_scalar(y[:].rearrange("p t f -> p (t f)"), x[:].rearrange("p t f -> p (t f)"), ALPHA, None,
                                       ALU.mult))
                base = layer * 2 * MLP_STEPS
                with dve.Fori(0, MLP_STEPS) as it:
                    for j in range(2):
                        dve.wait_ge(s_relu, it * 2 + (base + j + 1 + EARLY))
                        h2 = hT[:, 4 * j:4 * j + 4, :].rearrange("p a c -> p (a c)")
                        dve.tensor_tensor(h2, h2, h2, ALU.mult).then_inc(s_hT, 1)
                    dve.wait_ge(s_used, it * 8 + (FIRST[f"mlp{layer}"] + 8))
                    dve.wait_ge(s_acc, it + (layer * MLP_STEPS + EARLY))
                    for t in range(TT):
                        for half in range(2):
                            cols = slice(half * 512, (half + 1) * 512)
                            i = dve.tensor_tensor(y[:, t, cols], ps[:, 2 * t + half, :], y[:, t, cols], ALU.add)
                    i.then_inc(s_acc, 1)
                dve.wait_ge(s_acc, (layer + 1) * MLP_STEPS + EARLY)

            for s in (s_relu, s_acc, s_mact, s_macc):
                dve.engine_nop().then_inc(s, EARLY)
            rows[0] = 2
            dve.wait_ge(s_x, 16)
            dve.engine_nop().then_inc(s_rows, 2)
            dve.wait_ge(s_const, 32)
            lam4 = R("lam").rearrange("p (a d) -> p a d", a=4)
            lp = y[:, 0, 0:2 * HD].rearrange("p (a d) -> p a d", a=2)
            link(dve.tensor_tensor(lp, lam4[:, 0:4:2, :], lam4[:, 1:4:2, :], ALU.mult))
            dve.tensor_reduce(lsum, lp, AX, ALU.add).then_inc(s_lam, 1)
            dve.wait_ge(s_lexp, 1)
            link(dve.tensor_tensor(lamc, lexp[:, 1:2], lexp[:, 0:1], ALU.subtract))
            link(dve.tensor_scalar(lamc, lamc, -LAM_INIT, None, ALU.add))
            take_turn("x0", xT)
            link(dve.tensor_scalar(negsink[:], R("sink"), -1.0, None, ALU.mult))
            dve.wait_ge(s_rot, 1)
            rope(qk[:, 0:4, :], raw[:, 0], 6, C("cos1"), C("sin1"), 4).then_inc(s_roped, 1)
            dve.wait_ge(s_rot, 2)
            dve.wait_ge(s_roped, 1)
            rope(qk[:, 4:8, :], raw[:, 1], 6, C("cos1"), C("sin1"), 4).then_inc(s_roped, 1)
            dve.wait_ge(s_rot, 3)
            dve.wait_ge(s_roped, 2)
            rope(qk[:, 8:12, :], raw[:, 0], 6, C("cos1"), C("sin1"), 4).then_inc(s_roped, 1)
            dve.wait_ge(s_rot, 4)
            dve.wait_ge(s_roped, 3)
            link(rope(qk[:, 16:18, :], raw[:, 1], 6, C("cos1"), C("sin1"), 2))
            for j in range(2):
                for g in range(2):
                    for o in range(2):
                        i = dve.tensor_copy(qk[o * HD:(o + 1) * HD, 12 + 2 * j + g, :], qk[g * HD:(g + 1) * HD, 16 + j, :])
            i.then_inc(s_roped, 1)
            dve.wait_ge(s_crot, 1)
            dve.tensor_tensor(kcd, kcraw, C("cosc"), ALU.mult)
            link(dve.tensor_tensor(kctmp, ps[:, 7, 0:2 * NCMP], C("sinc"), ALU.mult))
            dve.tensor_tensor(kcd, kcd, kctmp, ALU.add).then_inc(s_ckey, 1)
            attention("a0")
            rows_ready(2)
            take_turn("mix0", xT)
            residual("out_even")
            stats(5, vec[:, 0, :], vec[:, 1, :], s_vecA, 32)
            normed()
            take_turn("ln0", xT)
            mlp(0)
            stats(6, vec[:, 2, :], vec[:, 3, :], s_vecB, 32)
            normed()
            take_turn("ln1", xT)
            zmin, zabs, logf, csum, ones = (mix[0:16, i // 4, (i % 4) * 256:(i % 4 + 1) * 256] for i in range(5))
            dve.wait_ge(s_f, 1)
            fb = R("fbias", 16)
            link(dve.tensor_scalar(logf, ps[0:16, 7, 0:T], fb, None, ALU.add))
            dve.tensor_scalar(zmin, logf, 0.0, None, ALU.min)
            link(dve.tensor_scalar(ones, logf, 0.0, None, ALU.max))
            link(dve.tensor_tensor(zabs, ones, zmin, ALU.subtract))
            link(dve.memset(ones, 1.0))
            dve.engine_nop().then_inc(s_fdve, 1)
            dve.wait_ge(s_fact, 1)
            link(dve.tensor_tensor(logf, zmin, zabs, ALU.subtract))
            link(dve.tensor_tensor_scan(csum, ones, logf, 0.0, ALU.mult, ALU.add))
            link(dve.tensor_scalar(zmin, csum, -1.0, None, ALU.mult))
            link(dve.memset(foxq[64:66, :, :], 1.0))
            link(dve.memset(foxk[64:66, :, :], 1.0))
            dve.engine_nop().then_inc(s_fdve, 1)
            attention("a1")
            rows_ready(2)
            take_turn("mix1", xT)
            residual("out_odd")
            stats(7, vec[:, 0, :], vec[:, 1, :], s_vecA, 64)
            normed()
            take_turn("ln2", xT)
            dve.wait_ge(s_csil, 1)
            dve.tensor_copy(cb, csil[:, :, 0:1].to_broadcast([P, KT, P])).then_inc(s_cb, 1)
            mlp(1)
            stats(8, vec[:, 2, :], vec[:, 3, :], s_vecB, 64, turned=False)
            normed()
            dve.wait_ge(s_ss, 1)
            dve.tensor_scalar(var2, var_c, 1.0 / D, RMS_EPS, ALU.mult, ALU.add).then_inc(s_var, 1)
            dve.wait_ge(s_std, 9)
            inv_sqrt(rstd, var2, std2, nwt)
            for t in range(TT):
                link(dve.tensor_scalar(ctxr[:, t, :], ctxr[:, t, :], rstd[:, t:t + 1], None, ALU.mult))
            dve.wait_ge(s_ss, 2)
            dve.tensor_scalar(var2, ss, 1.0 / D, RMS_EPS, ALU.mult, ALU.add).then_inc(s_var, 1)
            dve.wait_ge(s_std, 10)
            inv_sqrt(rstd, var2, std2, nwt)
            for t in range(TT):
                link(dve.tensor_scalar(y[:, t, :], x[:, t, :], rstd[:, t:t + 1], None, ALU.mult))
            rows_ready(4)
            dve.wait_ge(s_used, FIRST["ada"] + 24)
            bada = R("bada").rearrange("p (i m) -> p i m", i=6)
            for i, s in enumerate((0, 1, 3, 4)):
                ins = dve.tensor_tensor(modT[:, 8 * i:8 * i + 8, :], ps[:, 6, 16 * i:16 * i + 16].rearrange("p (m c) -> p m c", c=2),
                                        bada[:, s, :].unsqueeze(2).to_broadcast([P, 8, 2]), ALU.add)
            link(ins)
            dve.engine_nop().then_inc(s_mod, 1)
            n1, n2 = R("norm1"), R("norm2")
            for c in range(2):
                dve.scalar_tensor_tensor(out=amod[:, 8 * c:8 * c + 8], in0=modT[:, 8:16, c], scalar=1.0, in1=n1,
                                         op0=ALU.add, op1=ALU.mult)
            link(dve.scalar_tensor_tensor(out=amod[:, 16:24], in0=modT[:, 24:32, 0], scalar=1.0, in1=n2, op0=ALU.add,
                                          op1=ALU.mult))
            dve.engine_nop().then_inc(s_mod, 1)
            dve.wait_ge(s_vecA, 96)
            for i in range(2):
                for half in range(2):
                    cols = slice(half * 512, (half + 1) * 512)
                    ins = dve.tensor_tensor(vec[:, i, cols], ps[:, 2 * i + half, :], vec[:, i, cols], ALU.add)
            link(ins)
            dve.engine_nop().then_inc(s_mod, 1)
            take_turn_mod("rms1", xT, amod[:, 0:8], modT[:, 0:8, 0])
            take_turn_mod("ctx", cT, amod[:, 8:16], modT[:, 0:8, 1])
            dve.wait_ge(s_rot, 5)
            rope(qk[:, 0:4, :], raw[:, 0], 6, C("cos2"), C("sin2"), 4).then_inc(s_roped, 1)
            dve.wait_ge(s_rot, 6)
            dve.wait_ge(s_roped, 5)
            link(rope(qk[:, 4:5, :], raw[:, 1], 0, C("cos2"), C("sin2"), 1))
            for g in range(2):
                for o in range(2):
                    i = dve.tensor_copy(qk[o * HD:(o + 1) * HD, 5 + g, :], qk[g * HD:(g + 1) * HD, 4, :])
            i.then_inc(s_roped, 1)
            attention("a2")
            rows_ready(2)
            take_turn("mix2", xT, 4)
            dve.engine_nop().then_inc(s_xTv, 2)
            dve.wait_ge(s_used, FIRST["out_2"] + 4)
            for t in range(TT):
                for half in range(2):
                    cols = slice(half * 512, (half + 1) * 512)
                    i = dve.tensor_tensor(y[:, t, cols], ps[:, 2 * t + half, :], vec[:, 0, cols], ALU.mult)
            link(i)
            for t in range(TT):
                i = dve.tensor_tensor(x[:, t, :], x[:, t, :], y[:, t, :], ALU.add)
            link(i)
            dve.engine_nop().then_inc(s_restaken, 1)
            dve.wait_ge(s_ss, 3)
            dve.tensor_scalar(var2, ss, 1.0 / D, RMS_EPS, ALU.mult, ALU.add).then_inc(s_var, 1)
            dve.wait_ge(s_std, 11)
            inv_sqrt(rstd, var2, std2, nwt)
            for t in range(TT):
                link(dve.tensor_scalar(y[:, t, :], x[:, t, :], rstd[:, t:t + 1], None, ALU.mult))
            rows_ready(2)
            take_turn_mod("rms2", xT, amod[:, 16:24], modT[:, 16:24, 0])
            link(dve.memset(y[:].rearrange("p t f -> p (t f)"), 0.0))
            link(dve.memset(weight[:].rearrange("p t e -> p (t e)"), 1.0))
            dve.wait_ge(s_score, 1)
            e3 = [P, TT, NEXP]
            link(dve.tensor_tensor(biased[:], score[:], R("rbias").unsqueeze(1).to_broadcast(e3), ALU.add))
            for t in range(TT):
                for g in range(8):
                    link(dve.max(top8[:, t, :], biased[:, t, 8 * g:8 * g + 8]))
                    link(dve.tensor_tensor(gsc[:, t, g:g + 1], top8[:, t, 0:1], top8[:, t, 1:2], ALU.add))
                link(dve.max(top8[:, t, :], gsc[:, t, :]))
                link(dve.max_index(gidx[:, t, :], top8[:, t, :], gsc[:, t, :]))
            link(dve.tensor_copy(gidxf[:], gidx[:]))
            for t in range(TT):
                link(dve.tensor_scalar(gmask[:, t, :], C("iota8"), gidxf[:, t, 0:1], None, ALU.is_equal))
                for r in range(1, 4):
                    link(dve.scalar_tensor_tensor(out=gmask[:, t, :], in0=C("iota8"), scalar=gidxf[:, t, r:r + 1],
                                                  in1=gmask[:, t, :], op0=ALU.is_equal, op1=ALU.add))
                b8 = biased[:, t, :].rearrange("p (g e) -> p g e", g=8)
                m8 = gmask[:, t, :].unsqueeze(2).to_broadcast([P, 8, 8])
                c8 = chosen[:, t, :].rearrange("p (g e) -> p g e", g=8)
                link(dve.tensor_tensor(b8, b8, m8, ALU.mult))
                link(dve.tensor_scalar(c8, m8, -1.0, 1e30, ALU.add, ALU.mult))
                link(dve.tensor_tensor(b8, b8, c8, ALU.add))
                link(dve.max(top8b[:, t, :], biased[:, t, :]))
                link(dve.match_replace(chosen[:, t, :], top8b[:, t, :], biased[:, t, :], 3e30))
            link(dve.tensor_scalar(chosen[:], chosen[:], 2e30, None, ALU.is_ge))
            link(dve.tensor_tensor(score[:], score[:], chosen[:], ALU.mult))
            link(dve.tensor_reduce(wsum, score[:], AX, ALU.add))
            link(dve.reciprocal(wsum, wsum))
            for t in range(TT):
                i = dve.tensor_scalar(weight[:, t, 1:NEXP + 1], score[:, t, :], wsum[:, t:t + 1], ROUTED_SCALE, ALU.mult,
                                      ALU.mult)
            link(i)

            def expert_act(odd):
                dve.tensor_tensor(actT[:, 2 * odd, :, :].rearrange("p t c -> p (t c)"), sg[:, odd, :],
                                  ps[:, 5 + 2 * odd, :], ALU.mult).then_inc(s_mact, 1)

            def expert_add(w):
                for t in range(TT):
                    for half in range(2):
                        cols = slice(half * 512, (half + 1) * 512)
                        i = dve.scalar_tensor_tensor(out=y[:, t, cols], in0=ps[:, 2 * t + half, :], scalar=w[t],
                                                     in1=y[:, t, cols], op0=ALU.mult, op1=ALU.add)
                i.then_inc(s_macc, 1)

            dve.wait_ge(s_msilu, 1)
            expert_act(0)
            with dve.Fori(0, NEXP // 8) as it:
                for j in range(8):
                    dve.wait_ge(s_msilu, it * 8 + (j + 2))
                    expert_act((j + 1) % 2)
                    dve.wait_ge(s_used, it * 24 + (FIRST["moe"] + 3 * j + 5))
                    dve.wait_ge(s_macc, it * 8 + (j + EARLY))
                    expert_add([weight[:, t, bass.ds(it * 8 + j, 1)] for t in range(TT)])
            dve.wait_ge(s_used, CHUNKS)
            dve.wait_ge(s_macc, NEXP + EARLY)
            expert_add([weight[:, t, NEXP:NEXP + 1] for t in range(TT)])
            dve.wait_ge(s_macc, NEXP + 1 + EARLY)
            link(dve.tensor_tensor(y[:], y[:], vec[:, 1:2, :].to_broadcast([P, TT, D]), ALU.mult))
            link(dve.tensor_tensor(x[:], x[:], y[:], ALU.add))
            dve.engine_nop().then_inc(s_macc, 1)
            dve.wait_ge(s_ss, 4)
            dve.tensor_scalar(var2, ss, 1.0 / D, RMS_EPS, ALU.mult, ALU.add).then_inc(s_var, 1)
            dve.wait_ge(s_std, 12)
            inv_sqrt(rstd, var2, std2, nwt)
            dve.wait_ge(s_vecB, 80)
            for t in range(TT):
                i = dve.scalar_tensor_tensor(out=x[:, t, :], in0=x[:, t, :], scalar=rstd[:, t:t + 1], in1=vec[:, 2, :],
                                             op0=ALU.mult, op1=ALU.mult)
                i.then_inc(s_normed, 1)

        @block.gpsimd
        def _(pool):
            def row(dst, src, s):
                pool.dma_start(dst, src.to_broadcast([P, D])).then_inc(s, 16)

            for i in range(2):
                row(vec[:, 2 * i, :], d_gain[0, i:i + 1, :], s_vecB if i else s_vecA)
                row(vec[:, 2 * i + 1, :], d_bias[0, i:i + 1, :], s_vecB if i else s_vecA)
            pool.wait_ge(s_const, 32)
            pool.wait_ge(s_projsb, 5)
            pe3 = R("pe").rearrange("p (j m) -> p j m", j=2)
            for j in range(2):
                for g in range(2):
                    pool.tensor_copy(cmpin[:, j, :, g, :], windows(XS(j), g)).then_inc(s_pool, 1)
                    pool.wait_ge(s_pool, 2 * j + g + 1)
                    pool.tensor_tensor(cmpin[:, j, :, g, :], cmpin[:, j, :, g, :],
                                       pe3[:, j, :].unsqueeze(2).to_broadcast([P, 16, NCMP]), ALU.add).then_inc(s_blk, 1)
            pool.wait_ge(s_normed, 1)
            row(vec[:, 0, :], d_gain[1, 0:1, :], s_vecA)
            row(vec[:, 1, :], d_bias[1, 0:1, :], s_vecA)
            pool.wait_ge(s_normed, 2)
            row(vec[:, 2, :], d_gain[1, 1:2, :], s_vecB)
            row(vec[:, 3, :], d_bias[1, 1:2, :], s_vecB)
            pool.wait_ge(s_fdve, 2)
            pool.dma_start(foxq[65:66, :, :], mix[0:16, 0, 768:1024]).then_inc(s_caug, 16)
            pool.dma_start(foxk[64:65, :, :], mix[0:16, 0, 0:256]).then_inc(s_caug, 16)
            pool.wait_ge(s_normed, 3)
            pool.dma_start(ctxr, d_ctx.rearrange("(t p) f -> p t f", p=P)).then_inc(s_ctx, 16)
            row(vec[:, 0, :], d_badarow[0:1, 0:D], s_vecA)
            row(vec[:, 1, :], d_badarow[0:1, D:2 * D], s_vecA)
            pool.wait_ge(s_normed, 4)
            row(vec[:, 2, :], d_final[0:1, :], s_vecB)
            pool.wait_ge(s_turn, TURN_AT["rms1"] + 4)
            pool.dma_start(poolmat, d_pool).then_inc(s_poolmat, 16)
            pool.wait_ge(s_vecA, 96)
            pool.wait_ge(s_vecB, 80)


def rope_tables(positions_and_freqs, rows):
    n = len(positions_and_freqs[0][0])
    cos, sin = np.ones((rows, n)), np.zeros((rows, n))
    for pos, inv, at in positions_and_freqs:
        ang = inv[:, None] * pos[None, :]
        for half in range(2):
            a = at + half * len(inv)
            cos[a:a + len(inv)], sin[a:a + len(inv)] = np.cos(ang), np.sin(ang)
    return cos, sin


def rotation(pairs):
    rot = np.zeros((P, P))
    for at, half in pairs:
        for i in range(half):
            rot[at + i, at + half + i] = -1.0
            rot[at + half + i, at + i] = 1.0
    return rot.T


def shape_constants():
    f = np.float32
    pos = np.arange(T).astype(f)
    inv1 = (f(500000.0) ** (-np.arange(8, dtype=f) / f(8))).astype(f)
    inv2 = (f(10000.0) ** (-np.arange(16, dtype=f) / f(16))).astype(f)
    cpos = (np.arange(NCMP) * 16 + 31).astype(f)
    c1, s1 = rope_tables([(pos, inv1, 0), (pos, inv1, HD)], P)
    cc, sc = rope_tables([(np.tile(cpos, 2), inv1, 0), (np.tile(cpos, 2), inv1, HD)], P)
    row, col = np.arange(T) // 64, np.arange(T) % 64
    c2, s2 = rope_tables([(p.astype(f), inv2, h * HD + o) for h in range(2) for p, o in ((row, 0), (col, 32))], P)
    q = np.arange(T).reshape(TT, P)
    k = np.arange(T)
    causal = np.where(k[None, None] <= q[:, :, None], 0.0, BIG)
    local = np.concatenate([np.where(np.abs(q[:, :, None] - k[None, None]) <= 128, 0.0, BIG), np.zeros((TT, P, T))], 2)
    valid = (np.arange(NCMP) * 16 + 31)[None, None] <= q[:, :, None]
    rows = lambda a: np.moveaxis(a, 0, 1).reshape(P, -1)
    parts = {
        "ident": np.eye(P), "rot1": rotation([(0, 8), (HD, 8)]), "rot2": rotation([(h * 32, 16) for h in range(4)]),
        "cos1": c1, "sin1": s1, "cos2": c2, "sin2": s2, "cosc": cc, "sinc": sc,
        "causal": rows(causal), "local": rows(local), "cmpmask": rows(np.where(valid, 0.0, BIG)),
        "rowvalid": rows(valid.any(2)[:, :, None].astype(f)), "iota8": np.tile(np.arange(8), (P, 1)),
    }
    consts = np.concatenate([parts[n] for n, _ in CONSTS], 1).astype(f)
    pool = np.zeros((4, T, T))
    for g, w in enumerate(POOL_WINDOWS):
        for t in range(T):
            lo, hi = max(t - w // 2, 0), min(t - w // 2 + w, T)
            pool[g, lo:hi, t] = 1.0 / (hi - lo)
            pool[g, t, t] -= 1.0
    pool = pool.reshape(4, TT, P, T).transpose(2, 0, 1, 3).astype(f)
    return np.ascontiguousarray(consts), np.ascontiguousarray(pool)


def k_major(w):
    return w.reshape(-1, P, w.shape[1]).transpose(1, 0, 2)


def panels(w, width, k_per):
    w = k_major(w)
    return [w[:, k:k + k_per, c:c + width] for c in range(0, w.shape[2], width) for k in range(0, w.shape[1], k_per)]


def lay_out_stream(a):
    chunks = []
    even = a["w_in_even"][0]
    chunks += panels(even[:, 0:2560], 512, 4) + panels(even[:, 2560:2816], 256, 8)
    for j in range(2):
        chunks += panels(a["nsa_cmp_w1"][0, j], 256, 8)
    for layer in range(2):
        if layer:
            chunks += panels(a["w_in_odd"][0][:, 0:3072], 512, 4)
        chunks += panels(a["w_out_odd" if layer else "w_out_even"][0], 1024, 2)
        up, down = a["mlp_w_up"][layer], a["mlp_w_down"][layer]
        for i in range(MLP_STEPS):
            chunks += panels(up[:, 1024 * i:1024 * (i + 1)], 512, 4) + panels(down[1024 * i:1024 * (i + 1)], 1024, 2)
    chunks += panels(a["w_ada_2"][0], 512, 4)
    w_in = a["w_in_2"][0]
    chunks += panels(w_in[:, 0:512], 512, 4) + panels(w_in[:, 512:768], 256, 8) + panels(w_in[:, 768:1280], 512, 4)
    chunks += panels(a["w_out_2"][0], 1024, 2)
    ups = [panels(np.concatenate([a["ws_gate_2"][0], a["ws_up_2"][0]], 1), 512, 4)]
    downs = [panels(a["ws_down_2"][0], 1024, 2)]
    for e in range(NEXP):
        ups.append(panels(np.concatenate([a["w_gate_2"][0, e], a["w_up_2"][0, e]], 1), 512, 4))
        downs.append(panels(a["w_down_2"][0, e], 1024, 2))
    chunks += ups[0]
    for e in range(NEXP):
        chunks += ups[e + 1] + downs[e]
    chunks += downs[NEXP]
    stream = np.empty((CHUNKS, P, SLOT), np.float32)
    for n, c in enumerate(chunks):
        stream[n] = c.reshape(P, SLOT)
    return stream


def lay_out_params(a):
    wide = lambda r: np.tile(r.reshape(1, -1), (P, 1))
    cols = lambda r: r.reshape(-1, P).T
    flat = lambda r: r.reshape(P, -1)
    w2 = a["nsa_cmp_w2"][0]
    fbias = np.zeros((P, 1), np.float32)
    fbias[0:16, 0] = a["fox_f_bias"][0]
    parts = {
        "pe": flat(a["nsa_pe"][0].reshape(2, 16, P).transpose(2, 0, 1)),
        "b1": cols(a["nsa_cmp_b1"][0]),
        "w2k": flat(np.concatenate([k_major(w2[0])] * 2, 2)),
        "w2v": flat(k_major(w2[1])),
        "wgate": flat(k_major(a["w_in_even"][0][:, 2816:2840])),
        "wforget": flat(k_major(a["w_in_odd"][0][:, 3072:3088])),
        "router": flat(k_major(a["w_router_2"][0])),
        "rbias": wide(a["router_bias_2"][0]),
        "poolw": flat(a["pool_w_2"][0].transpose(1, 0, 2)),
        "poolscale": cols(a["pool_scale_2"][0]),
        "cvec": flat(np.stack([cols(a["c_2"][0]), cols(a["c_ctx_2"])], 2)),
        "bada": cols(a["b_ada_2"][0]),
        "norm1": cols(a["norm1_g_2"][0]), "norm2": cols(a["norm2_g_2"][0]),
        "sink": wide(a["attn_sink_2"][0]), "lam": wide(a["diff_lambda"][0]), "subln": wide(a["diff_subln"][0]),
        "fbias": fbias,
    }
    return np.ascontiguousarray(np.concatenate([parts[n] for n, _ in PARAMS], 1))


def kernel(**inputs):
    import concourse.bacc as bacc
    from concourse.bass_utils import run_bass_kernel_spmd

    a = {name: np.asarray(value) for name, value in inputs.items()}
    consts, pool = shape_constants()
    b_ada = a["b_ada_2"][0]
    arrays = {
        "stream": lay_out_stream(a), "params": lay_out_params(a), "consts": consts, "poolmat": pool,
        "x": np.ascontiguousarray(a["x"][0]), "ctx": np.ascontiguousarray(a["ctx_2"][0]),
        "gain": np.ascontiguousarray(a["ln_gain"]), "bias": np.ascontiguousarray(a["ln_bias"]),
        "badarow": np.ascontiguousarray(np.concatenate([b_ada[2 * D:3 * D], b_ada[5 * D:6 * D]]).reshape(1, -1)),
        "final": np.ascontiguousarray(a["final_g_2"].reshape(1, -1)),
    }
    nc = bacc.Bacc("TRN2", target_bir_lowering=False, num_devices=1)
    aps = [nc.dram_tensor(f"in_{n}", v.shape, F32, kind="ExternalInput").ap() for n, v in arrays.items()]
    out = nc.dram_tensor("out_0", (T, D), F32, kind="ExternalOutput").ap()
    build(nc, *aps, out)
    r = run_bass_kernel_spmd(nc, [{f"in_{n}": v for n, v in arrays.items()}], core_ids=[0])
    return r.results[0]["out_0"].reshape(1, T, D)
```

```python
from contextlib import ExitStack
import math

import numpy as np

import concourse.bass as bass
from concourse import mybir

F32 = mybir.dt.float32
U32 = mybir.dt.uint32
ALU = mybir.AluOpType
ACT = mybir.ActivationFunctionType
AX = mybir.AxisListType.X

P = 128
D = 1024
T = 256
TT = T // P
KT = D // P
HD = 64
FF = 4096
SLOT = 2048
RING = 8
BIG = -1e30
LN_EPS = 1e-5
RMS_EPS = 1e-6
ALPHA = 4.0 ** 0.25
LAM_INIT = 0.8 - 0.6 * math.exp(-0.3 * 0)
NCMP = (T - 32) // 16 + 1
NEXP = 64
ROUTED_SCALE = 2.5
POOL_WINDOWS = (2, 4, 8, 16)
SCALE = HD ** -0.5

MLP_STEPS = 4
EARLY = 1
SECTIONS = [
    ("in_even", 11), ("cmp", 4), ("out_even", 4), ("mlp0", 8 * MLP_STEPS),
    ("in_odd", 12), ("out_odd", 4), ("mlp1", 8 * MLP_STEPS),
    ("ada", 24), ("in_2", 5), ("out_2", 4), ("shared", 3), ("moe", 3 * NEXP),
]
FIRST = {}
_n = 0
for _name, _count in SECTIONS:
    FIRST[_name] = _n
    _n += _count
CHUNKS = _n
RINGED = FIRST["moe"]

CAP = HD
ROUNDS = T // CAP - 1
NOV = ROUNDS * NEXP
MOE_SLOTS = 12
STEPS = NEXP // 4
MAX_MORE = (T * 8 // (CAP + 1) + 3) // 4

PARAMS = [
    ("pe", 32), ("b1", 4), ("w2k", 256), ("w2v", 128), ("wgate", 192), ("wforget", 128),
    ("router", 512), ("rbias", 64), ("poolw", 512), ("poolscale", 4), ("cvec", 16), ("bada", 48),
    ("norm1", 8), ("norm2", 8), ("sink", 8), ("lam", 256), ("subln", 128), ("fbias", 1),
]
CONSTS = [
    ("ident", 128), ("rot1", 128), ("rot2", 128), ("cos1", 256), ("sin1", 256), ("cos2", 256), ("sin2", 256),
    ("cosc", 2 * NCMP), ("sinc", 2 * NCMP), ("causal", 512), ("local", 1024), ("cmpmask", 2 * NCMP),
    ("rowvalid", 2), ("iota8", 8), ("iota1", CAP), ("before", P), ("ones", P), ("place1", 1), ("expert", NOV),
    ("evens4", MAX_MORE),
]


def columns(blocks):
    at, n = {}, 0
    for name, width in blocks:
        at[name] = (n, width)
        n += width
    return at, n


PARAM_AT, NPARAM = columns(PARAMS)
CONST_AT, NCONST = columns(CONSTS)
TURNS = ["x0", "mix0", "ln0", "ln1", "mix1", "ln2", "rms1", "ctx", "mix2", "rms2"]
TURN_AT = {name: 4 * i for i, name in enumerate(TURNS)}


def attention_units():
    units = []
    group = 0
    for qt in range(TT):
        for h0 in (0, 4):
            for c in range(4):
                units.append(("diff", qt, h0 + c, P * (qt + 1), c * 128, 128, group))
            group += 1
    for kind in ("slc", "win", "cmp"):
        for qt in range(TT):
            for h in range(8):
                units.append((kind, qt, h, NCMP if kind == "cmp" else P * (qt + 1), h * HD, HD, group))
            group += 1
    for qt in range(TT):
        for h0 in (0, 8):
            for h in range(8):
                units.append(("fox", qt, h0 + h, P * (qt + 1), h * HD, HD, group))
            group += 1
    for qt in range(TT):
        for h in range(8):
            units.append(("loc", qt, h, 2 * T, h * HD, HD, group))
        group += 1
    return units


UNITS = attention_units()
INSTANCES = {"a0": (0, 64), "a1": (64, 96), "a2": (96, 112)}


def group_units(g):
    return [u for u, unit in enumerate(UNITS) if unit[6] == g]


def build(nc, d_stream, d_params, d_consts, d_pool, d_x, d_ctx, d_gain, d_bias, d_badarow, d_final, d_out):
    with ExitStack() as ctx:
        def sb(name, shape, dt=F32):
            return ctx.enter_context(nc.sbuf_tensor(name, shape, dt))

        def sem(name):
            return ctx.enter_context(nc.semaphore(name))

        ring = sb("ring", [P, RING, SLOT])
        par = sb("par", [P, NPARAM])
        con = sb("con", [P, NCONST])
        x = sb("x_rows", [P, TT, D])
        y = sb("y_rows", [P, TT, D])
        mix = sb("mix_rows", [P, TT, D])
        xT = sb("xT", [P, KT, T])
        qk = sb("qk_tiles", [P, 32, T])
        v = sb("v_rows", [P, TT, D])
        masked = sb("masked", [P, 4, 512])
        prob = sb("prob", [P, 3, 512])
        probT = sb("probT", [P, 2, 512])
        vec = sb("vec_rows", [P, 4, D])
        negmax = sb("negmax", [P, len(UNITS)])
        esum = sb("esum", [P, len(UNITS)])
        small = sb("small", [P, 160])
        gate3 = sb("gate3", [P, TT, 24])
        vcmp = sb("vcmp", [P, 2, HD])
        negsink = sb("negsink", [P, 8])
        csil = sb("csil", [P, KT, 2])
        modT = sb("modT", [P, 32, 2])
        amod = sb("amod", [P, 48])
        sched = nc.dram_tensor("schedule", (P + 1, 1), mybir.dt.int32, kind="Internal").ap()
        score = sb("score", [P, TT, NEXP])
        biased = sb("biased", [P, TT, NEXP])
        chosen = sb("chosen", [P, TT, NEXP])
        weight = sb("weight", [P, TT, NEXP + 8])
        ps = ctx.enter_context(nc.psum_tensor("ps", [P, 8, 512], F32))

        s_full = [sem(f"slot_full{i}") for i in range(RING)]
        s_used = sem("chunks_used")
        s_const = sem("consts_loaded")
        s_x = sem("x_loaded")
        s_ctx = sem("ctx_loaded")
        s_poolmat = sem("poolmat_loaded")
        s_vecA = sem("vecA_loaded")
        s_vecB = sem("vecB_loaded")
        s_out = sem("out_stored")
        s_rows = sem("rows_ready")
        s_turn = sem("turned_psum")
        s_xT = sem("xT_by_act")
        s_xTv = sem("xT_by_dve")
        s_gates = sem("gates_psum")
        s_projsb = sem("proj_sbuf")
        s_rot = sem("rotated_psum")
        s_roped = sem("roped")
        s_blk = sem("cmp_blocks")
        s_hidsb = sem("cmp_hidden_sbuf")
        s_cmp = sem("cmp_kv_psum")
        s_cmpsb = sem("cmp_kv_sbuf")
        s_crot = sem("cmp_rotated")
        s_ckey = sem("cmp_keys_ready")
        s_sc = sem("scores_psum")
        s_mask = sem("masked_ready")
        s_exp = sem("exp_ready")
        s_pT = sem("probT_psum")
        s_pTsb = sem("probT_sbuf")
        s_o = sem("outs_psum")
        s_odone = sem("outs_taken")
        s_restaken = sem("residual_taken")
        s_var = sem("variance_ready")
        s_std = sem("std_ready")
        s_normed = sem("norms_done")
        s_relu = sem("mlp_relu")
        s_hT = sem("mlp_hidden")
        s_acc = sem("mlp_added")
        s_f = sem("forget_psum")
        s_fact = sem("forget_act")
        s_fdve = sem("forget_dve")
        s_caug = sem("forget_rows_placed")
        s_csil = sem("c_silu")
        s_cb = sem("c_rows_ready")
        s_mod = sem("mod_ready")
        s_ss = sem("square_sums")
        s_dps = sem("pool_psum")
        s_dsb = sem("pool_sbuf")
        s_esink = sem("sink_exp")
        s_sinkin = sem("sink_shifted")
        s_lam = sem("lambda_sums")
        s_lexp = sem("lambda_exps")
        s_rps = sem("router_psum")
        s_score = sem("router_scores")
        s_shsilu = sem("shared_silu")
        s_shact = sem("shared_act")
        s_h2 = sem("h2_rows_psum")
        s_h2sb = sem("h2_rows_sbuf")
        s_chosen = sem("experts_chosen")
        s_rank = sem("ranks_psum")
        s_sched = sem("schedule_ready")
        s_schedm = sem("schedule_in_memory")
        s_pick = sem("picked_columns")
        s_sel = sem("selection_ready")
        s_gather = sem("gathered_psum")
        s_hga = sem("gathered_by_act")
        s_hgv = sem("gathered_by_dve")
        s_silu = sem("expert_silu")
        s_hid2 = sem("expert_hidden")
        s_tps = sem("expert_turned_psum")
        s_tsb = sem("expert_turned_sbuf")
        s_ya = sem("slot_rows_by_act")
        s_yv = sem("slot_rows_by_dve")
        s_moe = sem("experts_summed")
        s_xfin = sem("x_final")
        m_full = [sem(f"expert_slot_full{i}") for i in range(MOE_SLOTS)]
        s_dve = sem("dve_chain")
        s_act = sem("act_chain")
        s_pool = sem("pool_chain")

        def windows(tiles, g):
            row = tiles[:, g, :]
            return bass.AP(row.tensor, row.offset, [row.ap[0], (2, 16), (16, NCMP)])

        def C(name, p=P):
            a, w = CONST_AT[name]
            return con[0:p, a:a + w]

        def R(name, p=P):
            a, w = PARAM_AT[name]
            return par[0:p, a:a + w]

        ident = C("ident")
        raw = masked[:].rearrange("p a b -> p (a b)").rearrange("p (s t c) -> p s t c", s=2, t=4)
        lamc = small[:, 0:1]
        var2 = small[:, 2:4]
        std2 = small[:, 4:6]
        rstd = small[:, 6:8]
        nwt = small[:, 8:10]
        mv = small[:, 10:14].rearrange("p (t s) -> p t s", t=2)
        bn = small[:, 16:40].rearrange("p (a s) -> p a s", a=4)
        ss = small[:, 40:42]
        lsum = small[:, 42:44]
        lexp = small[:, 44:46]
        coef = small[:, 48:56]
        dms = small[:, 56:58]
        top8 = small[:, 64:80].rearrange("p (t k) -> p t k", t=2)
        esink = small[:, 80:88]
        sinksh = small[:, 88:96]
        gsc = small[:, 96:112].rearrange("p (t k) -> p t k", t=2)
        gmask = small[:, 112:128].rearrange("p (t k) -> p t k", t=2)
        wsum = small[:, 128:130]
        var_c = small[:, 130:132]
        top8b = small[:, 136:152].rearrange("p (t k) -> p t k", t=2)
        drms = small[:, 152:154]
        dstd = small[:, 154:156]
        drs = small[:, 156:158]
        dnw = small[:, 158:160]
        gidx = sb("gidx", [P, TT, 8], U32)
        gidxf = sb("gidxf", [P, TT, 8])

        hT = qk[:, 0:8, :]
        XS = lambda j: qk[:, 20 + 2 * j:22 + 2 * j, :]
        cmpin = qk[:, 24:28, :].rearrange("p a b -> p (a b)")[:, 0:2 * 16 * 2 * NCMP].rearrange(
            "p (j m g n) -> p j m g n", j=2, m=16, g=2)
        kcraw = qk[:, 28, 0:2 * NCMP]
        kcd = qk[:, 28, 32:32 + 2 * NCMP]
        hidT = qk[:, 29, 0:4 * 2 * NCMP].rearrange("p (j t n) -> p j t n", j=2, t=2)
        kctmp = qk[:, 28, 64:64 + 2 * NCMP]
        foxq = qk[0:66, 0:16, :]
        foxk = qk[0:66, 16:32, :]
        ctxr = qk[:, 24:32, :].rearrange("p a b -> p (a b)").rearrange("p (t f) -> p t f", t=2)
        cT = qk[:, 16:24, :]
        poolmat = y[:].rearrange("p t f -> p (t f)").rearrange("p (g t c) -> p g t c", g=4, t=2)
        dT = qk[:, 9:13, :]
        cb = masked[:, 0:2, :].rearrange("p a b -> p (a b)").rearrange("p (k c) -> p k c", k=KT)
        qslots = qk[:].rearrange("p a b -> p (a b)").rearrange("p (s c) -> p s c", c=SLOT)
        moe_slot = lambda i: ring[:, i, :] if i < RING else qslots[:, i - RING, :]
        h2 = mix
        hg = masked[:, 0:2, :].rearrange("p a b -> p (a b)").rearrange("p (k c) -> p k c", k=KT)
        yslot = masked[:, 2:4, :].rearrange("p a b -> p (a b)")
        select = prob[:, 0, :].rearrange("p (s t c) -> p s t c", s=2, t=2)
        selectw = prob[:, 1, :].rearrange("p (s t c) -> p s t c", s=2, t=2)
        act2 = prob[:, 2, 0:256]
        sg2 = prob[:, 2, 256:512]
        shactT = v[:, 0, 0:512].rearrange("p (k c) -> p k c", k=2)
        shsg = v[:, 0, 512:1024]
        vflat = v[:, 1, :]
        rank1 = vflat[:, 0:128].rearrange("p (t e) -> p t e", t=2)
        over = vflat[:, 128:128 + NOV]
        overpos = vflat[:, 320:320 + NOV]
        onehot = vflat[:, 512:512 + NOV]
        scratch = vflat[:, 704:704 + NOV]
        colr = vflat[:, 900:904].rearrange("p (t s) -> p t s", t=2)
        colw = vflat[:, 904:908].rearrange("p (t s) -> p t s", t=2)
        kcount = vflat[:, 908:909]
        schedf = vflat[:, 909:911]
        tot = vflat[:, 911:912]
        rankr = y[:, 1, 0:2 * NOV].rearrange("p (t f) -> p t f", t=2)
        weightr = y[:, 1, 2 * NOV:4 * NOV].rearrange("p (t f) -> p t f", t=2)
        schedi = sb("schedule_ids", [P, 2], mybir.dt.int32)

        causal = C("causal").rearrange("p (q k) -> p q k", q=2)
        local = C("local").rearrange("p (q k) -> p q k", q=2)
        cmpmask = C("cmpmask").rearrange("p (q k) -> p q k", q=2)

        def unit_operands(u):
            kind, qt, h, nk, _, w, _ = UNITS[u]
            qs = slice(qt * P, (qt + 1) * P)
            lo = HD * (h % 2)
            half = slice(lo, lo + HD)
            g = h // 4
            tiles = range(qt + 1)
            if kind == "diff":
                return (qk[half, h // 2, qs], [(qk[half, 4 + h // 2, 0:nk], 0)], causal[:, qt, 0:nk],
                        [v[:, t, (h // 2) * P:(h // 2 + 1) * P] for t in tiles])
            if kind == "slc":
                return (qk[half, 8 + h // 2, qs], [(qk[half, 12 + g, 0:nk], 0)], causal[:, qt, 0:nk],
                        [v[:, t, 512 + g * HD:512 + (g + 1) * HD] for t in tiles])
            if kind == "win":
                return (qk[half, 8 + h // 2, qs], [(qk[half, 14 + g, 0:nk], 0)], causal[:, qt, 0:nk],
                        [v[:, t, 640 + g * HD:640 + (g + 1) * HD] for t in tiles])
            if kind == "cmp":
                return (qk[half, 8 + h // 2, qs], [(kcd[half, g * NCMP:(g + 1) * NCMP], 0)], cmpmask[:, qt, :],
                        [vcmp[0:NCMP, g, :]])
            if kind == "fox":
                return (foxq[:, h, qs], [(foxk[:, h, 0:nk], 0)], causal[:, qt, 0:nk],
                        [v[:, t, h * HD:(h + 1) * HD] for t in tiles])
            return (qk[half, h // 2, qs], [(qk[half, 5 + g, :], 0), (qk[half, 7 + g, :], T)], local[:, qt, :],
                    [v[:, t, g * HD:(g + 1) * HD] for t in range(2)]
                    + [v[:, t, 128 + g * HD:128 + (g + 1) * HD] for t in range(2)])

        block = ctx.enter_context(nc.Block())

        @block.sync
        def _(sp):
            for s in range(RING):
                sp.dma_start(ring[:, s, :], d_stream[s]).then_inc(s_full[s], 16)
                if s == 1:
                    sp.dma_start(par[:], d_params).then_inc(s_const, 16)
            with sp.Fori(1, RINGED // RING) as it:
                for s in range(RING):
                    sp.wait_ge(s_used, it * RING + (s - RING + 1))
                    sp.dma_start(ring[:, s, :], d_stream[bass.ds(it * RING + s, 1)].rearrange("o p c -> (o p) c")
                                 ).then_inc(s_full[s], 16)
            for n in range(RINGED // RING * RING, RINGED):
                sp.wait_ge(s_used, n - RING + 1)
                sp.dma_start(ring[:, n % RING, :], d_stream[n]).then_inc(s_full[n % RING], 16)

            def load(slot, index):
                sp.dma_start(moe_slot(slot), d_stream[bass.ds(index, 1)].rearrange("o p c -> (o p) c")
                             ).then_inc(m_full[slot], 16)

            def pair_chunks(j):
                return [(6 * j + 2 * c + a, 2 * j + a, c) for c in range(3) for a in range(2)]

            for j in range(2):
                for slot, e, c in pair_chunks(j):
                    if slot < RING:
                        sp.wait_ge(s_used, RINGED - RING + (slot - RINGED) % RING + 1)
                    elif slot == RING:
                        sp.wait_ge(s_odone, UNITS[-1][6] + 1)
                    sp.dma_start(moe_slot(slot), d_stream[RINGED + 3 * e + c]).then_inc(m_full[slot], 16)
            with sp.Fori(1, STEPS) as it:
                for j in range(2):
                    for slot, e, c in pair_chunks(j):
                        sp.wait_ge(s_used, it * 12 + (RINGED - 12 + slot + 1))
                        load(slot, it * 12 + (RINGED + 3 * e + c))
            sp.wait_ge(s_schedm, 32)
            more = sp.value_load(sched[P:P + 1, :], min_val=1, max_val=MAX_MORE)
            with sp.Fori(0, more) as it:
                for j in range(2):
                    ids = [sp.value_load(sched[bass.ds(it * 4 + (2 * j + a), 1), :], min_val=0, max_val=NEXP - 1)
                           for a in range(2)]
                    for slot, e, c in pair_chunks(j):
                        sp.wait_ge(s_used, it * 12 + (RINGED + 12 * (STEPS - 1) + slot + 1))
                        load(slot, ids[e % 2] * 3 + (RINGED + c))
            for t in range(TT):
                sp.wait_ge(s_normed, 5 + t)
                sp.dma_start(d_out[t * P:(t + 1) * P, :], x[:, t, :]).then_inc(s_out, 16)
            sp.wait_ge(s_out, 16 * TT)

        @block.tensor
        def _(pe):
            def chunk(n, per=0, it=0):
                pe.wait_ge(s_full[n % RING], it * (16 * per) + 16 * (n // RING + 1) if per else 16 * (n // RING + 1))
                return ring[:, n % RING, :]

            def turn(src, name, tiles=KT):
                for t in range(TT):
                    pe.wait_ge(s_rows, TT * TURNS.index(name) + t + 1)
                    for half in range(tiles // 4):
                        for j in range(4):
                            f = (4 * half + j) * P
                            mm = pe.transpose(ps[:, 4 + 2 * t + half, j * P:(j + 1) * P], src[:, t, f:f + P], ident)
                        mm.then_inc(s_turn, 4 // (tiles // 4) // 2)

            def wait_xT(name):
                pe.wait_ge(s_xT, 2 * (TURNS.index(name) + 1))
                pe.wait_ge(s_xTv, 2 * (TURNS.index(name) + 1))

            def panel(n0, started, jobs, k_per=4):
                width = SLOT // k_per
                for c in range(KT // k_per):
                    w = chunk(n0 + c).rearrange("p (k n) -> p k n", k=k_per)
                    for kind, src, col, n, bank, off in jobs:
                        for kk in range(k_per):
                            k = c * k_per + kk
                            if kind == "ws":
                                mm = pe.matmul(ps[0:n, bank, off:off + T], w[:, kk, col:col + n], src[:, k, :],
                                               start=bank not in started, stop=k == KT - 1, skip_group_check=True)
                                started.add(bank)
                            else:
                                t = kind
                                mm = pe.matmul(ps[:, bank, off:off + n], src[:, k, t * P:(t + 1) * P],
                                               w[:, kk, col:col + n], start=bank not in started, stop=k == KT - 1,
                                               skip_group_check=True)
                                started.add(bank)
                    mm.then_inc(s_used, 1)
                return mm

            def rotate(rot, src, bank, n):
                return pe.matmul(ps[:, bank, 0:n], rot, src, start=True, stop=True)

            def attention(name):
                a, b = INSTANCES[name]
                for i in range(a, b + 3):
                    if i < b:
                        lhs, keys, _, _ = unit_operands(i)
                        if UNITS[i][0] == "cmp" and UNITS[i - 1][0] != "cmp":
                            pe.wait_ge(s_ckey, 2)
                        if i >= 2:
                            pe.wait_ge(s_mask, i - 1)
                        for key, col in keys:
                            mm = pe.matmul(ps[:, i % 2, col:col + key.shape[1]], lhs, key, start=True, stop=True)
                        mm.then_inc(s_sc, 1)
                    u = i - 2
                    if a <= u < b:
                        nk = UNITS[u][3]
                        pe.wait_ge(s_exp, u + 1)
                        if u >= 2:
                            pe.wait_ge(s_pTsb, u - 1)
                        for t in range((nk + P - 1) // P):
                            n = min(P, nk - t * P)
                            mm = pe.transpose(ps[0:n, 2 + u % 2, t * P:(t + 1) * P], prob[:, u % 3, t * P:t * P + n], ident)
                        mm.then_inc(s_pT, 1)
                    u = i - 3
                    if a <= u < b:
                        _, _, _, vals = unit_operands(u)
                        _, _, _, nk, col, w, g = UNITS[u]
                        pe.wait_ge(s_pTsb, u + 1)
                        if u == group_units(g)[0] and g >= 2:
                            pe.wait_ge(s_odone, g - 1)
                        for t, val in enumerate(vals):
                            n = min(P, nk - t * P)
                            mm = pe.matmul(ps[:, 4 + g % 2, col:col + w], probT[0:n, u % 2, t * P:(t + 1) * P], val,
                                           start=t == 0, stop=t == len(vals) - 1)
                        if u == group_units(g)[-1]:
                            mm.then_inc(s_o, 1)

            def out_projection(n0):
                for c in range(4):
                    w = chunk(n0 + c).rearrange("p (k n) -> p k n", k=2)
                    for kk in range(2):
                        k = 2 * c + kk
                        for t in range(TT):
                            for half in range(2):
                                mm = pe.matmul(ps[:, 2 * t + half, :], xT[:, k, t * P:(t + 1) * P],
                                               w[:, kk, half * 512:(half + 1) * 512], start=k == 0, stop=k == KT - 1)
                    mm.then_inc(s_used, 1)

            def mlp(layer):
                n0 = FIRST[f"mlp{layer}"]
                pe_done = layer * 2 * MLP_STEPS
                with pe.Fori(0, MLP_STEPS) as it:
                    for j in range(2):
                        pe.wait_ge(s_relu, it * 2 + (pe_done + EARLY))
                        started = set()
                        for c in range(2):
                            w = chunk(n0 + 2 * j + c, 1, it).rearrange("p (k n) -> p k n", k=4)
                            for m in range(4):
                                bank = 4 + 2 * j + m // 2
                                for kk in range(4):
                                    k = 4 * c + kk
                                    mm = pe.matmul(ps[:, bank, (m % 2) * T:(m % 2 + 1) * T], w[:, kk, m * P:(m + 1) * P],
                                                   xT[:, k, :], start=bank not in started, stop=k == KT - 1,
                                                   skip_group_check=True)
                                    started.add(bank)
                            mm.then_inc(s_used, 1)
                    for c in range(4):
                        w = chunk(n0 + 4 + c, 1, it).rearrange("p (k n) -> p k n", k=2)
                        if c % 2 == 0:
                            pe.wait_ge(s_hT, it * 2 + (pe_done + c // 2 + 1))
                        if c == 0:
                            pe.wait_ge(s_acc, it + (layer * MLP_STEPS + EARLY))
                        for kk in range(2):
                            k = 2 * c + kk
                            for t in range(TT):
                                for half in range(2):
                                    mm = pe.matmul(ps[:, 2 * t + half, :], hT[:, k, t * P:(t + 1) * P],
                                                   w[:, kk, half * 512:(half + 1) * 512], start=k == 0, stop=k == 7)
                        mm.then_inc(s_used, 1)

            pe.wait_ge(s_const, 32)
            pe.wait_ge(s_x, 16)
            turn(x, "x0")
            wait_xT("x0")
            n0 = FIRST["in_even"]

            def ws4(bank, src=xT):
                return [("ws", src, m * P, P, bank + m // 2, (m % 2) * T) for m in range(4)]

            panel(n0, set(), ws4(0))
            panel(n0 + 2, set(), ws4(2))
            for m in range(2):
                pe.wait_ge(s_projsb, 1)
                mm = rotate(C("rot1"), raw[:, 0, 2 * m:2 * m + 2, :], 6 + m, 512)
            mm.then_inc(s_rot, 1)
            panel(n0 + 4, set(), [(t, xT, 0, 512, 4 + t, 0) for t in range(TT)])
            pe.wait_ge(s_roped, 1)
            pe.wait_ge(s_projsb, 2)
            for m in range(2):
                mm = rotate(C("rot1"), raw[:, 1, 2 * m:2 * m + 2, :], 6 + m, 512)
            mm.then_inc(s_rot, 1)
            panel(n0 + 6, set(), ws4(0))
            started = set()
            panel(n0 + 8, started, [("ws", xT, 0, P, 2, 0), ("ws", xT, P, P, 2, T), ("ws", xT, 2 * P, P, 3, 0),
                                    (0, xT, 3 * P, P, 3, T), (1, xT, 3 * P, P, 3, T + P)])
            pe.wait_ge(s_roped, 2)
            pe.wait_ge(s_projsb, 4)
            for m in range(2):
                mm = rotate(C("rot1"), raw[:, 0, 2 * m:2 * m + 2, :], 6 + m, 512)
            mm.then_inc(s_rot, 1)
            pe.wait_ge(s_projsb, 3)
            started = set()
            mm = panel(n0 + 10, started, [("ws", xT, 0, P, 4, 0), (0, xT, P, P, 4, T), (1, xT, P, P, 4, T + P)], 8)
            for t in range(TT):
                for k in range(KT):
                    mm = pe.matmul(ps[:, 5, t * 24:(t + 1) * 24], xT[:, k, t * P:(t + 1) * P],
                                   R("wgate")[:, k * 24:(k + 1) * 24], start=k == 0, stop=k == KT - 1)
            mm.then_inc(s_gates, 1)
            pe.wait_ge(s_roped, 3)
            pe.wait_ge(s_projsb, 6)
            rotate(C("rot1"), raw[:, 1, 0:2, :], 6, 512).then_inc(s_rot, 1)
            n0 = FIRST["cmp"]
            pe.wait_ge(s_blk, 4)
            for j in range(2):
                for c in range(2):
                    w = chunk(n0 + 2 * j + c).rearrange("p (m n) -> p m n", m=8)
                    for nt in range(2):
                        for mi in range(8):
                            m = 8 * c + mi
                            mm = pe.matmul(ps[:, 7, (2 * j + nt) * 32:(2 * j + nt) * 32 + 2 * NCMP],
                                           w[:, mi, nt * P:(nt + 1) * P],
                                           cmpin[:, j, m, :, :].rearrange("p g n -> p (g n)"),
                                           start=j == 0 and m == 0 and nt == 0, stop=m == 15, skip_group_check=True)
                    mm.then_inc(s_used, 1)
            pe.wait_ge(s_hidsb, 1)
            pe.wait_ge(s_roped, 4)
            for nt in range(2):
                mm = pe.matmul(ps[:, 6, 0:2 * NCMP], R("w2k")[:, nt * P:(nt + 1) * P], hidT[:, 0, nt, :],
                               start=nt == 0, stop=nt == 1)
            for g in range(2):
                for nt in range(2):
                    mm = pe.matmul(ps[0:NCMP, 6, 64 + g * HD:64 + (g + 1) * HD], hidT[:, 1, nt, g * NCMP:(g + 1) * NCMP],
                                   R("w2v")[:, nt * HD:(nt + 1) * HD], start=nt == 0, stop=nt == 1)
            mm.then_inc(s_cmp, 1)
            pe.wait_ge(s_cmpsb, 1)
            rotate(C("rot1"), kcraw, 7, 2 * NCMP).then_inc(s_crot, 1)
            attention("a0")
            turn(mix, "mix0")
            wait_xT("mix0")
            out_projection(FIRST["out_even"])
            turn(x, "ln0")
            wait_xT("ln0")
            mlp(0)
            turn(x, "ln1")
            wait_xT("ln1")
            n0 = FIRST["in_odd"]
            for j in range(4):
                if j >= 3:
                    pe.wait_ge(s_projsb, 6 + j - 2)
                panel(n0 + 2 * j, set(), ws4(2 * (j % 3)))
                if j == 0:
                    for k in range(KT):
                        mm = pe.matmul(ps[0:16, 7, 0:T], R("wforget")[:, k * 16:(k + 1) * 16], xT[:, k, :],
                                       start=k == 0, stop=k == KT - 1)
                    mm.then_inc(s_f, 1)
            for j in range(4, 6):
                pe.wait_ge(s_projsb, 6 + j - 2)
                b = 2 * (j % 3)
                panel(n0 + 2 * j, set(), [(t, xT, 0, 512, b + t, 0) for t in range(TT)])
            pe.wait_ge(s_projsb, 12)
            pe.wait_ge(s_caug, 32)
            attention("a1")
            turn(mix, "mix1")
            wait_xT("mix1")
            out_projection(FIRST["out_odd"])
            turn(x, "ln2")
            wait_xT("ln2")
            mlp(1)
            pe.wait_ge(s_cb, 1)
            pe.wait_ge(s_relu, 4 * MLP_STEPS + EARLY)
            pe.wait_ge(s_acc, 2 * MLP_STEPS + EARLY)
            n0 = FIRST["ada"]
            started = set()
            for i, what in enumerate(("sh1", "sc1", "g1", "sh2", "sc2", "g2")):
                for half in range(2):
                    for c in range(2):
                        w = chunk(n0 + 4 * i + 2 * half + c).rearrange("p (k n) -> p k n", k=4)
                        if what in ("g1", "g2"):
                            bank = (0 if what == "g1" else 2) + half
                            for kk in range(4):
                                k = 4 * c + kk
                                mm = pe.matmul(ps[:, bank, :], cb[:, k, :], w[:, kk, :], start=k == 0, stop=k == KT - 1)
                        else:
                            col = {"sh1": 0, "sc1": 8, "sh2": 16, "sc2": 24}[what] + 4 * half
                            for m in range(4):
                                for kk in range(4):
                                    k = 4 * c + kk
                                    mm = pe.matmul(ps[:, 6, 2 * (col + m):2 * (col + m) + 2], w[:, kk, m * P:(m + 1) * P],
                                                   csil[:, k, :], start=6 not in started, stop=k == KT - 1,
                                                   skip_group_check=True)
                                    started.add(6)
                        mm.then_inc(s_used, 1)
            pe.wait_ge(s_mod, 1)
            turn(y, "rms1")
            wait_xT("rms1")
            turn(ctxr, "ctx")
            wait_xT("ctx")
            n0 = FIRST["in_2"]
            pe.wait_ge(s_mod, 3)
            panel(n0, set(), ws4(0))
            jobs = [("ws", xT, 0, P, 2, 0), ("ws", cT, 0, P, 2, T)]
            jobs += [(t, xT, P, P, 3, t * P) for t in range(TT)] + [(t, cT, P, P, 3, T + t * P) for t in range(TT)]
            panel(n0 + 2, set(), jobs, 8)
            pe.wait_ge(s_projsb, 13)
            for m in range(2):
                mm = rotate(C("rot2"), raw[:, 0, 2 * m:2 * m + 2, :], 6 + m, 512)
            mm.then_inc(s_rot, 1)
            panel(n0 + 3, set(), [(t, xT, 0, 512, 4 + t, 0) for t in range(TT)])
            pe.wait_ge(s_projsb, 14)
            rotate(C("rot2"), raw[:, 1, 0, :], 0, T).then_inc(s_rot, 1)
            pe.wait_ge(s_projsb, 15)
            pe.wait_ge(s_poolmat, 16)
            for g in range(4):
                for t in range(TT):
                    mm = pe.matmul(ps[:, 4 + g // 2, (g % 2) * T:(g % 2 + 1) * T],
                                   v[:, t, 512 + g * P:512 + (g + 1) * P], poolmat[:, g, t, :], start=t == 0, stop=t == 1)
            mm.then_inc(s_dps, 1)
            pe.wait_ge(s_dsb, 1)
            pe.wait_ge(s_roped, 5)
            for g in range(4):
                mm = pe.matmul(ps[:, 6 + g // 2, (g % 2) * T:(g % 2 + 1) * T], R("poolw")[:, g * P:(g + 1) * P],
                               dT[:, g, :], start=True, stop=True)
            mm.then_inc(s_dps, 1)
            pe.wait_ge(s_roped, 6)
            pe.wait_ge(s_dsb, 2)
            attention("a2")
            turn(mix, "mix2", 4)
            wait_xT("mix2")
            out_projection(FIRST["out_2"])
            turn(y, "rms2")
            wait_xT("rms2")
            for t in range(TT):
                for k in range(KT):
                    mm = pe.matmul(ps[:, 6, t * NEXP:(t + 1) * NEXP], xT[:, k, t * P:(t + 1) * P],
                                   R("router")[:, k * NEXP:(k + 1) * NEXP], start=k == 0, stop=k == KT - 1)
            mm.then_inc(s_rps, 1)
            for t in range(TT):
                for half in range(2):
                    for j in range(4):
                        mm = pe.transpose(ps[:, 2 * t + half, j * P:(j + 1) * P], xT[:, 4 * half + j, t * P:(t + 1) * P], ident)
                    mm.then_inc(s_h2, 1)
            n0 = FIRST["shared"]
            panel(n0, set(), ws4(4))
            pe.wait_ge(s_chosen, 1)
            before, ones = C("before"), C("ones")
            for t, parts in enumerate(([(before, 0)], [(ones, 0), (before, 1)], [(ones, 0), (ones, 1)])):
                for i, (lhs, c) in enumerate(parts):
                    mm = pe.matmul(ps[:, 6, P + t * NEXP:P + (t + 1) * NEXP], lhs, chosen[:, c, :], start=i == 0,
                                   stop=i == len(parts) - 1)
            mm.then_inc(s_rank, 1)
            w = chunk(n0 + 2).rearrange("p (k n) -> p k n", k=2)
            pe.wait_ge(s_shact, 1)
            pe.wait_ge(s_h2sb, 4)
            for k in range(2):
                for t in range(TT):
                    for half in range(2):
                        mm = pe.matmul(ps[:, 2 * t + half, :], shactT[:, k, t * P:(t + 1) * P],
                                       w[:, k, half * 512:(half + 1) * 512], start=k == 0, stop=False, skip_group_check=True)
            mm.then_inc(s_used, 1)

            def gather():
                return [(k, t) for k in range(KT) for t in range(TT)]

            def do_gather(buf):
                for k, t in gather():
                    mm = pe.matmul(ps[:, 5 + k // 4, (k % 4) * P:(k % 4 + 1) * P], h2[:, t, k * P:(k + 1) * P],
                                   select[:, buf, t, :], start=t == 0, stop=t == TT - 1)
                mm.then_inc(s_gather, 1)

            def scatter(buf):
                for t in range(TT):
                    for half in range(2):
                        mm = pe.matmul(ps[:, 2 * t + half, :], probT[:, buf, 256 + t * P:256 + (t + 1) * P],
                                       yslot[:, half * 512:(half + 1) * 512], start=False, stop=False, skip_group_check=True)
                return mm

            pe.wait_ge(s_sel, 1)
            do_gather(0)
            pe.wait_ge(s_schedm, 32)
            more = pe.value_load(sched[P:P + 1, :], min_val=1, max_val=MAX_MORE)
            with pe.Fori(0, more + STEPS) as it:
                for j in range(2):
                    pe.wait_ge(s_hga, it * 2 + (j + 1))
                    pe.wait_ge(s_hgv, it * 2 + (j + 1))
                    pe.wait_ge(s_hid2, it * 2 + (j + EARLY))
                    for c in range(2):
                        ws = []
                        for a in range(2):
                            slot = 6 * j + 2 * c + a
                            pe.wait_ge(m_full[slot], it * 16 + 16)
                            ws.append(moe_slot(slot).rearrange("p (k n) -> p k n", k=4))
                        for kk in range(4):
                            k = 4 * c + kk
                            for a in range(2):
                                mm = pe.matmul(ps[a * CAP:(a + 1) * CAP, 4, :], hg[:, k, a * CAP:(a + 1) * CAP],
                                               ws[a][:, kk, :], start=k == 0, stop=k == KT - 1, skip_group_check=True)
                                if kk == 3:
                                    mm.then_inc(s_used, 1)
                    pe.wait_ge(s_sel, it * 2 + (j + 2))
                    pe.wait_ge(s_ya, it * 2 + (j + EARLY))
                    pe.wait_ge(s_yv, it * 2 + (j + EARLY))
                    do_gather((j + 1) % 2)
                    pe.wait_ge(s_hid2, it * 2 + (j + 1 + EARLY))
                    pe.wait_ge(s_tsb, it * 2 + (j + EARLY))
                    for k in range(2):
                        pe.transpose(ps[:, 7, k * P:(k + 1) * P], act2[:, k * P:(k + 1) * P], ident)
                    for t in range(TT):
                        mm = pe.transpose(ps[:, 7, 256 + t * P:256 + (t + 1) * P], selectw[:, j, t, :], ident)
                    mm.then_inc(s_tps, 1)
                    scatter((j + 1) % 2)
                    pe.wait_ge(s_tsb, it * 2 + (j + 1 + EARLY))
                    pe.wait_ge(s_hga, it * 2 + (j + 2))
                    pe.wait_ge(s_hgv, it * 2 + (j + 2))
                    ws = []
                    for a in range(2):
                        slot = 6 * j + 4 + a
                        pe.wait_ge(m_full[slot], it * 16 + 16)
                        ws.append(moe_slot(slot).rearrange("p (k n) -> p k n", k=2))
                    for k in range(2):
                        for half in range(2):
                            for a in range(2):
                                mm = pe.matmul(ps[a * CAP:(a + 1) * CAP, 5 + half, :],
                                               probT[:, j, k * P + a * CAP:k * P + (a + 1) * CAP],
                                               ws[a][:, k, half * 512:(half + 1) * 512], start=k == 0, stop=k == 1,
                                               skip_group_check=True)
                                if k == 1 and half == 1:
                                    mm.then_inc(s_used, 1)
            pe.wait_ge(s_ya, more * 2 + (2 * STEPS + EARLY))
            pe.wait_ge(s_yv, more * 2 + (2 * STEPS + EARLY))
            scatter(1).then_inc(s_moe, 1)

        @block.scalar
        def _(act):
            chain = [0]

            def link(ins):
                chain[0] += 1
                ins.then_inc(s_act, 1)
                act.wait_ge(s_act, chain[0])

            def panel_done(section, n):
                act.wait_ge(s_used, FIRST[section] + n)

            def take_turn(name, dst, tiles=KT):
                for t in range(TT):
                    act.wait_ge(s_turn, TURN_AT[name] + 2 * t + (1 if tiles == KT else 2))
                    act.activation(dst[:, 0:4, t * P:(t + 1) * P], ps[:, 4 + 2 * t, :].rearrange("p (j c) -> p j c", j=4),
                                   ACT.Copy).then_inc(s_xT, 1)

            def take_turn_mod(name, dst, a, b):
                for t in range(TT):
                    act.wait_ge(s_turn, TURN_AT[name] + 2 * t + 1)
                    for j in range(4):
                        i = act.activation(dst[:, j, t * P:(t + 1) * P], ps[:, 4 + 2 * t, j * P:(j + 1) * P],
                                           ACT.Identity, scale=a[:, j:j + 1], bias=b[:, j:j + 1])
                    i.then_inc(s_xT, 1)

            def copy(dst, src, **kw):
                return act.activation(dst, src, ACT.Copy, **kw)

            def copy_panel(dst, bank):
                for m in range(2):
                    i = copy(dst[:, 2 * m:2 * m + 2, :], ps[:, bank + m, :].rearrange("p (a c) -> p a c", a=2))
                return i

            def exps(name):
                a, b = INSTANCES[name]
                for u in range(a, b + 5):
                    if u < b:
                        nk = UNITS[u][3]
                        act.wait_ge(s_mask, u + 1)
                        if u >= 3:
                            act.wait_ge(s_pT, u - 2)
                        act.activation(prob[:, u % 3, 0:nk], masked[:, u % 3, 0:nk], ACT.Exp, bias=negmax[:, u:u + 1],
                                       scale=-1.0, accum_out=esum[:, u:u + 1]).then_inc(s_exp, 1)
                    if a <= u - 4 < b and group_units(UNITS[u - 4][6])[-1] == u - 4:
                        kind, qt, _, _, _, _, g = UNITS[u - 4]
                        if kind == "loc":
                            act.wait_ge(s_sinkin, qt + 1)
                            act.activation(esink, sinksh, ACT.Exp).then_inc(s_esink, 1)
                        if kind == "diff":
                            act.wait_ge(s_var, g + 1)
                            act.activation(dstd, drms, ACT.Sqrt).then_inc(s_std, 1)


            def std(k):
                act.wait_ge(s_var, k)
                act.activation(std2, var2, ACT.Sqrt).then_inc(s_std, 1)

            act.dma_start(x[:], d_x.rearrange("(t p) f -> p t f", p=P)).then_inc(s_x, 16)
            act.dma_start(con[:], d_consts).then_inc(s_const, 16)
            take_turn("x0", xT)
            act.wait_ge(s_lam, 1)
            act.activation(lexp, lsum, ACT.Exp).then_inc(s_lexp, 1)
            panel_done("in_even", 2)
            copy_panel(raw[:, 0], 0).then_inc(s_projsb, 1)
            panel_done("in_even", 4)
            copy_panel(raw[:, 1], 2).then_inc(s_projsb, 1)
            panel_done("in_even", 6)
            for t in range(TT):
                i = copy(v[:, t, 0:512], ps[:, 4 + t, :])
            i.then_inc(s_projsb, 1)
            panel_done("in_even", 8)
            act.wait_ge(s_roped, 1)
            copy_panel(raw[:, 0], 0).then_inc(s_projsb, 1)
            panel_done("in_even", 10)
            act.wait_ge(s_roped, 2)
            for j in range(2):
                for g in range(2):
                    rows = slice(g * HD, (g + 1) * HD)
                    copy(XS(j)[0:HD, g, :], ps[rows, 2, j * T:(j + 1) * T])
                    i = copy(XS(j)[HD:P, g, 0:T - 1], ps[rows, 2, j * T + 1:(j + 1) * T])
            copy(raw[:, 1, 0, :], ps[:, 3, 0:T])
            for t in range(TT):
                i = copy(v[:, t, 512:640], ps[:, 3, T + t * P:T + (t + 1) * P])
            i.then_inc(s_projsb, 1)
            act.wait_ge(s_gates, 1)
            copy(raw[:, 1, 1, :], ps[:, 4, 0:T])
            for t in range(TT):
                copy(v[:, t, 640:768], ps[:, 4, T + t * P:T + (t + 1) * P])
            act.activation(gate3[:], ps[:, 5, 0:48].rearrange("p (t c) -> p t c", t=2), ACT.Sigmoid).then_inc(s_projsb, 1)
            panel_done("cmp", 4)
            for j in range(2):
                for nt in range(2):
                    i = act.activation(hidT[:, j, nt, :], ps[:, 7, (2 * j + nt) * 32:(2 * j + nt) * 32 + 2 * NCMP],
                                       ACT.Gelu_apprx_tanh, bias=R("b1")[:, 2 * j + nt:2 * j + nt + 1])
            i.then_inc(s_hidsb, 1)
            act.wait_ge(s_cmp, 1)
            copy(vcmp[0:NCMP, :, :], ps[0:NCMP, 6, 64:64 + 2 * HD].rearrange("p (g d) -> p g d", g=2)).then_inc(s_ckey, 1)
            copy(kcraw, ps[:, 6, 0:2 * NCMP]).then_inc(s_cmpsb, 1)
            exps("a0")
            take_turn("mix0", xT)
            std(5)
            take_turn("ln0", xT)

            def mlp(layer):
                with act.Fori(0, MLP_STEPS) as it:
                    for j in range(2):
                        base = layer * 2 * MLP_STEPS
                        act.wait_ge(s_used, it * 8 + (FIRST[f"mlp{layer}"] + 2 * j + 2))
                        for m in range(2):
                            i = act.activation(hT[:, 4 * j + 2 * m:4 * j + 2 * m + 2, :],
                                               ps[:, 4 + 2 * j + m, :].rearrange("p (a c) -> p a c", a=2), ACT.Relu)
                        i.then_inc(s_relu, 1)

            mlp(0)
            std(6)
            take_turn("ln1", xT)
            for j in range(6):
                panel_done("in_odd", 2 * j + 2)
                b = 2 * (j % 3)
                if j < 4:
                    dst = foxq if j < 2 else foxk
                    for m in range(4):
                        h = 8 * (j % 2) + 2 * m
                        for o in range(2):
                            i = copy(dst[0:HD, h + o, :], ps[o * HD:(o + 1) * HD, b + m // 2, (m % 2) * T:(m % 2 + 1) * T],
                                     scale=SCALE if j < 2 else 1.0)
                else:
                    for t in range(TT):
                        i = copy(v[:, t, 512 * (j - 4):512 * (j - 3)], ps[:, b + t, :])
                i.then_inc(s_projsb, 1)
                if j == 0:
                    act.wait_ge(s_fdve, 1)
                    link(act.activation(mix[0:16, 0, 256:512], mix[0:16, 0, 256:512], ACT.Exp, scale=-1.0))
                    act.activation(mix[0:16, 0, 256:512], mix[0:16, 0, 256:512], ACT.Ln, bias=1.0).then_inc(s_fact, 1)
            exps("a1")
            take_turn("mix1", xT)
            std(7)
            take_turn("ln2", xT)
            act.activation(csil[:].rearrange("p k c -> p (k c)"), R("cvec"), ACT.Silu).then_inc(s_csil, 1)
            mlp(1)
            std(8)
            act.wait_ge(s_ctx, 16)
            for t in range(TT):
                i = act.activation(mix[:, t, :], ctxr[:, t, :], ACT.Square, accum_out=var_c[:, t:t + 1])
            i.then_inc(s_ss, 1)
            act.wait_ge(s_ss, 1)
            act.wait_ge(s_normed, 4)
            for t in range(TT):
                i = act.activation(mix[:, t, :], x[:, t, :], ACT.Square, accum_out=ss[:, t:t + 1])
            i.then_inc(s_ss, 1)
            act.wait_ge(s_var, 9)
            act.activation(std2, var2, ACT.Sqrt).then_inc(s_std, 1)
            act.wait_ge(s_var, 10)
            act.activation(std2, var2, ACT.Sqrt).then_inc(s_std, 1)
            act.wait_ge(s_mod, 2)
            take_turn_mod("rms1", xT, amod[:, 0:8], modT[:, 0:8, 0])
            take_turn_mod("ctx", cT, amod[:, 8:16], modT[:, 0:8, 1])
            panel_done("in_2", 2)
            copy_panel(raw[:, 0], 0).then_inc(s_projsb, 1)
            panel_done("in_2", 3)
            copy(raw[:, 1, 0, :], ps[:, 2, 0:T])
            for g in range(2):
                for o in range(2):
                    copy(qk[o * HD:(o + 1) * HD, 7 + g, :], ps[g * HD:(g + 1) * HD, 2, T:2 * T])
            for t in range(TT):
                copy(v[:, t, 0:128], ps[:, 3, t * P:(t + 1) * P])
                i = copy(v[:, t, 128:256], ps[:, 3, T + t * P:T + (t + 1) * P])
            i.then_inc(s_projsb, 1)
            panel_done("in_2", 5)
            for t in range(TT):
                i = copy(v[:, t, 512:1024], ps[:, 4 + t, :])
            i.then_inc(s_projsb, 1)
            act.wait_ge(s_dps, 1)
            copy_panel(dT, 4).then_inc(s_dsb, 1)
            act.wait_ge(s_dps, 2)
            for g in range(4):
                i = act.activation(xT[:, 4 + g, :], ps[:, 6 + g // 2, (g % 2) * T:(g % 2 + 1) * T],
                                   ACT.Identity, scale=R("poolscale")[:, g:g + 1])
            i.then_inc(s_dsb, 1)
            exps("a2")
            take_turn("mix2", xT, 4)
            act.wait_ge(s_restaken, 3)
            for t in range(TT):
                i = act.activation(mix[:, t, :], x[:, t, :], ACT.Square, accum_out=ss[:, t:t + 1])
            i.then_inc(s_ss, 1)
            std(11)
            take_turn_mod("rms2", xT, amod[:, 16:24], modT[:, 16:24, 0])
            act.wait_ge(s_rps, 1)
            act.activation(score[:], ps[:, 6, 0:2 * NEXP].rearrange("p (t e) -> p t e", t=2), ACT.Sigmoid).then_inc(s_score, 1)
            act.wait_ge(s_ss, 3)
            for t in range(TT):
                for half in range(2):
                    act.wait_ge(s_h2, 2 * t + half + 1)
                    copy(h2[:, t, half * 512:(half + 1) * 512], ps[:, 2 * t + half, :]).then_inc(s_h2sb, 1)
            panel_done("shared", 2)
            act.activation(shsg, ps[:, 4, :], ACT.Silu).then_inc(s_shsilu, 1)

            def take_gathered(n):
                act.wait_ge(s_gather, n)
                copy(hg[:, 0:4, :].rearrange("p k c -> p (k c)"), ps[:, 5, :]).then_inc(s_hga, 1)

            take_gathered(1)
            act.wait_ge(s_schedm, 32)
            more = act.value_load(sched[P:P + 1, :], min_val=1, max_val=MAX_MORE)
            with act.Fori(0, more + STEPS) as it:
                for j in range(2):
                    act.wait_ge(s_used, it * 12 + (RINGED + 6 * j + 4))
                    act.wait_ge(s_hid2, it * 2 + (j + EARLY))
                    act.activation(sg2, ps[:, 4, 0:256], ACT.Silu).then_inc(s_silu, 1)
                    take_gathered(it * 2 + (j + 2))
                    act.wait_ge(s_used, it * 12 + (RINGED + 6 * j + 6))
                    copy(yslot[:, 0:512], ps[:, 5, :]).then_inc(s_ya, 1)
            act.wait_ge(s_xfin, 1)
            for t in range(TT):
                i = act.activation(mix[:, t, :], x[:, t, :], ACT.Square, accum_out=ss[:, t:t + 1])
            i.then_inc(s_ss, 1)
            std(12)

        @block.vector
        def _(dve):
            chain = [0]

            def link(ins):
                chain[0] += 1
                ins.then_inc(s_dve, 1)
                dve.wait_ge(s_dve, chain[0])

            def take_turn(name, dst, tiles=KT):
                for t in range(TT):
                    dve.wait_ge(s_turn, TURN_AT[name] + 2 * t + 2)
                    if tiles == KT:
                        dve.tensor_copy(dst[:, 4:8, t * P:(t + 1) * P],
                                        ps[:, 5 + 2 * t, :].rearrange("p (j c) -> p j c", j=4)).then_inc(s_xTv, 1)

            def take_turn_mod(name, dst, a, b):
                for t in range(TT):
                    dve.wait_ge(s_turn, TURN_AT[name] + 2 * t + 2)
                    for j in range(4):
                        i = dve.tensor_scalar(dst[:, 4 + j, t * P:(t + 1) * P], ps[:, 5 + 2 * t, j * P:(j + 1) * P],
                                              a[:, 4 + j:5 + j], b[:, 4 + j:5 + j], ALU.mult, ALU.add)
                    i.then_inc(s_xTv, 1)

            def rope(out, src, banks, cos, sin, tiles):
                for m in range((tiles + 1) // 2):
                    n = min(2, tiles - 2 * m)
                    s3 = [P, n, T]
                    o, i0 = out[:, 2 * m:2 * m + n, :], src[:, 2 * m:2 * m + n, :]
                    rot = ps[:, banks + m, 0:n * T].rearrange("p (a c) -> p a c", a=n)
                    part = probT[:, 0, 0:n * T].rearrange("p (a c) -> p a c", a=n)
                    dve.tensor_tensor(o, i0, cos.unsqueeze(1).to_broadcast(s3), ALU.mult)
                    link(dve.tensor_tensor(part, rot, sin.unsqueeze(1).to_broadcast(s3), ALU.mult))
                    i = dve.tensor_tensor(o, o, part, ALU.add)
                    if 2 * m + n < tiles:
                        link(i)
                return i

            def inv_sqrt(out, var, std, tmp):
                link(dve.reciprocal(out, std))
                link(dve.tensor_tensor(tmp, out, out, ALU.mult))
                link(dve.tensor_tensor(tmp, tmp, var, ALU.mult))
                link(dve.tensor_scalar(tmp, tmp, -0.5, 1.5, ALU.mult, ALU.add))
                link(dve.tensor_tensor(out, out, tmp, ALU.mult))

            def take_group(g):
                units = group_units(g)
                kind, qt, h0 = UNITS[units[0]][:3]
                a, n = units[0], len(units)
                bank = 4 + g % 2
                dve.wait_ge(s_o, g + 1)
                if kind == "loc":
                    dve.tensor_tensor(sinksh, R("sink"), negmax[:, a:a + n], ALU.add).then_inc(s_sinkin, 1)
                    dve.wait_ge(s_esink, qt + 1)
                    link(dve.tensor_tensor(esum[:, a:a + n], esum[:, a:a + n], esink, ALU.add))
                link(dve.reciprocal(coef[:, 0:n], esum[:, a:a + n]))
                if kind == "diff":
                    o4 = y[:, 0, 0:512].rearrange("p (c w) -> p c w", c=4)
                    link(dve.tensor_tensor(o4, ps[:, bank, :].rearrange("p (c w) -> p c w", c=4),
                                           coef[:, 0:4].unsqueeze(2).to_broadcast([P, 4, P]), ALU.mult))
                    o2 = y[:, 0, 0:512].rearrange("p (h c w) -> p h c w", h=2, c=2)
                    dif = y[:, 1, 0:256].rearrange("p (h w) -> p h w", h=2)
                    sq = y[:, 1, 256:512].rearrange("p (h w) -> p h w", h=2)
                    for h in range(2):
                        i = dve.scalar_tensor_tensor(out=dif[:, h, :], in0=o2[:, h, 1, :], scalar=lamc, in1=o2[:, h, 0, :],
                                                     op0=ALU.mult, op1=ALU.add)
                    link(i)
                    link(dve.tensor_tensor(sq, dif, dif, ALU.mult))
                    link(dve.tensor_reduce(dms, sq, AX, ALU.add))
                    dve.tensor_scalar(drms, dms, 1.0 / P, LN_EPS, ALU.mult, ALU.add).then_inc(s_var, 1)
                    dve.wait_ge(s_std, g + 1)
                    inv_sqrt(drs, drms, dstd, dnw)
                    link(dve.tensor_tensor(dif, dif, drs.unsqueeze(2).to_broadcast([P, 2, P]), ALU.mult))
                    out = mix[:, qt, (h0 // 2) * P:(h0 // 2 + 2) * P].rearrange("p (h w) -> p h w", h=2)
                    link(dve.tensor_tensor(out, dif, R("subln").unsqueeze(1).to_broadcast([P, 2, P]), ALU.mult))
                    dve.tensor_scalar(out, out, 1.0 - LAM_INIT, None, ALU.mult).then_inc(s_odone, 1)
                    dve.wait_ge(s_odone, g + 1)
                    return
                if kind in ("slc", "win", "cmp"):
                    b = {"cmp": 0, "slc": 1, "win": 2}[kind]
                    gates = gate3[:, qt, :].rearrange("p (h b) -> p h b", b=3)[:, :, b]
                    link(dve.tensor_tensor(coef, coef, gates, ALU.mult))
                    if kind == "cmp":
                        link(dve.tensor_scalar(coef, coef, C("rowvalid")[:, qt:qt + 1], None, ALU.mult))
                    out = mix[:, qt, 512:1024]
                else:
                    out = mix[:, qt, h0 * HD:(h0 + 8) * HD]
                out3 = out.rearrange("p (h w) -> p h w", h=8)
                o3 = ps[:, bank, :].rearrange("p (h w) -> p h w", h=8)
                c3 = coef.unsqueeze(2).to_broadcast([P, 8, HD])
                if kind in ("win", "cmp"):
                    tmp = y[:, 0, 0:512].rearrange("p (h w) -> p h w", h=8)
                    link(dve.tensor_tensor(tmp, o3, c3, ALU.mult))
                    i = dve.tensor_tensor(out3, out3, tmp, ALU.add)
                else:
                    i = dve.tensor_tensor(out3, o3, c3, ALU.mult)
                i.then_inc(s_odone, 1)
                dve.wait_ge(s_odone, g + 1)

            def attention(name):
                a, b = INSTANCES[name]
                taken = 0
                for i in range(a, b + 5):
                    if i < b:
                        kind, qt, h, nk, _, _, _ = UNITS[i]
                        _, _, mask, _ = unit_operands(i)
                        dve.wait_ge(s_sc, i + 1)
                        if i >= 3:
                            dve.wait_ge(s_exp, i - 2)
                        first = negsink[:, h:h + 1] if kind == "loc" else 1e38
                        dve.tensor_tensor_reduce(out=masked[:, i % 3, 0:nk], in0=ps[:, i % 2, 0:nk], in1=mask,
                                                 scale=-1.0 if kind == "fox" else -SCALE, scalar=first,
                                                 op0=ALU.add, op1=ALU.min, accum_out=negmax[:, i:i + 1]).then_inc(s_mask, 1)
                    u = i - 2
                    if a <= u < b:
                        nk = UNITS[u][3]
                        n = P if nk >= P else nk
                        w = P * ((nk + P - 1) // P)
                        dve.wait_ge(s_pT, u + 1)
                        dve.tensor_copy(probT[0:n, u % 2, 0:w], ps[0:n, 2 + u % 2, 0:w]).then_inc(s_pTsb, 1)
                    u = i - 4
                    if a <= u < b and u == group_units(UNITS[u][6])[-1]:
                        take_group(UNITS[u][6])

            def stats(k, g_row, b_row, s_vec, v_vec, turned=True):
                for t in range(TT):
                    for half in range(2):
                        i = dve.bn_stats(bn[:, 2 * t + half, :], y[:, t, half * 512:(half + 1) * 512])
                link(i)
                for t in range(TT):
                    i = dve.bn_aggr(mv[:, t, :], bn[:, 2 * t:2 * t + 2, :])
                link(i)
                dve.tensor_scalar(var2, mv[:, :, 1], LN_EPS, None, ALU.add).then_inc(s_var, 1)
                dve.wait_ge(s_std, k)
                inv_sqrt(rstd, var2, std2, nwt)
                dve.wait_ge(s_vec, v_vec)
                for t in range(TT):
                    link(dve.scalar_tensor_tensor(out=y[:, t, :], in0=y[:, t, :], scalar=mv[:, t, 0:1], in1=g_row,
                                                  op0=ALU.subtract, op1=ALU.mult))
                    i = dve.scalar_tensor_tensor(out=x[:, t, :], in0=y[:, t, :], scalar=rstd[:, t:t + 1], in1=b_row,
                                                 op0=ALU.mult, op1=ALU.add)
                    if turned:
                        i.then_inc(s_rows, 1)
                if turned:
                    rows[0] += TT
                    dve.wait_ge(s_rows, rows[0])
                else:
                    link(i)

            rows = [0]

            def rows_ready(n=1):
                rows[0] += n
                dve.engine_nop().then_inc(s_rows, n)

            def normed():
                dve.engine_nop().then_inc(s_normed, 1)

            def residual(k):
                dve.wait_ge(s_used, FIRST[k] + 4)
                for t in range(TT):
                    for half in range(2):
                        cols = slice(half * 512, (half + 1) * 512)
                        i = dve.scalar_tensor_tensor(out=y[:, t, cols], in0=x[:, t, cols], scalar=ALPHA,
                                                     in1=ps[:, 2 * t + half, :], op0=ALU.mult, op1=ALU.add)
                link(i)
                dve.engine_nop().then_inc(s_restaken, 1)

            def mlp(layer):
                link(dve.tensor_scalar(y[:].rearrange("p t f -> p (t f)"), x[:].rearrange("p t f -> p (t f)"), ALPHA, None,
                                       ALU.mult))
                base = layer * 2 * MLP_STEPS
                with dve.Fori(0, MLP_STEPS) as it:
                    for j in range(2):
                        dve.wait_ge(s_relu, it * 2 + (base + j + 1 + EARLY))
                        h2 = hT[:, 4 * j:4 * j + 4, :].rearrange("p a c -> p (a c)")
                        dve.tensor_tensor(h2, h2, h2, ALU.mult).then_inc(s_hT, 1)
                    dve.wait_ge(s_used, it * 8 + (FIRST[f"mlp{layer}"] + 8))
                    dve.wait_ge(s_acc, it + (layer * MLP_STEPS + EARLY))
                    for t in range(TT):
                        for half in range(2):
                            cols = slice(half * 512, (half + 1) * 512)
                            i = dve.tensor_tensor(y[:, t, cols], ps[:, 2 * t + half, :], y[:, t, cols], ALU.add)
                    i.then_inc(s_acc, 1)
                dve.wait_ge(s_acc, (layer + 1) * MLP_STEPS + EARLY)

            for s in (s_relu, s_acc, s_hid2, s_tsb, s_tps, s_ya, s_yv):
                dve.engine_nop().then_inc(s, EARLY)
            rows[0] = 2
            dve.wait_ge(s_x, 16)
            dve.engine_nop().then_inc(s_rows, 2)
            dve.wait_ge(s_const, 32)
            lam4 = R("lam").rearrange("p (a d) -> p a d", a=4)
            lp = y[:, 0, 0:2 * HD].rearrange("p (a d) -> p a d", a=2)
            link(dve.tensor_tensor(lp, lam4[:, 0:4:2, :], lam4[:, 1:4:2, :], ALU.mult))
            dve.tensor_reduce(lsum, lp, AX, ALU.add).then_inc(s_lam, 1)
            dve.wait_ge(s_lexp, 1)
            link(dve.tensor_tensor(lamc, lexp[:, 1:2], lexp[:, 0:1], ALU.subtract))
            link(dve.tensor_scalar(lamc, lamc, -LAM_INIT, None, ALU.add))
            take_turn("x0", xT)
            link(dve.tensor_scalar(negsink[:], R("sink"), -1.0, None, ALU.mult))
            dve.wait_ge(s_rot, 1)
            rope(qk[:, 0:4, :], raw[:, 0], 6, C("cos1"), C("sin1"), 4).then_inc(s_roped, 1)
            dve.wait_ge(s_rot, 2)
            dve.wait_ge(s_roped, 1)
            rope(qk[:, 4:8, :], raw[:, 1], 6, C("cos1"), C("sin1"), 4).then_inc(s_roped, 1)
            dve.wait_ge(s_rot, 3)
            dve.wait_ge(s_roped, 2)
            rope(qk[:, 8:12, :], raw[:, 0], 6, C("cos1"), C("sin1"), 4).then_inc(s_roped, 1)
            dve.wait_ge(s_rot, 4)
            dve.wait_ge(s_roped, 3)
            link(rope(qk[:, 16:18, :], raw[:, 1], 6, C("cos1"), C("sin1"), 2))
            for j in range(2):
                for g in range(2):
                    for o in range(2):
                        i = dve.tensor_copy(qk[o * HD:(o + 1) * HD, 12 + 2 * j + g, :], qk[g * HD:(g + 1) * HD, 16 + j, :])
            i.then_inc(s_roped, 1)
            dve.wait_ge(s_crot, 1)
            dve.tensor_tensor(kcd, kcraw, C("cosc"), ALU.mult)
            link(dve.tensor_tensor(kctmp, ps[:, 7, 0:2 * NCMP], C("sinc"), ALU.mult))
            dve.tensor_tensor(kcd, kcd, kctmp, ALU.add).then_inc(s_ckey, 1)
            attention("a0")
            rows_ready(2)
            take_turn("mix0", xT)
            residual("out_even")
            stats(5, vec[:, 0, :], vec[:, 1, :], s_vecA, 32)
            normed()
            take_turn("ln0", xT)
            mlp(0)
            stats(6, vec[:, 2, :], vec[:, 3, :], s_vecB, 32)
            normed()
            take_turn("ln1", xT)
            zmin, zabs, logf, csum, ones = (mix[0:16, i // 4, (i % 4) * 256:(i % 4 + 1) * 256] for i in range(5))
            dve.wait_ge(s_f, 1)
            fb = R("fbias", 16)
            link(dve.tensor_scalar(logf, ps[0:16, 7, 0:T], fb, None, ALU.add))
            dve.tensor_scalar(zmin, logf, 0.0, None, ALU.min)
            link(dve.tensor_scalar(ones, logf, 0.0, None, ALU.max))
            link(dve.tensor_tensor(zabs, ones, zmin, ALU.subtract))
            link(dve.memset(ones, 1.0))
            dve.engine_nop().then_inc(s_fdve, 1)
            dve.wait_ge(s_fact, 1)
            link(dve.tensor_tensor(logf, zmin, zabs, ALU.subtract))
            link(dve.tensor_tensor_scan(csum, ones, logf, 0.0, ALU.mult, ALU.add))
            link(dve.tensor_scalar(zmin, csum, -1.0, None, ALU.mult))
            link(dve.memset(foxq[64:66, :, :], 1.0))
            link(dve.memset(foxk[64:66, :, :], 1.0))
            dve.engine_nop().then_inc(s_fdve, 1)
            attention("a1")
            rows_ready(2)
            take_turn("mix1", xT)
            residual("out_odd")
            stats(7, vec[:, 0, :], vec[:, 1, :], s_vecA, 64)
            normed()
            take_turn("ln2", xT)
            dve.wait_ge(s_csil, 1)
            dve.tensor_copy(cb, csil[:, :, 0:1].to_broadcast([P, KT, P])).then_inc(s_cb, 1)
            mlp(1)
            stats(8, vec[:, 2, :], vec[:, 3, :], s_vecB, 64, turned=False)
            normed()
            dve.wait_ge(s_ss, 1)
            dve.tensor_scalar(var2, var_c, 1.0 / D, RMS_EPS, ALU.mult, ALU.add).then_inc(s_var, 1)
            dve.wait_ge(s_std, 9)
            inv_sqrt(rstd, var2, std2, nwt)
            for t in range(TT):
                link(dve.tensor_scalar(ctxr[:, t, :], ctxr[:, t, :], rstd[:, t:t + 1], None, ALU.mult))
            dve.wait_ge(s_ss, 2)
            dve.tensor_scalar(var2, ss, 1.0 / D, RMS_EPS, ALU.mult, ALU.add).then_inc(s_var, 1)
            dve.wait_ge(s_std, 10)
            inv_sqrt(rstd, var2, std2, nwt)
            for t in range(TT):
                link(dve.tensor_scalar(y[:, t, :], x[:, t, :], rstd[:, t:t + 1], None, ALU.mult))
            rows_ready(4)
            dve.wait_ge(s_used, FIRST["ada"] + 24)
            bada = R("bada").rearrange("p (i m) -> p i m", i=6)
            for i, s in enumerate((0, 1, 3, 4)):
                ins = dve.tensor_tensor(modT[:, 8 * i:8 * i + 8, :], ps[:, 6, 16 * i:16 * i + 16].rearrange("p (m c) -> p m c", c=2),
                                        bada[:, s, :].unsqueeze(2).to_broadcast([P, 8, 2]), ALU.add)
            link(ins)
            dve.engine_nop().then_inc(s_mod, 1)
            n1, n2 = R("norm1"), R("norm2")
            for c in range(2):
                dve.scalar_tensor_tensor(out=amod[:, 8 * c:8 * c + 8], in0=modT[:, 8:16, c], scalar=1.0, in1=n1,
                                         op0=ALU.add, op1=ALU.mult)
            link(dve.scalar_tensor_tensor(out=amod[:, 16:24], in0=modT[:, 24:32, 0], scalar=1.0, in1=n2, op0=ALU.add,
                                          op1=ALU.mult))
            dve.engine_nop().then_inc(s_mod, 1)
            dve.wait_ge(s_vecA, 96)
            for i in range(2):
                for half in range(2):
                    cols = slice(half * 512, (half + 1) * 512)
                    ins = dve.tensor_tensor(vec[:, i, cols], ps[:, 2 * i + half, :], vec[:, i, cols], ALU.add)
            link(ins)
            dve.engine_nop().then_inc(s_mod, 1)
            take_turn_mod("rms1", xT, amod[:, 0:8], modT[:, 0:8, 0])
            take_turn_mod("ctx", cT, amod[:, 8:16], modT[:, 0:8, 1])
            dve.wait_ge(s_rot, 5)
            rope(qk[:, 0:4, :], raw[:, 0], 6, C("cos2"), C("sin2"), 4).then_inc(s_roped, 1)
            dve.wait_ge(s_rot, 6)
            dve.wait_ge(s_roped, 5)
            link(rope(qk[:, 4:5, :], raw[:, 1], 0, C("cos2"), C("sin2"), 1))
            for g in range(2):
                for o in range(2):
                    i = dve.tensor_copy(qk[o * HD:(o + 1) * HD, 5 + g, :], qk[g * HD:(g + 1) * HD, 4, :])
            i.then_inc(s_roped, 1)
            attention("a2")
            rows_ready(2)
            take_turn("mix2", xT, 4)
            dve.engine_nop().then_inc(s_xTv, 2)
            dve.wait_ge(s_used, FIRST["out_2"] + 4)
            for t in range(TT):
                for half in range(2):
                    cols = slice(half * 512, (half + 1) * 512)
                    i = dve.tensor_tensor(y[:, t, cols], ps[:, 2 * t + half, :], vec[:, 0, cols], ALU.mult)
            link(i)
            for t in range(TT):
                i = dve.tensor_tensor(x[:, t, :], x[:, t, :], y[:, t, :], ALU.add)
            link(i)
            dve.engine_nop().then_inc(s_restaken, 1)
            dve.wait_ge(s_ss, 3)
            dve.tensor_scalar(var2, ss, 1.0 / D, RMS_EPS, ALU.mult, ALU.add).then_inc(s_var, 1)
            dve.wait_ge(s_std, 11)
            inv_sqrt(rstd, var2, std2, nwt)
            for t in range(TT):
                link(dve.tensor_scalar(y[:, t, :], x[:, t, :], rstd[:, t:t + 1], None, ALU.mult))
            rows_ready(2)
            take_turn_mod("rms2", xT, amod[:, 16:24], modT[:, 16:24, 0])
            link(dve.memset(weight[:].rearrange("p t e -> p (t e)"), 1.0))
            dve.wait_ge(s_score, 1)
            e3 = [P, TT, NEXP]
            link(dve.tensor_tensor(biased[:], score[:], R("rbias").unsqueeze(1).to_broadcast(e3), ALU.add))
            for t in range(TT):
                for g in range(8):
                    link(dve.max(top8[:, t, :], biased[:, t, 8 * g:8 * g + 8]))
                    link(dve.tensor_tensor(gsc[:, t, g:g + 1], top8[:, t, 0:1], top8[:, t, 1:2], ALU.add))
                link(dve.max(top8[:, t, :], gsc[:, t, :]))
                link(dve.max_index(gidx[:, t, :], top8[:, t, :], gsc[:, t, :]))
            link(dve.tensor_copy(gidxf[:], gidx[:]))
            for t in range(TT):
                link(dve.tensor_scalar(gmask[:, t, :], C("iota8"), gidxf[:, t, 0:1], None, ALU.is_equal))
                for r in range(1, 4):
                    link(dve.scalar_tensor_tensor(out=gmask[:, t, :], in0=C("iota8"), scalar=gidxf[:, t, r:r + 1],
                                                  in1=gmask[:, t, :], op0=ALU.is_equal, op1=ALU.add))
                b8 = biased[:, t, :].rearrange("p (g e) -> p g e", g=8)
                m8 = gmask[:, t, :].unsqueeze(2).to_broadcast([P, 8, 8])
                c8 = chosen[:, t, :].rearrange("p (g e) -> p g e", g=8)
                link(dve.tensor_tensor(b8, b8, m8, ALU.mult))
                link(dve.tensor_scalar(c8, m8, -1.0, 1e30, ALU.add, ALU.mult))
                link(dve.tensor_tensor(b8, b8, c8, ALU.add))
                link(dve.max(top8b[:, t, :], biased[:, t, :]))
                link(dve.match_replace(chosen[:, t, :], top8b[:, t, :], biased[:, t, :], 3e30))
            dve.tensor_scalar(chosen[:], chosen[:], 2e30, None, ALU.is_ge).then_inc(s_chosen, 1)
            dve.wait_ge(s_chosen, 1)
            link(dve.tensor_tensor(score[:], score[:], chosen[:], ALU.mult))
            link(dve.tensor_reduce(wsum, score[:], AX, ALU.add))
            link(dve.reciprocal(wsum, wsum))
            for t in range(TT):
                i = dve.tensor_scalar(weight[:, t, 0:NEXP], score[:, t, :], wsum[:, t:t + 1], ROUTED_SCALE, ALU.mult,
                                      ALU.mult)
            link(i)
            dve.wait_ge(s_shsilu, 1)
            dve.tensor_tensor(shactT[:].rearrange("p k c -> p (k c)"), shsg, ps[:, 5, :], ALU.mult).then_inc(s_shact, 1)
            dve.wait_ge(s_rank, 1)
            link(dve.scalar_tensor_tensor(out=rank1, in0=ps[:, 6, P:P + 2 * NEXP].rearrange("p (t e) -> p t e", t=2),
                                          scalar=1.0, in1=chosen[:], op0=ALU.add, op1=ALU.mult))
            for r in range(ROUNDS):
                cols = slice(r * NEXP, (r + 1) * NEXP)
                dve.tensor_scalar(over[:, cols], ps[:, 6, P + 2 * NEXP:P + 3 * NEXP], float(CAP * (r + 1)), None, ALU.is_gt)
                dve.tensor_scalar(rankr[:, :, cols], rank1, -float(CAP * (r + 1)), None, ALU.add)
                i = dve.tensor_copy(weightr[:, :, cols], weight[:, :, 0:NEXP])
            link(i)
            link(dve.memset(onehot, 1.0))
            link(dve.tensor_tensor_scan(scratch, onehot, over, 0.0, ALU.mult, ALU.add))
            dve.tensor_copy(tot, scratch[:, NOV - 1:NOV])
            link(dve.tensor_tensor(overpos, scratch, over, ALU.mult))
            link(dve.tensor_scalar(onehot, overpos, C("place1"), None, ALU.is_equal))
            link(dve.tensor_tensor(scratch, onehot, C("expert"), ALU.mult))
            link(dve.tensor_reduce(schedf[:, 0:1], scratch, AX, ALU.add))
            link(dve.tensor_scalar(scratch[:, 0:MAX_MORE], C("evens4"), tot, None, ALU.is_lt))
            link(dve.tensor_reduce(schedf[:, 1:2], scratch[:, 0:MAX_MORE], AX, ALU.add))
            link(dve.tensor_scalar(schedf[:, 1:2], schedf[:, 1:2], 1.0, None, ALU.max))
            dve.tensor_copy(schedi[:], schedf).then_inc(s_sched, 1)
            link(dve.memset(kcount, 0.0))
            link(dve.memset(yslot, 0.0))
            link(dve.memset(probT[:, 1, :], 0.0))

            def select_experts(buf, cols):
                for t in range(TT):
                    for a in range(2):
                        r, w = cols(t, a)
                        sl = slice(a * CAP, (a + 1) * CAP)
                        dve.tensor_scalar(select[:, buf, t, sl], C("iota1"), r, None, ALU.is_equal)
                        i = dve.tensor_scalar(selectw[:, buf, t, sl], C("iota1"), r, w, ALU.is_equal, ALU.mult)
                i.then_inc(s_sel, 1)

            def first_round(e):
                return lambda t, a: (rank1[:, t, bass.ds(e + a, 1)], weight[:, t, bass.ds(e + a, 1)])

            def fixed_round(e):
                return lambda t, a: (rank1[:, t, e + a:e + a + 1], weight[:, t, e + a:e + a + 1])

            def pick_again(wait_base, it, per):
                n = [0]

                def step(ins):
                    n[0] += 1
                    ins.then_inc(s_pick, 1)
                    if per:
                        dve.wait_ge(s_pick, it * per + (wait_base + n[0]))
                    else:
                        dve.wait_ge(s_pick, wait_base + n[0])

                for a in range(2):
                    step(dve.tensor_scalar(kcount, kcount, 1.0, None, ALU.add))
                    step(dve.tensor_scalar(onehot, overpos, kcount, None, ALU.is_equal))
                    for t in range(TT):
                        for src, col in ((rankr, colr), (weightr, colw)):
                            step(dve.tensor_tensor(scratch, onehot, src[:, t, :], ALU.mult))
                            step(dve.tensor_reduce(col[:, t, a:a + 1], scratch, AX, ALU.add))
                return n[0]

            def again(t, a):
                return colr[:, t, a:a + 1], colw[:, t, a:a + 1]

            def take_gathered(n):
                dve.wait_ge(s_gather, n)
                dve.tensor_copy(hg[:, 4:8, :].rearrange("p k c -> p (k c)"), ps[:, 6, :]).then_inc(s_hgv, 1)

            def pair(j, p, used):
                dve.wait_ge(s_silu, p + (j + 1))
                dve.tensor_tensor(act2, sg2, ps[:, 4, 256:512], ALU.mult).then_inc(s_hid2, 1)
                take_gathered(p + (j + 2))
                dve.wait_ge(s_tps, p + (j + 1 + EARLY))
                dve.tensor_copy(probT[:, j, :], ps[:, 7, :]).then_inc(s_tsb, 1)
                dve.wait_ge(s_used, used + (RINGED + 6 * j + 6))
                dve.tensor_copy(yslot[:, 512:1024], ps[:, 6, :]).then_inc(s_yv, 1)

            select_experts(0, fixed_round(0))
            take_gathered(1)
            with dve.Fori(0, STEPS - 1) as it:
                for j in range(2):
                    dve.wait_ge(s_tps, it * 2 + (j + EARLY))
                    select_experts((j + 1) % 2, first_round(it * 4 + (2 * j + 2)))
                    pair(j, it * 2, it * 12)
            last = STEPS - 1
            dve.wait_ge(s_tps, 2 * last + EARLY)
            select_experts(1, fixed_round(NEXP - 2))
            pair(0, 2 * last, 12 * last)
            dve.wait_ge(s_tps, 2 * last + 1 + EARLY)
            picks = pick_again(0, 0, 0)
            select_experts(0, again)
            pair(1, 2 * last, 12 * last)
            dve.wait_ge(s_schedm, 32)
            more = dve.value_load(sched[P:P + 1, :], min_val=1, max_val=MAX_MORE)
            with dve.Fori(0, more) as it:
                for j in range(2):
                    dve.wait_ge(s_tps, it * 2 + (2 * STEPS + j + EARLY))
                    pick_again(picks * (j + 1), it, 2 * picks)
                    select_experts((j + 1) % 2, again)
                    pair(j, it * 2 + 2 * STEPS, it * 12 + 12 * STEPS)
            dve.wait_ge(s_moe, 1)
            for t in range(TT):
                for half in range(2):
                    cols = slice(half * 512, (half + 1) * 512)
                    i = dve.tensor_tensor(y[:, t, cols], ps[:, 2 * t + half, :], vec[:, 1, cols], ALU.mult)
            link(i)
            dve.tensor_tensor(x[:], x[:], y[:], ALU.add).then_inc(s_xfin, 1)
            dve.wait_ge(s_xfin, 1)
            dve.wait_ge(s_ss, 4)
            dve.tensor_scalar(var2, ss, 1.0 / D, RMS_EPS, ALU.mult, ALU.add).then_inc(s_var, 1)
            dve.wait_ge(s_std, 12)
            inv_sqrt(rstd, var2, std2, nwt)
            dve.wait_ge(s_vecB, 80)
            for t in range(TT):
                i = dve.scalar_tensor_tensor(out=x[:, t, :], in0=x[:, t, :], scalar=rstd[:, t:t + 1], in1=vec[:, 2, :],
                                             op0=ALU.mult, op1=ALU.mult)
                i.then_inc(s_normed, 1)

        @block.gpsimd
        def _(pool):
            def row(dst, src, s):
                pool.dma_start(dst, src.to_broadcast([P, D])).then_inc(s, 16)

            for i in range(2):
                row(vec[:, 2 * i, :], d_gain[0, i:i + 1, :], s_vecB if i else s_vecA)
                row(vec[:, 2 * i + 1, :], d_bias[0, i:i + 1, :], s_vecB if i else s_vecA)
            pool.wait_ge(s_const, 32)
            pool.wait_ge(s_projsb, 5)
            pe3 = R("pe").rearrange("p (j m) -> p j m", j=2)
            for j in range(2):
                for g in range(2):
                    pool.tensor_copy(cmpin[:, j, :, g, :], windows(XS(j), g)).then_inc(s_pool, 1)
                    pool.wait_ge(s_pool, 2 * j + g + 1)
                    pool.tensor_tensor(cmpin[:, j, :, g, :], cmpin[:, j, :, g, :],
                                       pe3[:, j, :].unsqueeze(2).to_broadcast([P, 16, NCMP]), ALU.add).then_inc(s_blk, 1)
            pool.wait_ge(s_normed, 1)
            row(vec[:, 0, :], d_gain[1, 0:1, :], s_vecA)
            row(vec[:, 1, :], d_bias[1, 0:1, :], s_vecA)
            pool.wait_ge(s_normed, 2)
            row(vec[:, 2, :], d_gain[1, 1:2, :], s_vecB)
            row(vec[:, 3, :], d_bias[1, 1:2, :], s_vecB)
            pool.wait_ge(s_fdve, 2)
            pool.dma_start(foxq[65:66, :, :], mix[0:16, 0, 768:1024]).then_inc(s_caug, 16)
            pool.dma_start(foxk[64:65, :, :], mix[0:16, 0, 0:256]).then_inc(s_caug, 16)
            pool.wait_ge(s_normed, 3)
            pool.dma_start(ctxr, d_ctx.rearrange("(t p) f -> p t f", p=P)).then_inc(s_ctx, 16)
            row(vec[:, 0, :], d_badarow[0:1, 0:D], s_vecA)
            row(vec[:, 1, :], d_badarow[0:1, D:2 * D], s_vecA)
            pool.wait_ge(s_normed, 4)
            row(vec[:, 2, :], d_final[0:1, :], s_vecB)
            pool.wait_ge(s_turn, TURN_AT["rms1"] + 4)
            pool.dma_start(poolmat, d_pool).then_inc(s_poolmat, 16)
            pool.wait_ge(s_vecA, 96)
            pool.wait_ge(s_vecB, 80)
            pool.wait_ge(s_sched, 1)
            pool.dma_start(sched[0:P, :], schedi[:, 0:1]).then_inc(s_schedm, 16)
            pool.dma_start(sched[P:P + 1, :], schedi[0:1, 1:2]).then_inc(s_schedm, 16)
            pool.wait_ge(s_schedm, 32)


def rope_tables(positions_and_freqs, rows):
    n = len(positions_and_freqs[0][0])
    cos, sin = np.ones((rows, n)), np.zeros((rows, n))
    for pos, inv, at in positions_and_freqs:
        ang = inv[:, None] * pos[None, :]
        for half in range(2):
            a = at + half * len(inv)
            cos[a:a + len(inv)], sin[a:a + len(inv)] = np.cos(ang), np.sin(ang)
    return cos, sin


def rotation(pairs):
    rot = np.zeros((P, P))
    for at, half in pairs:
        for i in range(half):
            rot[at + i, at + half + i] = -1.0
            rot[at + half + i, at + i] = 1.0
    return rot.T


def shape_constants():
    f = np.float32
    pos = np.arange(T).astype(f)
    inv1 = (f(500000.0) ** (-np.arange(8, dtype=f) / f(8))).astype(f)
    inv2 = (f(10000.0) ** (-np.arange(16, dtype=f) / f(16))).astype(f)
    cpos = (np.arange(NCMP) * 16 + 31).astype(f)
    c1, s1 = rope_tables([(pos, inv1, 0), (pos, inv1, HD)], P)
    cc, sc = rope_tables([(np.tile(cpos, 2), inv1, 0), (np.tile(cpos, 2), inv1, HD)], P)
    row, col = np.arange(T) // 64, np.arange(T) % 64
    c2, s2 = rope_tables([(p.astype(f), inv2, h * HD + o) for h in range(2) for p, o in ((row, 0), (col, 32))], P)
    q = np.arange(T).reshape(TT, P)
    k = np.arange(T)
    causal = np.where(k[None, None] <= q[:, :, None], 0.0, BIG)
    local = np.concatenate([np.where(np.abs(q[:, :, None] - k[None, None]) <= 128, 0.0, BIG), np.zeros((TT, P, T))], 2)
    valid = (np.arange(NCMP) * 16 + 31)[None, None] <= q[:, :, None]
    rows = lambda a: np.moveaxis(a, 0, 1).reshape(P, -1)
    parts = {
        "ident": np.eye(P), "rot1": rotation([(0, 8), (HD, 8)]), "rot2": rotation([(h * 32, 16) for h in range(4)]),
        "cos1": c1, "sin1": s1, "cos2": c2, "sin2": s2, "cosc": cc, "sinc": sc,
        "causal": rows(causal), "local": rows(local), "cmpmask": rows(np.where(valid, 0.0, BIG)),
        "rowvalid": rows(valid.any(2)[:, :, None].astype(f)), "iota8": np.tile(np.arange(8), (P, 1)),
        "iota1": np.tile(np.arange(1, CAP + 1), (P, 1)), "before": np.triu(np.ones((P, P)), 1), "ones": np.ones((P, P)),
        "place1": np.arange(1, P + 1).reshape(P, 1), "expert": np.tile(np.arange(NEXP), (P, ROUNDS)),
        "evens4": np.tile(4 * np.arange(MAX_MORE), (P, 1)),
    }
    consts = np.concatenate([parts[n] for n, _ in CONSTS], 1).astype(f)
    pool = np.zeros((4, T, T))
    for g, w in enumerate(POOL_WINDOWS):
        for t in range(T):
            lo, hi = max(t - w // 2, 0), min(t - w // 2 + w, T)
            pool[g, lo:hi, t] = 1.0 / (hi - lo)
            pool[g, t, t] -= 1.0
    pool = pool.reshape(4, TT, P, T).transpose(2, 0, 1, 3).astype(f)
    return np.ascontiguousarray(consts), np.ascontiguousarray(pool)


def k_major(w):
    return w.reshape(-1, P, w.shape[1]).transpose(1, 0, 2)


def panels(w, width, k_per):
    w = k_major(w)
    return [w[:, k:k + k_per, c:c + width] for c in range(0, w.shape[2], width) for k in range(0, w.shape[1], k_per)]


def lay_out_stream(a):
    chunks = []
    even = a["w_in_even"][0]
    chunks += panels(even[:, 0:2560], 512, 4) + panels(even[:, 2560:2816], 256, 8)
    for j in range(2):
        chunks += panels(a["nsa_cmp_w1"][0, j], 256, 8)
    for layer in range(2):
        if layer:
            chunks += panels(a["w_in_odd"][0][:, 0:3072], 512, 4)
        chunks += panels(a["w_out_odd" if layer else "w_out_even"][0], 1024, 2)
        up, down = a["mlp_w_up"][layer], a["mlp_w_down"][layer]
        for i in range(MLP_STEPS):
            chunks += panels(up[:, 1024 * i:1024 * (i + 1)], 512, 4) + panels(down[1024 * i:1024 * (i + 1)], 1024, 2)
    chunks += panels(a["w_ada_2"][0], 512, 4)
    w_in = a["w_in_2"][0]
    chunks += panels(w_in[:, 0:512], 512, 4) + panels(w_in[:, 512:768], 256, 8) + panels(w_in[:, 768:1280], 512, 4)
    chunks += panels(a["w_out_2"][0], 1024, 2)
    experts = [(a["ws_gate_2"][0], a["ws_up_2"][0], a["ws_down_2"][0])]
    experts += [(a["w_gate_2"][0, e], a["w_up_2"][0, e], a["w_down_2"][0, e]) for e in range(NEXP)]
    for gate, up, down in experts:
        chunks += panels(np.concatenate([gate, up], 1), 512, 4) + panels(down, 1024, 2)
    stream = np.empty((CHUNKS, P, SLOT), np.float32)
    for n, c in enumerate(chunks):
        stream[n] = c.reshape(P, SLOT)
    return stream


def lay_out_params(a):
    wide = lambda r: np.tile(r.reshape(1, -1), (P, 1))
    cols = lambda r: r.reshape(-1, P).T
    flat = lambda r: r.reshape(P, -1)
    w2 = a["nsa_cmp_w2"][0]
    fbias = np.zeros((P, 1), np.float32)
    fbias[0:16, 0] = a["fox_f_bias"][0]
    parts = {
        "pe": flat(a["nsa_pe"][0].reshape(2, 16, P).transpose(2, 0, 1)),
        "b1": cols(a["nsa_cmp_b1"][0]),
        "w2k": flat(np.concatenate([k_major(w2[0])] * 2, 2)),
        "w2v": flat(k_major(w2[1])),
        "wgate": flat(k_major(a["w_in_even"][0][:, 2816:2840])),
        "wforget": flat(k_major(a["w_in_odd"][0][:, 3072:3088])),
        "router": flat(k_major(a["w_router_2"][0])),
        "rbias": wide(a["router_bias_2"][0]),
        "poolw": flat(a["pool_w_2"][0].transpose(1, 0, 2)),
        "poolscale": cols(a["pool_scale_2"][0]),
        "cvec": flat(np.stack([cols(a["c_2"][0]), cols(a["c_ctx_2"])], 2)),
        "bada": cols(a["b_ada_2"][0]),
        "norm1": cols(a["norm1_g_2"][0]), "norm2": cols(a["norm2_g_2"][0]),
        "sink": wide(a["attn_sink_2"][0]), "lam": wide(a["diff_lambda"][0]), "subln": wide(a["diff_subln"][0]),
        "fbias": fbias,
    }
    return np.ascontiguousarray(np.concatenate([parts[n] for n, _ in PARAMS], 1))


def kernel(**inputs):
    import concourse.bacc as bacc
    from concourse.bass_utils import run_bass_kernel_spmd

    a = {name: np.asarray(value) for name, value in inputs.items()}
    consts, pool = shape_constants()
    b_ada = a["b_ada_2"][0]
    arrays = {
        "stream": lay_out_stream(a), "params": lay_out_params(a), "consts": consts, "poolmat": pool,
        "x": np.ascontiguousarray(a["x"][0]), "ctx": np.ascontiguousarray(a["ctx_2"][0]),
        "gain": np.ascontiguousarray(a["ln_gain"]), "bias": np.ascontiguousarray(a["ln_bias"]),
        "badarow": np.ascontiguousarray(np.concatenate([b_ada[2 * D:3 * D], b_ada[5 * D:6 * D]]).reshape(1, -1)),
        "final": np.ascontiguousarray(a["final_g_2"].reshape(1, -1)),
    }
    nc = bacc.Bacc("TRN2", target_bir_lowering=False, num_devices=1)
    aps = [nc.dram_tensor(f"in_{n}", v.shape, F32, kind="ExternalInput").ap() for n, v in arrays.items()]
    out = nc.dram_tensor("out_0", (T, D), F32, kind="ExternalOutput").ap()
    build(nc, *aps, out)
    r = run_bass_kernel_spmd(nc, [{f"in_{n}": v for n, v in arrays.items()}], core_ids=[0])
    return r.results[0]["out_0"].reshape(1, T, D)
```

```python
from contextlib import ExitStack
import math

import numpy as np

import concourse.bass as bass
from concourse import mybir

F32 = mybir.dt.float32
U32 = mybir.dt.uint32
ALU = mybir.AluOpType
ACT = mybir.ActivationFunctionType
AX = mybir.AxisListType.X

P = 128
D = 1024
T = 256
TT = T // P
KT = D // P
HD = 64
SLOT = 2048
RING = 8
BIG = -1e30
LN_EPS = 1e-5
RMS_EPS = 1e-6
ALPHA = 4.0 ** 0.25
LAM_INIT = 0.8 - 0.6 * math.exp(-0.3 * 0)
NCMP = (T - 32) // 16 + 1
NEXP = 64
ROUTED_SCALE = 2.5
POOL_WINDOWS = (2, 4, 8, 16)
SCALE = HD ** -0.5

MLP_STEPS = 4
EARLY = 1
MOD_VECTORS = ((0, 1), (2, 5, 3, 4))
MOD_CHUNKS = tuple(4 * len(v) // MLP_STEPS for v in MOD_VECTORS)
MOD_OPS = 16
SECTIONS = [
    ("kv_cmp", 2), ("qk_diff", 4), ("cmp", 4), ("v_diff", 2), ("kv_win", 1), ("q_nsa", 2), ("out_even", 4),
    ("mlp0", 8 * MLP_STEPS), ("in_odd", 12), ("out_odd", 4), ("mlp1", 8 * MLP_STEPS),
    ("in_2", 5), ("out_2", 4), ("shared", 3), ("moe", 3 * NEXP),
]
FIRST = {}
_n = 0
for _name, _count in SECTIONS:
    FIRST[_name] = _n
    _n += _count
CHUNKS = _n
RINGED = FIRST["moe"]

CAP = HD
ROUNDS = T // CAP - 1
NOV = ROUNDS * NEXP
MOE_SLOTS = 12
STEPS = NEXP // 4
MAX_MORE = (T * 8 // (CAP + 1) + 3) // 4

PARAMS = [
    ("pe", 32), ("b1", 4), ("w2k", 256), ("w2v", 128), ("wgate", 192), ("wforget", 128),
    ("router", 512), ("rbias", 64), ("poolw", 512), ("poolscale", 4), ("cvec", 16), 
    ("norm1", 8), ("norm2", 8), ("sink", 8), ("lam", 256), ("subln", 128), ("fbias", 1),
]
CONSTS = [
    ("ident", 128), ("rot1", 128), ("rot2", 128), ("cos1", 256), ("sin1", 256), ("cos2", 256), ("sin2", 256),
    ("cosc", 2 * NCMP), ("sinc", 2 * NCMP), ("causal", 512), ("local", 1024), ("cmpmask", 2 * NCMP),
    ("rowvalid", 2), ("iota8", 8), ("iota1", CAP), ("before", P), ("ones", P), ("place1", 1), ("expert", NOV),
    ("evens4", MAX_MORE),
]


def columns(blocks):
    at, n = {}, 0
    for name, width in blocks:
        at[name] = (n, width)
        n += width
    return at, n


PARAM_AT, NPARAM = columns(PARAMS)
CONST_AT, NCONST = columns(CONSTS)
TURNS = ["x0", "mix0", "ln0", "ln1", "mix1", "ln2", "ctx", "rms1", "mix2", "rms2"]
TURN_AT = {name: 4 * i for i, name in enumerate(TURNS)}


def attention_units():
    units = []
    group = 0
    for qt in range(TT):
        for h0 in (0, 4):
            for c in range(4):
                units.append(("diff", qt, h0 + c, P * (qt + 1), c * 128, 128, group))
            group += 1
    for kind in ("slc", "win", "cmp"):
        for qt in range(TT):
            for h in range(8):
                units.append((kind, qt, h, NCMP if kind == "cmp" else P * (qt + 1), h * HD, HD, group))
            group += 1
    for qt in range(TT):
        for h0 in (0, 8):
            for h in range(8):
                units.append(("fox", qt, h0 + h, P * (qt + 1), h * HD, HD, group))
            group += 1
    for qt in range(TT):
        for h in range(8):
            units.append(("loc", qt, h, 2 * T, h * HD, HD, group))
        group += 1
    return units


UNITS = attention_units()
INSTANCES = {"a0": (0, 64), "a1": (64, 96), "a2": (96, 112)}


LN_WARM = (0, 3)
START_WARM = 2
DIFF_NORM_AT = 40
ROPE_AT = 5


def group_units(g):
    return [u for u, unit in enumerate(UNITS) if unit[6] == g]


def build(nc, d_stream, d_params, d_consts, d_pool, d_x, d_ctx, d_gain, d_bias, d_ada, d_bada, d_final, d_out):
    with ExitStack() as ctx:
        def sb(name, shape, dt=F32):
            return ctx.enter_context(nc.sbuf_tensor(name, shape, dt))

        def sem(name):
            return ctx.enter_context(nc.semaphore(name))

        ring = sb("ring", [P, RING, SLOT])
        par = sb("par", [P, NPARAM])
        con = sb("con", [P, NCONST])
        x = sb("x_rows", [P, TT, D])
        y = sb("y_rows", [P, TT, D])
        mix = sb("mix_rows", [P, TT, D])
        xT = sb("xT", [P, KT, T])
        qk = sb("qk_tiles", [P, 32, T])
        v = sb("v_rows", [P, TT, D])
        pairs = sb("masked_and_probs", [P, 8, 512])
        masked, prob = pairs[:, 0:4, :], pairs[:, 4:8, :]
        probT = sb("probT", [P, 2, 512])
        vec = sb("vec_rows", [P, 4, D])
        gaterow = sb("gate_rows", [P, 2, D])
        negmax = sb("negmax", [P, len(UNITS)])
        esum = sb("esum", [P, len(UNITS)])
        small = sb("small", [P, 200])
        gate3 = sb("gate3", [P, TT, 24])
        vcmp = sb("vcmp", [P, 2, HD])
        negsink = sb("negsink", [P, 8])
        csil = sb("csil", [P, KT, 2])
        modT = sb("modT", [P, 32, 2])
        amod = sb("amod", [P, 48])
        sched = nc.dram_tensor("schedule", (P + 1, 1), mybir.dt.int32, kind="Internal").ap()
        ps = ctx.enter_context(nc.psum_tensor("ps", [P, 8, 512], F32))

        s_full = [sem(f"slot_full{i}") for i in range(RING)]
        s_used = sem("chunks_used")
        s_const = sem("consts_loaded")
        s_ident = sem("identity_loaded")
        s_x = [sem(f"x_loaded{t}") for t in range(TT)]
        s_ctx = sem("ctx_loaded")
        s_poolmat = sem("poolmat_loaded")
        s_vecA = sem("vecA_loaded")
        s_vecB = sem("vecB_loaded")
        s_ada = [sem(f"modulation_slot_full{i}") for i in range(4)]
        s_zero = sem("modulation_sums_zeroed")
        s_bada = sem("modulation_bias_loaded")
        s_mod = sem("modulation_products")
        s_mps = sem("modulation_psum")
        s_msb = sem("modulation_sbuf")
        s_x3 = sem("first_block_rows")
        s_quarter = sem("product_quarters_psum")
        s_out = sem("out_stored")
        s_rows = sem("rows_ready")
        s_turn = sem("turned_psum")
        s_xT = sem("xT_by_act")
        s_xTv = sem("xT_by_dve")
        s_gates = sem("gates_psum")
        s_projsb = sem("proj_sbuf")
        s_rot = sem("rotated_psum")
        s_roped = sem("roped")
        s_blk = sem("cmp_blocks")
        s_hrow = sem("cmp_hidden_rows")
        s_hps = sem("cmp_hidden_psum")
        s_hidsb = sem("cmp_hidden_sbuf")
        s_cmp = sem("cmp_kv_psum")
        s_cmpsb = sem("cmp_kv_sbuf")
        s_crot = sem("cmp_rotated")
        s_ckey = sem("cmp_keys_ready")
        s_sc = sem("scores_psum")
        s_mask = sem("masked_ready")
        s_exp = sem("exp_ready")
        s_pT = sem("probT_psum")
        s_pTsb = sem("probT_sbuf")
        s_o = sem("outs_psum")
        s_odone = sem("outs_taken")
        s_restaken = sem("residual_taken")
        s_var = sem("variance_ready")
        s_std = sem("std_ready")
        s_normed = sem("norms_done")
        s_relu = sem("mlp_relu")
        s_hT = sem("mlp_hidden")
        s_acc = sem("mlp_added")
        s_f = sem("forget_psum")
        s_fact = sem("forget_act")
        s_fdve = sem("forget_dve")
        s_caug = sem("forget_rows_placed")
        s_csil = sem("c_silu")
        s_ss = sem("square_sums")
        s_dps = sem("pool_psum")
        s_dsb = sem("pool_sbuf")
        s_esink = sem("sink_exp")
        s_sinkin = sem("sink_shifted")
        s_lam = sem("lambda_sums")
        s_lexp = sem("lambda_exps")
        s_rps = sem("router_psum")
        s_score = sem("router_scores")
        s_shsilu = sem("shared_silu")
        s_shact = sem("shared_act")
        s_h2 = sem("h2_rows_psum")
        s_h2sb = sem("h2_rows_sbuf")
        s_chosen = sem("experts_chosen")
        s_rank = sem("ranks_psum")
        s_sched = sem("schedule_ready")
        s_schedm = sem("schedule_in_memory")
        s_pick = sem("picked_columns")
        s_sel = sem("selection_ready")
        s_gather = sem("gathered_psum")
        s_hga = sem("gathered_by_act")
        s_hgv = sem("gathered_by_dve")
        s_silu = sem("expert_silu")
        s_hid2 = sem("expert_hidden")
        s_tps = sem("expert_turned_psum")
        s_tsb = sem("expert_turned_sbuf")
        s_ya = sem("slot_rows_by_act")
        s_yv = sem("slot_rows_by_dve")
        s_moe = sem("experts_summed")
        s_xfin = sem("x_final")
        m_full = [sem(f"expert_slot_full{i}") for i in range(MOE_SLOTS)]
        s_dve = sem("dve_chain")
        s_act = sem("act_chain")
        s_pool = sem("pool_chain")

        def windows(tiles, g):
            row = tiles[:, g, :]
            return bass.AP(row.tensor, row.offset, [row.ap[0], (2, 16), (16, NCMP)])

        def C(name, p=P):
            a, w = CONST_AT[name]
            return con[0:p, a:a + w]

        def R(name, p=P):
            a, w = PARAM_AT[name]
            return par[0:p, a:a + w]

        raw = masked.rearrange("p a b -> p (a b)").rearrange("p (s t c) -> p s t c", s=2, t=4)
        score, biased, chosen, weight = (vec[:, 0, 128 * i:128 * (i + 1)].rearrange("p (t e) -> p t e", t=TT)
                                         for i in range(4))
        ident = C("ident")
        lamc = small[:, 0:1]
        var2 = small[:, 2:4]
        std2 = small[:, 4:6]
        rstd = small[:, 6:8]
        nwt = small[:, 8:10]
        mv = small[:, 10:14].rearrange("p (t s) -> p t s", t=2)
        bn = small[:, 16:40].rearrange("p (a s) -> p a s", a=4)
        ss = small[:, 40:42]
        lsum = small[:, 42:44]
        lexp = small[:, 44:46]
        coef = small[:, 48:56]
        dms, drms, dstd, drs, dnw = (small[:, 160 + 8 * i:168 + 8 * i] for i in range(5))
        top8 = small[:, 64:80].rearrange("p (t k) -> p t k", t=2)
        warmed = small[:, 46:47]
        esink = small[:, 80:88]
        sinksh = small[:, 88:96]
        gsc = small[:, 96:112].rearrange("p (t k) -> p t k", t=2)
        gmask = small[:, 112:128].rearrange("p (t k) -> p t k", t=2)
        wsum = small[:, 128:130]
        var_c = small[:, 130:132]
        top8b = small[:, 136:152].rearrange("p (t k) -> p t k", t=2)
        gidx = sb("gidx", [P, TT, 8], U32)
        gidxf = sb("gidxf", [P, TT, 8])

        hT = qk[:, 0:8, :]
        XS = lambda j: qk[:, 20 + 2 * j:22 + 2 * j, :]
        cmpin = qk[:, 24:28, :].rearrange("p a b -> p (a b)")[:, 0:2 * 16 * 2 * NCMP].rearrange(
            "p (j m g n) -> p j m g n", j=2, m=16, g=2)
        kcraw = qk[:, 28, 0:2 * NCMP]
        kcd = qk[:, 28, 32:32 + 2 * NCMP]
        hidT = qk[:, 29, 0:4 * 2 * NCMP].rearrange("p (j t n) -> p j t n", j=2, t=2)
        hrow = qk[:, 30, :]
        kctmp = qk[:, 28, 64:64 + 2 * NCMP]
        foxq = qk[0:66, 0:16, :]
        foxk = qk[0:66, 16:32, :]
        ctxr = qk[:, 24:32, :].rearrange("p a b -> p (a b)").rearrange("p (t f) -> p t f", t=2)
        cT = qk[:, 16:24, :]
        poolmat = y[:].rearrange("p t f -> p (t f)").rearrange("p (g t c) -> p g t c", g=4, t=2)
        dT = qk[:, 9:13, :]
        mod_slot = [v[:].rearrange("p t f -> p (t f)"), qk[:, 8:16, :].rearrange("p a b -> p (a b)"),
                    qk[:, 16:24, :].rearrange("p a b -> p (a b)"), mix[:].rearrange("p t f -> p (t f)")]
        mod_slot = [w.rearrange("p (k n) -> p k n", k=4) for w in mod_slot]
        mod_sum = pairs[:].rearrange("p a b -> p (a b)")
        kvraw = qk[:, 18:20, :]
        raw2 = qk[:, 20:24, :]
        ropetmp = qk[:, 24:26, :].rearrange("p a b -> p (a b)")
        qslots = qk[:].rearrange("p a b -> p (a b)").rearrange("p (s c) -> p s c", c=SLOT)
        moe_slot = lambda i: ring[:, i, :] if i < RING else qslots[:, i - RING, :]
        h2 = mix
        hg = masked[:, 0:2, :].rearrange("p a b -> p (a b)").rearrange("p (k c) -> p k c", k=KT)
        yslot = masked[:, 2:4, :].rearrange("p a b -> p (a b)")
        select = prob[:, 0, :].rearrange("p (s t c) -> p s t c", s=2, t=2)
        selectw = prob[:, 1, :].rearrange("p (s t c) -> p s t c", s=2, t=2)
        act2 = prob[:, 2, 0:256]
        sg2 = prob[:, 2, 256:512]
        shactT = v[:, 0, 0:512].rearrange("p (k c) -> p k c", k=2)
        shsg = v[:, 0, 512:1024]
        vflat = v[:, 1, :]
        rank1 = vflat[:, 0:128].rearrange("p (t e) -> p t e", t=2)
        over = vflat[:, 128:128 + NOV]
        overpos = vflat[:, 320:320 + NOV]
        onehot = vflat[:, 512:512 + NOV]
        scratch = vflat[:, 704:704 + NOV]
        colr = vflat[:, 900:904].rearrange("p (t s) -> p t s", t=2)
        colw = vflat[:, 904:908].rearrange("p (t s) -> p t s", t=2)
        col4 = vflat[:, 900:908].rearrange("p (w s) -> p w s", w=4)
        kcount = vflat[:, 908:909]
        schedf = vflat[:, 909:911]
        tot = vflat[:, 911:912]
        rankr = y[:, 1, 0:2 * NOV].rearrange("p (t f) -> p t f", t=2)
        weightr = y[:, 1, 2 * NOV:4 * NOV].rearrange("p (t f) -> p t f", t=2)
        again_rows = y[:, 1, 0:4 * NOV].rearrange("p (w f) -> p w f", w=4)
        picked = y[:, 0, 0:4 * NOV].rearrange("p (w f) -> p w f", w=4)
        schedi = sb("schedule_ids", [P, 2], mybir.dt.int32)

        causal = C("causal").rearrange("p (q k) -> p q k", q=2)
        local = C("local").rearrange("p (q k) -> p q k", q=2)
        cmpmask = C("cmpmask").rearrange("p (q k) -> p q k", q=2)

        def scores(u):
            return ps[:, u % 2 if UNITS[u][0] == "diff" else (0, 1, 6, 7)[u % 4], :]

        def unit_operands(u):
            kind, qt, h, nk, _, w, _ = UNITS[u]
            qs = slice(qt * P, (qt + 1) * P)
            lo = HD * (h % 2)
            half = slice(lo, lo + HD)
            g = h // 4
            tiles = range(qt + 1)
            if kind == "diff":
                return (qk[half, h // 2, qs], [(qk[half, 4 + h // 2, 0:nk], 0)], causal[:, qt, 0:nk],
                        [v[:, t, (h // 2) * P:(h // 2 + 1) * P] for t in tiles])
            if kind == "slc":
                return (qk[half, 8 + h // 2, qs], [(qk[half, 12 + g, 0:nk], 0)], causal[:, qt, 0:nk],
                        [v[:, t, 512 + g * HD:512 + (g + 1) * HD] for t in tiles])
            if kind == "win":
                return (qk[half, 8 + h // 2, qs], [(qk[half, 14 + g, 0:nk], 0)], causal[:, qt, 0:nk],
                        [v[:, t, 640 + g * HD:640 + (g + 1) * HD] for t in tiles])
            if kind == "cmp":
                return (qk[half, 8 + h // 2, qs], [(kcd[half, g * NCMP:(g + 1) * NCMP], 0)], cmpmask[:, qt, :],
                        [vcmp[0:NCMP, g, :]])
            if kind == "fox":
                return (foxq[:, h, qs], [(foxk[:, h, 0:nk], 0)], causal[:, qt, 0:nk],
                        [v[:, t, h * HD:(h + 1) * HD] for t in tiles])
            return (qk[half, h // 2, qs], [(qk[half, 5 + g, :], 0), (qk[half, 7 + g, :], T)], local[:, qt, :],
                    [v[:, t, g * HD:(g + 1) * HD] for t in range(2)]
                    + [v[:, t, 128 + g * HD:128 + (g + 1) * HD] for t in range(2)])

        block = ctx.enter_context(nc.Block())

        @block.sync
        def _(sp):
            for t in range(TT):
                sp.dma_start(x[:, t, :], d_x[t * P:(t + 1) * P, :]).then_inc(s_x[t], 16)
            for s in range(RING):
                sp.dma_start(ring[:, s, :], d_stream[s]).then_inc(s_full[s], 16)
                if s == 3:
                    sp.dma_start(par[:], d_params).then_inc(s_const, 16)
            with sp.Fori(1, RINGED // RING) as it:
                for s in range(RING):
                    sp.wait_ge(s_used, it * RING + (s - RING + 1))
                    sp.dma_start(ring[:, s, :], d_stream[bass.ds(it * RING + s, 1)].rearrange("o p c -> (o p) c")
                                 ).then_inc(s_full[s], 16)
            for n in range(RINGED // RING * RING, RINGED):
                sp.wait_ge(s_used, n - RING + 1)
                sp.dma_start(ring[:, n % RING, :], d_stream[n]).then_inc(s_full[n % RING], 16)

            def load(slot, index):
                sp.dma_start(moe_slot(slot), d_stream[bass.ds(index, 1)].rearrange("o p c -> (o p) c")
                             ).then_inc(m_full[slot], 16)

            def pair_chunks(j):
                return [(6 * j + 2 * c + a, 2 * j + a, c) for c in range(3) for a in range(2)]

            for j in range(2):
                for slot, e, c in pair_chunks(j):
                    if slot < RING:
                        sp.wait_ge(s_used, RINGED - RING + (slot - RINGED) % RING + 1)
                    elif slot == RING:
                        sp.wait_ge(s_odone, UNITS[-1][6] + 1)
                    sp.dma_start(moe_slot(slot), d_stream[RINGED + 3 * e + c]).then_inc(m_full[slot], 16)
            with sp.Fori(1, STEPS) as it:
                for j in range(2):
                    for slot, e, c in pair_chunks(j):
                        sp.wait_ge(s_used, it * 12 + (RINGED - 12 + slot + 1))
                        load(slot, it * 12 + (RINGED + 3 * e + c))
            sp.wait_ge(s_schedm, 32)
            more = sp.value_load(sched[P:P + 1, :], min_val=1, max_val=MAX_MORE)
            with sp.Fori(0, more) as it:
                for j in range(2):
                    ids = [sp.value_load(sched[bass.ds(it * 4 + (2 * j + a), 1), :], min_val=0, max_val=NEXP - 1)
                           for a in range(2)]
                    for slot, e, c in pair_chunks(j):
                        sp.wait_ge(s_used, it * 12 + (RINGED + 12 * (STEPS - 1) + slot + 1))
                        load(slot, ids[e % 2] * 3 + (RINGED + c))
            for t in range(TT):
                sp.wait_ge(s_normed, 5 + t)
                sp.dma_start(d_out[t * P:(t + 1) * P, :], x[:, t, :]).then_inc(s_out, 16)
            sp.wait_ge(s_out, 16 * TT)

        @block.tensor
        def _(pe):
            def chunk(n, per=0, it=0):
                pe.wait_ge(s_full[n % RING], it * (16 * per) + 16 * (n // RING + 1) if per else 16 * (n // RING + 1))
                return ring[:, n % RING, :]

            def keep_warm(n, bank=7):
                for _ in range(n):
                    pe.matmul(ps[:, bank, :], ident, C("causal"), start=True, stop=True)

            def turn(src, name, tiles=KT, warm=(0, 0), between=None):
                for t in range(TT):
                    if between and t == 1:
                        between()
                    keep_warm(warm[t])
                    pe.wait_ge(s_rows, TT * TURNS.index(name) + t + 1)
                    for half in range(tiles // 4):
                        for j in range(4):
                            f = (4 * half + j) * P
                            mm = pe.transpose(ps[:, 4 + 2 * t + half, j * P:(j + 1) * P], src[:, t, f:f + P], ident)
                        mm.then_inc(s_turn, 4 // (tiles // 4) // 2)

            def wait_xT(name):
                pe.wait_ge(s_xT, 2 * (TURNS.index(name) + 1))
                pe.wait_ge(s_xTv, 2 * (TURNS.index(name) + 1))

            def panel(n0, started, jobs, k_per=4, between=None):
                width = SLOT // k_per
                for c in range(KT // k_per):
                    w = chunk(n0 + c).rearrange("p (k n) -> p k n", k=k_per)
                    for kind, src, col, n, bank, off in jobs:
                        for kk in range(k_per):
                            k = c * k_per + kk
                            if kind == "ws":
                                mm = pe.matmul(ps[0:n, bank, off:off + T], w[:, kk, col:col + n], src[:, k, :],
                                               start=bank not in started, stop=k == KT - 1, skip_group_check=True)
                                started.add(bank)
                            else:
                                t = kind
                                mm = pe.matmul(ps[:, bank, off:off + n], src[:, k, t * P:(t + 1) * P],
                                               w[:, kk, col:col + n], start=bank not in started, stop=k == KT - 1,
                                               skip_group_check=True)
                                started.add(bank)
                    mm.then_inc(s_used, 1)
                    if between and c == 0:
                        between()

            def rotate(rot, src, bank, n):
                return pe.matmul(ps[:, bank, 0:n], rot, src, start=True, stop=True)

            def attention(name):
                a, b = INSTANCES[name]
                for i in range(a, b + 4):
                    if i < b and i % 2 == 0:
                        if UNITS[i][0] == "slc" and UNITS[i - 1][0] == "diff":
                            pe.wait_ge(s_roped, 4)
                        if i >= 2:
                            pe.wait_ge(s_mask, i if UNITS[i][0] == "diff" or i < 18 else i - 2)
                        pair = [unit_operands(i + n)[:2] for n in range(2)]
                        for k in range(len(pair[0][1])):
                            for n, (lhs, keys) in enumerate(pair):
                                key, col = keys[k]
                                mm = pe.matmul(scores(i + n)[:, col:col + key.shape[1]], lhs, key, start=True, stop=True)
                                if k == len(keys) - 1:
                                    mm.then_inc(s_sc, 1)
                        if i < a + 4:
                            keep_warm(START_WARM, 4 + (UNITS[a][6] + 1) % 2)
                    u = i - 3
                    if a <= u < b:
                        nk = UNITS[u][3]
                        pe.wait_ge(s_exp, u + 1)
                        if u >= 2:
                            pe.wait_ge(s_pTsb, u - 1)
                        for t in range((nk + P - 1) // P):
                            n = min(P, nk - t * P)
                            mm = pe.transpose(ps[0:n, 2 + u % 2, t * P:(t + 1) * P], prob[:, u % 4, t * P:t * P + n], ident)
                        mm.then_inc(s_pT, 1)
                    u = i - 4
                    if a <= u < b:
                        _, _, _, vals = unit_operands(u)
                        _, _, _, nk, col, w, g = UNITS[u]
                        pe.wait_ge(s_pTsb, u + 1)
                        if u == group_units(g)[0] and g >= 2:
                            pe.wait_ge(s_odone, g - 1)
                        for t, val in enumerate(vals):
                            n = min(P, nk - t * P)
                            mm = pe.matmul(ps[:, 4 + g % 2, col:col + w], probT[0:n, u % 2, t * P:(t + 1) * P], val,
                                           start=t == 0, stop=t == len(vals) - 1)
                        if u == group_units(g)[-1]:
                            mm.then_inc(s_o, 1)

            def mod_columns(first, tiles, bank, at=0):
                for m in range(tiles):
                    f = first + m * P
                    mm = pe.matmul(ps[:, bank, at + m:at + m + 1], mod_sum[:, f:f + P], C("ones")[:, 0:1],
                                   start=True, stop=True)
                mm.then_inc(s_mps, 1)

            def mod_row(vector):
                for half in range(2):
                    f = vector * D + half * 512
                    mm = pe.matmul(ps[:, 2 * vector + half, :], C("ones"), mod_sum[:, f:f + 512], start=True, stop=True)
                mm.then_inc(s_mps, 1)

            def out_projection(n0):
                ws = [chunk(n0 + c).rearrange("p (k n) -> p k n", k=2) for c in range(4)]
                for q in range(4):
                    t, half = q // 2, q % 2
                    for k in range(KT):
                        mm = pe.matmul(ps[:, q, :], xT[:, k, t * P:(t + 1) * P],
                                       ws[k // 2][:, k % 2, half * 512:(half + 1) * 512], start=k == 0, stop=k == KT - 1)
                        if q == 3 and k % 2 == 1:
                            mm.then_inc(s_used, 1)
                    if q < 3:
                        mm.then_inc(s_quarter, 1)

            def mlp(layer, hook=None):
                n0 = FIRST[f"mlp{layer}"]
                pe_done = layer * 2 * MLP_STEPS

                def step(it, last):
                    for j in range(2):
                        pe.wait_ge(s_relu, it * 2 + (pe_done + EARLY))
                        started = set()
                        for c in range(2):
                            w = chunk(n0 + 2 * j + c, 1, it).rearrange("p (k n) -> p k n", k=4)
                            for m in range(4):
                                bank = 4 + 2 * j + m // 2
                                for kk in range(4):
                                    k = 4 * c + kk
                                    mm = pe.matmul(ps[:, bank, (m % 2) * T:(m % 2 + 1) * T], w[:, kk, m * P:(m + 1) * P],
                                                   xT[:, k, :], start=bank not in started, stop=k == KT - 1,
                                                   skip_group_check=True)
                                    started.add(bank)
                            mm.then_inc(s_used, 1)
                    pe.wait_ge(s_acc, it + (layer * MLP_STEPS + EARLY))
                    ws = []
                    for q in range(4):
                        t, half = q // 2, q % 2
                        for k in range(8):
                            if q == 0 and k % 2 == 0:
                                ws.append(chunk(n0 + 4 + k // 2, 1, it).rearrange("p (k n) -> p k n", k=2))
                            if q == 0 and k % 4 == 0:
                                pe.wait_ge(s_hT, it * 2 + (pe_done + k // 4 + 1))
                            mm = pe.matmul(ps[:, q, :], hT[:, k, t * P:(t + 1) * P],
                                           ws[k // 2][:, k % 2, half * 512:(half + 1) * 512], start=k == 0, stop=k == 7)
                            if q == 3 and k % 2 == 1:
                                mm.then_inc(s_used, 1)
                        if q < 3:
                            mm.then_inc(s_quarter, 1)
                        if last and hook and q == 0:
                            hook()

                with pe.Fori(0, MLP_STEPS - 1) as it:
                    step(it, False)
                step(MLP_STEPS - 1, True)

            pe.wait_ge(s_ident, 16)
            turn(x, "x0")
            wait_xT("x0")

            def ws4(bank, src=xT):
                return [("ws", src, m * P, P, bank + m // 2, (m % 2) * T) for m in range(4)]

            def rotate4(rot, s, dst=6):
                for m in range(2):
                    mm = rotate(rot, raw[:, s, 2 * m:2 * m + 2, :], dst + m, 512)
                mm.then_inc(s_rot, 1)

            panel(FIRST["kv_cmp"], set(), [("ws", xT, 0, P, 0, 0), ("ws", xT, P, P, 0, T), ("ws", xT, 2 * P, P, 1, 0),
                                           (0, xT, 3 * P, P, 1, T), (1, xT, 3 * P, P, 1, T + P)])
            panel(FIRST["qk_diff"], set(), ws4(2))
            pe.wait_ge(s_const, 32)
            pe.wait_ge(s_projsb, 1)
            panel(FIRST["qk_diff"] + 2, set(), ws4(0))
            pe.wait_ge(s_projsb, 2)
            rotate4(C("rot1"), 0)
            n0 = FIRST["cmp"]
            pe.wait_ge(s_blk, 4)
            for c in range(2):
                ws = [chunk(n0 + 2 * c + j).rearrange("p (m n) -> p m n", m=8) for j in range(2)]
                for mi in range(8):
                    m = 8 * c + mi
                    for j in range(2):
                        mm = pe.matmul(ps[j * HD:j * HD + 2 * NCMP, 4, 0:256], cmpin[:, j, m, :, :].rearrange("p g n -> p (g n)"),
                                       ws[j][:, mi, :], start=m == 0, stop=m == 15, skip_group_check=True)
                        if mi == 7:
                            mm.then_inc(s_used, 1)

            def turn_hidden():
                pe.wait_ge(s_hrow, 1)
                for j in range(2):
                    rows = slice(j * HD, j * HD + 2 * NCMP)
                    for nt in range(2):
                        mm = pe.transpose(ps[:, 4 + j, nt * 32:nt * 32 + 2 * NCMP],
                                          hrow[rows, nt * P:(nt + 1) * P], ident[rows, rows])
                mm.then_inc(s_hps, 1)

            panel(FIRST["v_diff"], set(), [(t, xT, 0, 512, 2 + t, 0) for t in range(TT)],
                  between=turn_hidden)
            pe.wait_ge(s_roped, 1)
            pe.wait_ge(s_projsb, 3)
            rotate4(C("rot1"), 1)
            pe.wait_ge(s_hidsb, 1)
            for nt in range(2):
                mm = pe.matmul(ps[:, 5, 0:2 * NCMP], R("w2k")[:, nt * P:(nt + 1) * P], hidT[:, 0, nt, :],
                               start=nt == 0, stop=nt == 1)
            for g in range(2):
                for nt in range(2):
                    mm = pe.matmul(ps[0:NCMP, 5, 64 + g * HD:64 + (g + 1) * HD], hidT[:, 1, nt, g * NCMP:(g + 1) * NCMP],
                                   R("w2v")[:, nt * HD:(nt + 1) * HD], start=nt == 0, stop=nt == 1)
            mm.then_inc(s_cmp, 1)
            panel(FIRST["kv_win"], set(), [("ws", xT, 0, P, 0, 0), (0, xT, P, P, 0, T), (1, xT, P, P, 0, T + P)], 8)
            pe.wait_ge(s_cmpsb, 1)
            for t in range(TT):
                for k in range(KT):
                    mm = pe.matmul(ps[:, 5, 256 + t * 24:256 + (t + 1) * 24], xT[:, k, t * P:(t + 1) * P],
                                   R("wgate")[:, k * 24:(k + 1) * 24], start=k == 0, stop=k == KT - 1)
            mm.then_inc(s_gates, 1)
            rotate(C("rot1"), kcraw, 4, 2 * NCMP).then_inc(s_crot, 1)
            pe.wait_ge(s_projsb, 4)
            started = set()

            def rotate_kv():
                pe.wait_ge(s_projsb, 5)
                rotate(C("rot1"), kvraw, 1, 512).then_inc(s_rot, 1)

            panel(FIRST["q_nsa"], started, ws4(2), between=rotate_kv)
            pe.wait_ge(s_projsb, 6)
            pe.wait_ge(s_roped, 2)
            for m in range(2):
                mm = rotate(C("rot1"), raw2[:, 2 * m:2 * m + 2, :], 6 + m, 512)
            mm.then_inc(s_rot, 1)
            pe.wait_ge(s_roped, 3)
            pe.wait_ge(s_ckey, 2)
            attention("a0")
            turn(mix, "mix0")
            wait_xT("mix0")
            out_projection(FIRST["out_even"])
            turn(x, "ln0", warm=LN_WARM)
            wait_xT("ln0")
            mlp(0)

            def x_columns():
                pe.wait_ge(s_mod, MOD_OPS * MLP_STEPS)
                pe.wait_ge(s_acc, MLP_STEPS + EARLY)
                mod_columns(0, 16, 3)

            turn(x, "ln1", between=x_columns)
            wait_xT("ln1")
            n0 = FIRST["in_odd"]
            for j in range(4):
                if j == 1:
                    pe.wait_ge(s_msb, 1)
                if j >= 3:
                    pe.wait_ge(s_projsb, 6 + j - 2)
                panel(n0 + 2 * j, set(), ws4(2 * (j % 3)))
                if j == 0:
                    for k in range(KT):
                        mm = pe.matmul(ps[0:16, 7, 0:T], R("wforget")[:, k * 16:(k + 1) * 16], xT[:, k, :],
                                       start=k == 0, stop=k == KT - 1)
                    mm.then_inc(s_f, 1)
                    mod_columns(2 * D, 16, 3, 16)
            for j in range(4, 6):
                pe.wait_ge(s_projsb, 6 + j - 2)
                b = 2 * (j % 3)
                panel(n0 + 2 * j, set(), [(t, xT, 0, 512, b + t, 0) for t in range(TT)])
            pe.wait_ge(s_projsb, 12)
            pe.wait_ge(s_caug, 32)
            attention("a1")
            turn(mix, "mix1")
            wait_xT("mix1")
            out_projection(FIRST["out_odd"])
            turn(x, "ln2", warm=LN_WARM)
            wait_xT("ln2")

            def turn_context():
                pe.wait_ge(s_relu, 4 * MLP_STEPS + EARLY)
                turn(ctxr, "ctx")

            mlp(1, turn_context)
            pe.wait_ge(s_mod, 2 * MOD_OPS * MLP_STEPS)
            pe.wait_ge(s_acc, 2 * MLP_STEPS + EARLY)
            mod_row(1)
            mod_row(0)
            wait_xT("ctx")
            w = chunk(FIRST["in_2"]).rearrange("p (k n) -> p k n", k=8)

            def keys_values(src, col, start):
                for k in range(KT):
                    pe.matmul(ps[:, 2, col:col + T], w[:, k, 0:P], src[:, k, :], start=start and k == 0, stop=k == KT - 1,
                              skip_group_check=True)
                for t in range(TT):
                    for k in range(KT):
                        mm = pe.matmul(ps[:, 3, col + t * P:col + (t + 1) * P], src[:, k, t * P:(t + 1) * P], w[:, k, P:2 * P],
                                       start=start and k == 0 and t == 0, stop=k == KT - 1, skip_group_check=True)
                return mm

            pe.wait_ge(s_msb, 2)
            keys_values(cT, T, True)
            turn(y, "rms1")
            wait_xT("rms1")
            keys_values(xT, 0, False).then_inc(s_used, 1)
            n0 = FIRST["in_2"] + 1
            pe.wait_ge(s_msb, 3)
            panel(n0, set(), ws4(0))
            pe.wait_ge(s_projsb, 13)
            rotate(C("rot2"), raw[:, 1, 0, :], 4, T).then_inc(s_rot, 1)
            pe.wait_ge(s_roped, 5)
            panel(n0 + 2, set(), [(t, xT, 0, 512, 4 + t, 0) for t in range(TT)])
            pe.wait_ge(s_projsb, 14)
            rotate4(C("rot2"), 0)
            pe.wait_ge(s_projsb, 15)
            pe.wait_ge(s_poolmat, 16)
            for g in range(4):
                for t in range(TT):
                    mm = pe.matmul(ps[:, 4 + g // 2, (g % 2) * T:(g % 2 + 1) * T],
                                   v[:, t, 512 + g * P:512 + (g + 1) * P], poolmat[:, g, t, :], start=t == 0, stop=t == 1)
            mm.then_inc(s_dps, 1)
            mod_columns(2 * D, 16, 0)
            pe.wait_ge(s_dsb, 1)
            pe.wait_ge(s_roped, 6)
            for g in range(4):
                mm = pe.matmul(ps[:, 6 + g // 2, (g % 2) * T:(g % 2 + 1) * T], R("poolw")[:, g * P:(g + 1) * P],
                               dT[:, g, :], start=True, stop=True)
            mm.then_inc(s_dps, 1)
            pe.wait_ge(s_dsb, 2)
            pe.wait_ge(s_msb, 4)
            attention("a2")
            turn(mix, "mix2", 4)
            wait_xT("mix2")
            out_projection(FIRST["out_2"])
            turn(y, "rms2", warm=LN_WARM)
            wait_xT("rms2")
            for t in range(TT):
                for k in range(KT):
                    mm = pe.matmul(ps[:, 6, t * NEXP:(t + 1) * NEXP], xT[:, k, t * P:(t + 1) * P],
                                   R("router")[:, k * NEXP:(k + 1) * NEXP], start=k == 0, stop=k == KT - 1)
            mm.then_inc(s_rps, 1)
            for t in range(TT):
                for half in range(2):
                    for j in range(4):
                        mm = pe.transpose(ps[:, 2 * t + half, j * P:(j + 1) * P], xT[:, 4 * half + j, t * P:(t + 1) * P], ident)
                    mm.then_inc(s_h2, 1)
            n0 = FIRST["shared"]
            panel(n0, set(), ws4(4))
            pe.wait_ge(s_chosen, 1)
            before, ones = C("before"), C("ones")
            for t, parts in enumerate(([(before, 0)], [(ones, 0), (before, 1)], [(ones, 0), (ones, 1)])):
                for i, (lhs, c) in enumerate(parts):
                    mm = pe.matmul(ps[:, 6, P + t * NEXP:P + (t + 1) * NEXP], lhs, chosen[:, c, :], start=i == 0,
                                   stop=i == len(parts) - 1)
            mm.then_inc(s_rank, 1)
            w = chunk(n0 + 2).rearrange("p (k n) -> p k n", k=2)
            pe.wait_ge(s_shact, 1)
            pe.wait_ge(s_h2sb, 4)
            for k in range(2):
                for t in range(TT):
                    for half in range(2):
                        mm = pe.matmul(ps[:, 2 * t + half, :], shactT[:, k, t * P:(t + 1) * P],
                                       w[:, k, half * 512:(half + 1) * 512], start=k == 0, stop=False, skip_group_check=True)
            mm.then_inc(s_used, 1)

            def gather(buf):
                for k, t in [(k, t) for k in range(KT) for t in range(TT)]:
                    mm = pe.matmul(ps[:, 5 + k // 4, (k % 4) * P:(k % 4 + 1) * P], h2[:, t, k * P:(k + 1) * P],
                                   select[:, buf, t, :], start=t == 0, stop=t == TT - 1)
                mm.then_inc(s_gather, 1)

            def scatter(buf, last=False):
                for t in range(TT):
                    for half in range(2):
                        mm = pe.matmul(ps[:, 2 * t + half, :], probT[:, buf, 256 + t * P:256 + (t + 1) * P],
                                       yslot[:, half * 512:(half + 1) * 512], start=False, stop=False, skip_group_check=True)
                        if last:
                            mm.then_inc(s_moe, 1)

            pe.wait_ge(s_sel, 1)
            gather(0)
            pe.wait_ge(s_schedm, 32)
            more = pe.value_load(sched[P:P + 1, :], min_val=1, max_val=MAX_MORE)
            with pe.Fori(0, more + STEPS) as it:
                for j in range(2):
                    pe.wait_ge(s_hga, it * 2 + (j + 1))
                    pe.wait_ge(s_hgv, it * 2 + (j + 1))
                    pe.wait_ge(s_hid2, it * 2 + (j + EARLY))
                    for c in range(2):
                        ws = []
                        for a in range(2):
                            slot = 6 * j + 2 * c + a
                            pe.wait_ge(m_full[slot], it * 16 + 16)
                            ws.append(moe_slot(slot).rearrange("p (k n) -> p k n", k=4))
                        for kk in range(4):
                            k = 4 * c + kk
                            for a in range(2):
                                mm = pe.matmul(ps[a * CAP:(a + 1) * CAP, 4, :], hg[:, k, a * CAP:(a + 1) * CAP],
                                               ws[a][:, kk, :], start=k == 0, stop=k == KT - 1, skip_group_check=True)
                                if kk == 3:
                                    mm.then_inc(s_used, 1)
                    pe.wait_ge(s_sel, it * 2 + (j + 2))
                    pe.wait_ge(s_ya, it * 2 + (j + EARLY))
                    pe.wait_ge(s_yv, it * 2 + (j + EARLY))
                    gather((j + 1) % 2)
                    pe.wait_ge(s_hid2, it * 2 + (j + 1 + EARLY))
                    pe.wait_ge(s_tsb, it * 2 + (j + EARLY))
                    for k in range(2):
                        pe.transpose(ps[:, 7, k * P:(k + 1) * P], act2[:, k * P:(k + 1) * P], ident)
                    for t in range(TT):
                        mm = pe.transpose(ps[:, 7, 256 + t * P:256 + (t + 1) * P], selectw[:, j, t, :], ident)
                    mm.then_inc(s_tps, 1)
                    scatter((j + 1) % 2)
                    pe.wait_ge(s_tsb, it * 2 + (j + 1 + EARLY))
                    pe.wait_ge(s_hga, it * 2 + (j + 2))
                    pe.wait_ge(s_hgv, it * 2 + (j + 2))
                    ws = []
                    for a in range(2):
                        slot = 6 * j + 4 + a
                        pe.wait_ge(m_full[slot], it * 16 + 16)
                        ws.append(moe_slot(slot).rearrange("p (k n) -> p k n", k=2))
                    for k in range(2):
                        for half in range(2):
                            for a in range(2):
                                mm = pe.matmul(ps[a * CAP:(a + 1) * CAP, 5 + half, :],
                                               probT[:, j, k * P + a * CAP:k * P + (a + 1) * CAP],
                                               ws[a][:, k, half * 512:(half + 1) * 512], start=k == 0, stop=k == 1,
                                               skip_group_check=True)
                                if k == 1 and half == 1:
                                    mm.then_inc(s_used, 1)
            pe.wait_ge(s_ya, more * 2 + (2 * STEPS + EARLY))
            pe.wait_ge(s_yv, more * 2 + (2 * STEPS + EARLY))
            scatter(1, True)

        @block.scalar
        def _(act):
            chain = [0]

            def link(ins):
                chain[0] += 1
                ins.then_inc(s_act, 1)
                act.wait_ge(s_act, chain[0])

            def panel_done(section, n):
                act.wait_ge(s_used, FIRST[section] + n)

            def take_turn(name, dst, tiles=KT):
                for t in range(TT):
                    act.wait_ge(s_turn, TURN_AT[name] + 2 * t + (1 if tiles == KT else 2))
                    act.activation(dst[:, 0:4, t * P:(t + 1) * P], ps[:, 4 + 2 * t, :].rearrange("p (j c) -> p j c", j=4),
                                   ACT.Copy).then_inc(s_xT, 1)

            def take_turn_mod(name, dst, a, b):
                for t in range(TT):
                    act.wait_ge(s_turn, TURN_AT[name] + 2 * t + 1)
                    for j in range(4):
                        i = act.activation(dst[:, j, t * P:(t + 1) * P], ps[:, 4 + 2 * t, j * P:(j + 1) * P],
                                           ACT.Identity, scale=a[:, j:j + 1], bias=b[:, j:j + 1])
                    i.then_inc(s_xT, 1)

            def copy(dst, src, **kw):
                return act.activation(dst, src, ACT.Copy, **kw)

            def copy_panel(dst, bank):
                for m in range(2):
                    i = copy(dst[:, 2 * m:2 * m + 2, :], ps[:, bank + m, :].rearrange("p (a c) -> p a c", a=2))
                return i

            def exps(name):
                a, b = INSTANCES[name]
                for u in range(a, b + 6):
                    if u < b:
                        nk = UNITS[u][3]
                        act.wait_ge(s_mask, u + 1)
                        if u >= 4:
                            act.wait_ge(s_pT, u - 3)
                        act.activation(prob[:, u % 4, 0:nk], masked[:, u % 4, 0:nk], ACT.Exp, bias=negmax[:, u:u + 1],
                                       scale=-1.0, accum_out=esum[:, u:u + 1]).then_inc(s_exp, 1)
                    if a <= u - 5 < b and group_units(UNITS[u - 5][6])[-1] == u - 5:
                        kind, qt, _, _, _, _, g = UNITS[u - 5]
                        if kind == "loc":
                            act.wait_ge(s_sinkin, qt + 1)
                            act.activation(esink, sinksh, ACT.Exp).then_inc(s_esink, 1)
                    if u == DIFF_NORM_AT:
                        act.wait_ge(s_var, 1)
                        act.activation(dstd, drms, ACT.Sqrt).then_inc(s_std, 1)

            def warm():
                act.activation(warmed, C("ones")[:, 0:1], ACT.Sqrt)

            norms = [1]

            def std(t=None):
                norms[0] += 1
                act.wait_ge(s_var, norms[0])
                cols = slice(0, TT) if t is None else slice(t, t + 1)
                act.activation(std2[:, cols], var2[:, cols], ACT.Sqrt).then_inc(s_std, 1)

            def stds():
                for t in range(TT):
                    std(t)

            def mean_squares(ready, before):
                for t in range(TT):
                    act.wait_ge(ready, before + t + 1)
                    act.activation(mix[:, t, :], x[:, t, :], ACT.Square, accum_out=ss[:, t:t + 1]).then_inc(s_ss, 1)
                    std(t)

            act.dma_start(con[:, 0:P], d_consts[:, 0:P]).then_inc(s_ident, 16)
            take_turn("x0", xT)
            act.dma_start(con[:, P:], d_consts[:, P:]).then_inc(s_const, 16)
            act.wait_ge(s_const, 32)
            act.activation(csil[:].rearrange("p k c -> p (k c)"), R("cvec"), ACT.Silu).then_inc(s_csil, 1)
            act.wait_ge(s_lam, 1)
            act.activation(lexp, lsum, ACT.Exp).then_inc(s_lexp, 1)
            panel_done("kv_cmp", 2)
            for j in range(2):
                for g in range(2):
                    rows = slice(g * HD, (g + 1) * HD)
                    copy(XS(j)[0:HD, g, :], ps[rows, 0, j * T:(j + 1) * T])
                    i = copy(XS(j)[HD:P, g, 0:T - 1], ps[rows, 0, j * T + 1:(j + 1) * T])
            copy(kvraw[:, 0, :], ps[:, 1, 0:T])
            for t in range(TT):
                i = copy(v[:, t, 512:640], ps[:, 1, T + t * P:T + (t + 1) * P])
            i.then_inc(s_projsb, 1)
            panel_done("qk_diff", 2)
            copy_panel(raw[:, 0], 2).then_inc(s_projsb, 1)
            panel_done("qk_diff", 4)
            copy_panel(raw[:, 1], 0).then_inc(s_projsb, 1)
            panel_done("cmp", 4)
            for j in range(2):
                i = copy(hrow[j * HD:j * HD + 2 * NCMP, :], ps[j * HD:j * HD + 2 * NCMP, 4, 0:256])
            i.then_inc(s_hrow, 1)
            act.wait_ge(s_hps, 1)
            for j in range(2):
                for nt in range(2):
                    i = act.activation(hidT[:, j, nt, :], ps[:, 4 + j, nt * 32:nt * 32 + 2 * NCMP],
                                       ACT.Gelu_apprx_tanh, bias=R("b1")[:, 2 * j + nt:2 * j + nt + 1])
            i.then_inc(s_hidsb, 1)
            panel_done("v_diff", 2)
            for t in range(TT):
                i = copy(v[:, t, 0:512], ps[:, 2 + t, :])
            i.then_inc(s_projsb, 1)
            act.wait_ge(s_cmp, 1)
            copy(vcmp[0:NCMP, :, :], ps[0:NCMP, 5, 64:64 + 2 * HD].rearrange("p (g d) -> p g d", g=2)).then_inc(s_ckey, 1)
            copy(kcraw, ps[:, 5, 0:2 * NCMP]).then_inc(s_cmpsb, 1)
            act.wait_ge(s_gates, 1)
            copy(kvraw[:, 1, :], ps[:, 0, 0:T])
            for t in range(TT):
                copy(v[:, t, 640:768], ps[:, 0, T + t * P:T + (t + 1) * P])
            act.activation(gate3[:], ps[:, 5, 256:304].rearrange("p (t c) -> p t c", t=2), ACT.Sigmoid).then_inc(s_projsb, 1)
            panel_done("q_nsa", 2)
            copy_panel(raw2, 2).then_inc(s_projsb, 1)
            exps("a0")
            warm()
            take_turn("mix0", xT)
            stds()
            take_turn("ln0", xT)

            def mlp(layer):
                with act.Fori(0, MLP_STEPS) as it:
                    for j in range(2):
                        base = layer * 2 * MLP_STEPS
                        act.wait_ge(s_used, it * 8 + (FIRST[f"mlp{layer}"] + 2 * j + 2))
                        for m in range(2):
                            i = act.activation(hT[:, 4 * j + 2 * m:4 * j + 2 * m + 2, :],
                                               ps[:, 4 + 2 * j + m, :].rearrange("p (a c) -> p a c", a=2), ACT.Relu)
                        i.then_inc(s_relu, 1)

            mlp(0)
            stds()
            take_turn("ln1", xT)
            for j in range(6):
                panel_done("in_odd", 2 * j + 2)
                b = 2 * (j % 3)
                if j < 4:
                    dst = foxq if j < 2 else foxk
                    for m in range(4):
                        h = 8 * (j % 2) + 2 * m
                        for o in range(2):
                            i = copy(dst[0:HD, h + o, :], ps[o * HD:(o + 1) * HD, b + m // 2, (m % 2) * T:(m % 2 + 1) * T],
                                     scale=SCALE if j < 2 else 1.0)
                else:
                    for t in range(TT):
                        i = copy(v[:, t, 512 * (j - 4):512 * (j - 3)], ps[:, b + t, :])
                i.then_inc(s_projsb, 1)
                if j == 0:
                    act.wait_ge(s_fdve, 1)
                    link(act.activation(mix[0:16, 0, 256:512], mix[0:16, 0, 256:512], ACT.Exp, scale=-1.0))
                    act.activation(mix[0:16, 0, 256:512], mix[0:16, 0, 256:512], ACT.Ln, bias=1.0).then_inc(s_fact, 1)
            exps("a1")
            warm()
            take_turn("mix1", xT)
            stds()
            take_turn("ln2", xT)
            act.wait_ge(s_ctx, 16)
            for t in range(TT):
                i = act.activation(mix[:, t, :], ctxr[:, t, :], ACT.Square, accum_out=var_c[:, t:t + 1])
            i.then_inc(s_ss, 1)
            act.wait_ge(s_ss, 1)
            std()
            mlp(1)
            act.wait_ge(s_mod, 2 * MOD_OPS * MLP_STEPS)
            take_turn_mod("ctx", cT, amod[:, 8:16], modT[:, 0:8, 1])
            stds()
            for i in range(2):
                act.wait_ge(s_mps, 3 + i)
                copy(gaterow[:, 1 - i, :], ps[:, 2 * (1 - i):2 * (1 - i) + 2, :].rearrange("p a b -> p (a b)")).then_inc(s_msb, 1)
            mean_squares(s_x3, 0)
            take_turn_mod("rms1", xT, amod[:, 0:8], modT[:, 0:8, 0])
            panel_done("in_2", 1)
            copy(raw[:, 1, 0, :], ps[:, 2, 0:T])
            for g in range(2):
                for o in range(2):
                    copy(qk[o * HD:(o + 1) * HD, 7 + g, :], ps[g * HD:(g + 1) * HD, 2, T:2 * T])
            for t in range(TT):
                copy(v[:, t, 0:128], ps[:, 3, t * P:(t + 1) * P])
                i = copy(v[:, t, 128:256], ps[:, 3, T + t * P:T + (t + 1) * P])
            i.then_inc(s_projsb, 1)
            panel_done("in_2", 3)
            copy_panel(raw[:, 0], 0).then_inc(s_projsb, 1)
            panel_done("in_2", 5)
            for t in range(TT):
                i = copy(v[:, t, 512:1024], ps[:, 4 + t, :])
            i.then_inc(s_projsb, 1)
            act.wait_ge(s_dps, 1)
            copy_panel(dT, 4).then_inc(s_dsb, 1)
            act.wait_ge(s_mps, 5)
            copy(modT[:, 16:32, 0], ps[:, 0, 0:16]).then_inc(s_msb, 1)
            act.wait_ge(s_dps, 2)
            for g in range(4):
                i = act.activation(xT[:, 4 + g, :], ps[:, 6 + g // 2, (g % 2) * T:(g % 2 + 1) * T],
                                   ACT.Identity, scale=R("poolscale")[:, g:g + 1])
            i.then_inc(s_dsb, 1)
            exps("a2")
            warm()
            take_turn("mix2", xT, 4)
            mean_squares(s_restaken, 0)
            take_turn_mod("rms2", xT, amod[:, 16:24], modT[:, 16:24, 0])
            act.wait_ge(s_rps, 1)
            act.activation(score, ps[:, 6, 0:2 * NEXP].rearrange("p (t e) -> p t e", t=2), ACT.Sigmoid).then_inc(s_score, 1)
            act.wait_ge(s_ss, 5)
            for t in range(TT):
                for half in range(2):
                    act.wait_ge(s_h2, 2 * t + half + 1)
                    copy(h2[:, t, half * 512:(half + 1) * 512], ps[:, 2 * t + half, :]).then_inc(s_h2sb, 1)
            panel_done("shared", 2)
            act.activation(shsg, ps[:, 4, :], ACT.Silu).then_inc(s_shsilu, 1)

            def take_gathered(n):
                act.wait_ge(s_gather, n)
                copy(hg[:, 0:4, :].rearrange("p k c -> p (k c)"), ps[:, 5, :]).then_inc(s_hga, 1)

            take_gathered(1)
            act.wait_ge(s_schedm, 32)
            more = act.value_load(sched[P:P + 1, :], min_val=1, max_val=MAX_MORE)
            with act.Fori(0, more + STEPS) as it:
                for j in range(2):
                    act.wait_ge(s_used, it * 12 + (RINGED + 6 * j + 4))
                    act.wait_ge(s_hid2, it * 2 + (j + EARLY))
                    act.activation(sg2, ps[:, 4, 0:256], ACT.Silu).then_inc(s_silu, 1)
                    take_gathered(it * 2 + (j + 2))
                    act.wait_ge(s_used, it * 12 + (RINGED + 6 * j + 6))
                    copy(yslot[:, 0:512], ps[:, 5, :]).then_inc(s_ya, 1)
            warm()
            mean_squares(s_xfin, 0)

        @block.vector
        def _(dve):
            chain = [0]

            def link(ins):
                chain[0] += 1
                ins.then_inc(s_dve, 1)
                dve.wait_ge(s_dve, chain[0])

            def take_turn(name, dst, tiles=KT):
                for t in range(TT):
                    dve.wait_ge(s_turn, TURN_AT[name] + 2 * t + 2)
                    if tiles == KT:
                        dve.tensor_copy(dst[:, 4:8, t * P:(t + 1) * P],
                                        ps[:, 5 + 2 * t, :].rearrange("p (j c) -> p j c", j=4)).then_inc(s_xTv, 1)

            def take_turn_mod(name, dst, a, b):
                for t in range(TT):
                    dve.wait_ge(s_turn, TURN_AT[name] + 2 * t + 2)
                    for j in range(4):
                        i = dve.tensor_scalar(dst[:, 4 + j, t * P:(t + 1) * P], ps[:, 5 + 2 * t, j * P:(j + 1) * P],
                                              a[:, 4 + j:5 + j], b[:, 4 + j:5 + j], ALU.mult, ALU.add)
                    i.then_inc(s_xTv, 1)

            def rope(out, src, banks, cos, sin, tiles, tmp=None):
                for m in range((tiles + 1) // 2):
                    n = min(2, tiles - 2 * m)
                    s3 = [P, n, T]
                    o, i0 = out[:, 2 * m:2 * m + n, :], src[:, 2 * m:2 * m + n, :]
                    rot = ps[:, banks + m, 0:n * T].rearrange("p (a c) -> p a c", a=n)
                    part = (probT[:, 0, 0:n * T] if tmp is None else tmp).rearrange("p (a c) -> p a c", a=n)
                    dve.tensor_tensor(o, i0, cos.unsqueeze(1).to_broadcast(s3), ALU.mult)
                    link(dve.tensor_tensor(part, rot, sin.unsqueeze(1).to_broadcast(s3), ALU.mult))
                    i = dve.tensor_tensor(o, o, part, ALU.add)
                    if 2 * m + n < tiles:
                        link(i)
                return i

            def inv_sqrt(out, var, std, tmp):
                link(dve.reciprocal(out, std))
                link(dve.tensor_tensor(tmp, out, out, ALU.mult))
                link(dve.tensor_tensor(tmp, tmp, var, ALU.mult))
                link(dve.tensor_scalar(tmp, tmp, -0.5, 1.5, ALU.mult, ALU.add))
                link(dve.tensor_tensor(out, out, tmp, ALU.mult))

            def take_group(g):
                units = group_units(g)
                kind, qt, h0 = UNITS[units[0]][:3]
                a, n = units[0], len(units)
                bank = 4 + g % 2
                dve.wait_ge(s_o, g + 1)
                if kind == "loc":
                    dve.tensor_tensor(sinksh, R("sink"), negmax[:, a:a + n], ALU.add).then_inc(s_sinkin, 1)
                    dve.wait_ge(s_esink, qt + 1)
                    link(dve.tensor_tensor(esum[:, a:a + n], esum[:, a:a + n], esink, ALU.add))
                link(dve.reciprocal(coef[:, 0:n], esum[:, a:a + n]))
                if kind == "diff":
                    o4 = y[:, 0, 0:512].rearrange("p (c w) -> p c w", c=4)
                    link(dve.tensor_tensor(o4, ps[:, bank, :].rearrange("p (c w) -> p c w", c=4),
                                           coef[:, 0:4].unsqueeze(2).to_broadcast([P, 4, P]), ALU.mult))
                    o2 = y[:, 0, 0:512].rearrange("p (h c w) -> p h c w", h=2, c=2)
                    dif = mix[:, qt, (h0 // 2) * P:(h0 // 2 + 2) * P].rearrange("p (h w) -> p h w", h=2)
                    sq = y[:, 1, 0:256].rearrange("p (h w) -> p h w", h=2)
                    for h in range(2):
                        i = dve.scalar_tensor_tensor(out=dif[:, h, :], in0=o2[:, h, 1, :], scalar=lamc, in1=o2[:, h, 0, :],
                                                     op0=ALU.mult, op1=ALU.add)
                    i.then_inc(s_odone, 1)
                    dve.wait_ge(s_odone, g + 1)
                    link(dve.tensor_tensor(sq, dif, dif, ALU.mult))
                    link(dve.tensor_reduce(dms[:, 2 * g:2 * g + 2], sq, AX, ALU.add))
                    return
                if kind in ("slc", "win", "cmp"):
                    b = {"cmp": 0, "slc": 1, "win": 2}[kind]
                    gates = gate3[:, qt, :].rearrange("p (h b) -> p h b", b=3)[:, :, b]
                    link(dve.tensor_tensor(coef, coef, gates, ALU.mult))
                    if kind == "cmp":
                        link(dve.tensor_scalar(coef, coef, C("rowvalid")[:, qt:qt + 1], None, ALU.mult))
                    out = mix[:, qt, 512:1024]
                else:
                    out = mix[:, qt, h0 * HD:(h0 + 8) * HD]
                out3 = out.rearrange("p (h w) -> p h w", h=8)
                o3 = ps[:, bank, :].rearrange("p (h w) -> p h w", h=8)
                c3 = coef.unsqueeze(2).to_broadcast([P, 8, HD])
                if kind in ("win", "cmp"):
                    tmp = y[:, 0, 0:512].rearrange("p (h w) -> p h w", h=8)
                    link(dve.tensor_tensor(tmp, o3, c3, ALU.mult))
                    i = dve.tensor_tensor(out3, out3, tmp, ALU.add)
                else:
                    i = dve.tensor_tensor(out3, o3, c3, ALU.mult)
                i.then_inc(s_odone, 1)
                dve.wait_ge(s_odone, g + 1)

            def norm_diff():
                def variance():
                    dve.tensor_scalar(drms, dms, 1.0 / P, LN_EPS, ALU.mult, ALU.add).then_inc(s_var, 1)

                def root():
                    dve.wait_ge(s_std, 1)
                    inv_sqrt(drs, drms, dstd, dnw)
                    link(dve.tensor_scalar(drs, drs, 1.0 - LAM_INIT, None, ALU.mult))

                def scale(t, gain):
                    dif = mix[:, t, 0:512].rearrange("p (h w) -> p h w", h=4)
                    by = R("subln").unsqueeze(1) if gain else drs[:, 4 * t:4 * t + 4].unsqueeze(2)
                    return lambda: link(dve.tensor_tensor(dif, dif, by.to_broadcast([P, 4, P]), ALU.mult))

                return {DIFF_NORM_AT: variance, DIFF_NORM_AT + 2: root} | {
                    DIFF_NORM_AT + 3 + 2 * t + gain: scale(t, gain) for t in range(TT) for gain in range(2)}

            def attention(name, hooks):
                a, b = INSTANCES[name]
                for i in range(a, b + 6):
                    if i < b:
                        kind, qt, h, nk, _, _, _ = UNITS[i]
                        _, _, mask, _ = unit_operands(i)
                        dve.wait_ge(s_sc, i + 1)
                        if i >= 4:
                            dve.wait_ge(s_exp, i - 3)
                        first = negsink[:, h:h + 1] if kind == "loc" else 1e38
                        dve.tensor_tensor_reduce(out=masked[:, i % 4, 0:nk], in0=scores(i)[:, 0:nk], in1=mask,
                                                 scale=-1.0 if kind == "fox" else -SCALE, scalar=first,
                                                 op0=ALU.add, op1=ALU.min, accum_out=negmax[:, i:i + 1]).then_inc(s_mask, 1)
                    u = i - 3
                    if a <= u < b:
                        nk = UNITS[u][3]
                        n = P if nk >= P else nk
                        w = P * ((nk + P - 1) // P)
                        dve.wait_ge(s_pT, u + 1)
                        dve.tensor_copy(probT[0:n, u % 2, 0:w], ps[0:n, 2 + u % 2, 0:w]).then_inc(s_pTsb, 1)
                    u = i - 5
                    if a <= u < b and u == group_units(UNITS[u][6])[-1]:
                        take_group(UNITS[u][6])
                    if i - a in hooks:
                        hooks[i - a]()

            def half_stats(q):
                i = dve.bn_stats(bn[:, q, :], y[:, q // 2, (q % 2) * 512:(q % 2 + 1) * 512])
                if q % 2 == 1:
                    link(i)
                    link(dve.bn_aggr(mv[:, q // 2, :], bn[:, q - 1:q + 1, :]))

            norms = [1]
            rows = [0]

            def layer_norm(t, g_row, b_row, s_vec, v_vec, turned=True):
                norms[0] += 1
                c = slice(t, t + 1)
                dve.tensor_scalar(var2[:, c], mv[:, t, 1:2], LN_EPS, None, ALU.add).then_inc(s_var, 1)
                dve.wait_ge(s_vec, v_vec)
                link(dve.scalar_tensor_tensor(out=y[:, t, :], in0=y[:, t, :], scalar=mv[:, t, 0:1], in1=g_row,
                                              op0=ALU.subtract, op1=ALU.mult))
                dve.wait_ge(s_std, norms[0])
                inv_sqrt(rstd[:, c], var2[:, c], std2[:, c], nwt[:, c])
                i = dve.scalar_tensor_tensor(out=x[:, t, :], in0=y[:, t, :], scalar=rstd[:, c], in1=b_row,
                                             op0=ALU.mult, op1=ALU.add)
                if turned:
                    rows[0] += 1
                    i.then_inc(s_rows, 1)
                    dve.wait_ge(s_rows, rows[0])
                else:
                    i.then_inc(s_x3, 1)
                    dve.wait_ge(s_x3, t + 1)

            def inverse_rms(t, sums):
                norms[0] += 1
                c = slice(t, t + 1)
                dve.wait_ge(s_ss, sums)
                dve.tensor_scalar(var2[:, c], ss[:, c], 1.0 / D, RMS_EPS, ALU.mult, ALU.add).then_inc(s_var, 1)
                dve.wait_ge(s_std, norms[0])
                inv_sqrt(rstd[:, c], var2[:, c], std2[:, c], nwt[:, c])

            def rms_rows(t, sums):
                inverse_rms(t, sums)
                link(dve.tensor_scalar(y[:, t, :], x[:, t, :], rstd[:, t:t + 1], None, ALU.mult))
                rows_ready(1)

            def rows_ready(n=1):
                rows[0] += n
                dve.engine_nop().then_inc(s_rows, n)

            def normed():
                dve.engine_nop().then_inc(s_normed, 1)

            def residual(section, before, norm):
                for q in range(4):
                    t, cols = q // 2, slice((q % 2) * 512, (q % 2 + 1) * 512)
                    if q < 3:
                        dve.wait_ge(s_quarter, before + q + 1)
                    else:
                        dve.wait_ge(s_used, FIRST[section] + 4)
                    link(dve.scalar_tensor_tensor(out=y[:, t, cols], in0=x[:, t, cols], scalar=ALPHA, in1=ps[:, q, :],
                                                  op0=ALU.mult, op1=ALU.add))
                    half_stats(q)
                    if q % 2 == 1:
                        norm(q // 2)

            def modulate(layer, it, piece):
                per = MOD_CHUNKS[layer]
                ops = 4 * piece
                if layer == 0:
                    c, terms = piece // 2, [(2 * (piece % 2) + n // 2, n % 2) for n in range(4)]
                else:
                    c, terms = piece, [(n, 0) for n in range(4)]
                if ops % (MOD_OPS // per) == 0:
                    before = 16 * MLP_STEPS if layer and c < MOD_CHUNKS[0] else 0
                    dve.wait_ge(s_ada[c], it * 16 + (before + 16))
                for n, (kk, cond) in enumerate(terms):
                    at = mod_sum[:, bass.ds(it * (256 * per) + (cond * 2 * D + c // 2 * 512), 512)]
                    dve.scalar_tensor_tensor(out=at, in0=mod_slot[c][:, kk, :], scalar=csil[:, 4 * (c % 2) + kk, cond:cond + 1],
                                             in1=at, op0=ALU.mult, op1=ALU.add).then_inc(s_mod, 1)
                    dve.wait_ge(s_mod, it * MOD_OPS + (layer * MOD_OPS * MLP_STEPS + ops + n + 1))

            def mlp(layer, norm, hook=None):
                dve.wait_ge(s_bada, (32, 80)[layer])
                link(dve.tensor_scalar(y[:].rearrange("p t f -> p (t f)"), x[:].rearrange("p t f -> p (t f)"), ALPHA, None,
                                       ALU.mult))
                base = layer * 2 * MLP_STEPS

                def step(it, last):
                    for j in range(2):
                        dve.wait_ge(s_relu, it * 2 + (base + j + 1 + EARLY))
                        h2 = hT[:, 4 * j:4 * j + 4, :].rearrange("p a c -> p (a c)")
                        dve.tensor_tensor(h2, h2, h2, ALU.mult).then_inc(s_hT, 1)
                        modulate(layer, it, 2 * j)
                        modulate(layer, it, 2 * j + 1)
                    dve.wait_ge(s_acc, it + (layer * MLP_STEPS + EARLY))
                    for q in range(4):
                        if q < 3:
                            dve.wait_ge(s_quarter, it * 3 + (3 * layer * (MLP_STEPS + 1) + 3 + q + 1))
                        else:
                            dve.wait_ge(s_used, it * 8 + (FIRST[f"mlp{layer}"] + 8))
                        half = y[:, q // 2, (q % 2) * 512:(q % 2 + 1) * 512]
                        i = dve.tensor_tensor(half, ps[:, q, :], half, ALU.add)
                        if last and q < 3:
                            link(i)
                            half_stats(q)
                            if q == 0 and hook:
                                hook()
                            if q == 1:
                                norm(0)
                    i.then_inc(s_acc, 1)

                with dve.Fori(0, MLP_STEPS - 1) as it:
                    step(it, False)
                step(MLP_STEPS - 1, True)
                dve.wait_ge(s_acc, (layer + 1) * MLP_STEPS + EARLY)
                half_stats(3)
                norm(1)

            for s in (s_relu, s_acc, s_hid2, s_tsb, s_tps, s_ya, s_yv):
                dve.engine_nop().then_inc(s, EARLY)
            rows[0] = 2
            for t in range(TT):
                dve.wait_ge(s_x[t], 16)
                dve.engine_nop().then_inc(s_rows, 1)
            take_turn("x0", xT)
            dve.wait_ge(s_const, 32)
            lam4 = R("lam").rearrange("p (a d) -> p a d", a=4)
            lp = y[:, 0, 0:2 * HD].rearrange("p (a d) -> p a d", a=2)
            link(dve.tensor_tensor(lp, lam4[:, 0:4:2, :], lam4[:, 1:4:2, :], ALU.mult))
            dve.tensor_reduce(lsum, lp, AX, ALU.add).then_inc(s_lam, 1)
            dve.wait_ge(s_csil, 1)
            dve.wait_ge(s_lexp, 1)
            link(dve.tensor_tensor(lamc, lexp[:, 1:2], lexp[:, 0:1], ALU.subtract))
            link(dve.tensor_scalar(lamc, lamc, -LAM_INIT, None, ALU.add))
            link(dve.tensor_scalar(negsink[:], R("sink"), -1.0, None, ALU.mult))
            dve.wait_ge(s_rot, 1)
            rope(qk[:, 0:4, :], raw[:, 0], 6, C("cos1"), C("sin1"), 4).then_inc(s_roped, 1)
            dve.wait_ge(s_rot, 2)
            dve.wait_ge(s_roped, 1)
            rope(qk[:, 4:8, :], raw[:, 1], 6, C("cos1"), C("sin1"), 4).then_inc(s_roped, 1)
            dve.wait_ge(s_crot, 1)
            dve.tensor_tensor(kcd, kcraw, C("cosc"), ALU.mult)
            link(dve.tensor_tensor(kctmp, ps[:, 4, 0:2 * NCMP], C("sinc"), ALU.mult))
            dve.tensor_tensor(kcd, kcd, kctmp, ALU.add).then_inc(s_ckey, 1)
            dve.wait_ge(s_rot, 3)
            dve.wait_ge(s_roped, 2)
            link(rope(qk[:, 16:18, :], kvraw, 1, C("cos1"), C("sin1"), 2))
            for j in range(2):
                for g in range(2):
                    for o in range(2):
                        i = dve.tensor_copy(qk[o * HD:(o + 1) * HD, 12 + 2 * j + g, :], qk[g * HD:(g + 1) * HD, 16 + j, :])
            i.then_inc(s_roped, 1)

            def rope_nsa(m):
                two = slice(2 * m, 2 * m + 2)
                o, src = qk[:, 8:12, :][:, two], raw2[:, two]
                part = ropetmp.rearrange("p (a c) -> p a c", a=2)
                rot = ps[:, 6 + m, :].rearrange("p (a c) -> p a c", a=2)
                cos, sin = (C(n).unsqueeze(1).to_broadcast([P, 2, T]) for n in ("cos1", "sin1"))

                def rotated():
                    dve.wait_ge(s_rot, 4)
                    link(dve.tensor_tensor(part, rot, sin, ALU.mult))

                def add():
                    i = dve.tensor_tensor(o, o, part, ALU.add)
                    if m == 0:
                        link(i)
                    else:
                        i.then_inc(s_roped, 1)

                return {ROPE_AT + 3 * m: lambda: link(dve.tensor_tensor(o, src, cos, ALU.mult)),
                        ROPE_AT + 3 * m + 1: rotated, ROPE_AT + 3 * m + 2: add}

            attention("a0", rope_nsa(0) | rope_nsa(1) | norm_diff())
            rows_ready(2)
            take_turn("mix0", xT)
            residual("out_even", 0, lambda t: layer_norm(t, vec[:, 0, :], vec[:, 1, :], s_vecA, 32))
            normed()
            take_turn("ln0", xT)
            mlp(0, lambda t: layer_norm(t, vec[:, 2, :], vec[:, 3, :], s_vecB, 32))
            normed()
            take_turn("ln1", xT)
            dve.wait_ge(s_mps, 2)
            for c in range(2):
                i = dve.tensor_copy(modT[:, 0:16, c], ps[:, 3, 16 * c:16 * c + 16])
            link(i)
            for c in range(2):
                i = dve.scalar_tensor_tensor(out=amod[:, 8 * c:8 * c + 8], in0=modT[:, 8:16, c], scalar=1.0, in1=R("norm1"),
                                             op0=ALU.add, op1=ALU.mult)
            i.then_inc(s_msb, 1)
            zmin, zabs, logf, csum, ones = (mix[0:16, i // 4, (i % 4) * 256:(i % 4 + 1) * 256] for i in range(5))
            dve.wait_ge(s_f, 1)
            fb = R("fbias", 16)
            link(dve.tensor_scalar(logf, ps[0:16, 7, 0:T], fb, None, ALU.add))
            dve.tensor_scalar(zmin, logf, 0.0, None, ALU.min)
            link(dve.tensor_scalar(ones, logf, 0.0, None, ALU.max))
            link(dve.tensor_tensor(zabs, ones, zmin, ALU.subtract))
            link(dve.memset(ones, 1.0))
            dve.engine_nop().then_inc(s_fdve, 1)
            dve.wait_ge(s_fact, 1)
            link(dve.tensor_tensor(logf, zmin, zabs, ALU.subtract))
            link(dve.tensor_tensor_scan(csum, ones, logf, 0.0, ALU.mult, ALU.add))
            link(dve.tensor_scalar(zmin, csum, -1.0, None, ALU.mult))
            link(dve.memset(foxq[64:66, :, :], 1.0))
            link(dve.memset(foxk[64:66, :, :], 1.0))
            dve.engine_nop().then_inc(s_fdve, 1)
            attention("a1", {})
            rows_ready(2)
            take_turn("mix1", xT)
            residual("out_odd", 3 * (MLP_STEPS + 1), lambda t: layer_norm(t, vec[:, 0, :], vec[:, 1, :], s_vecA, 64))
            normed()
            take_turn("ln2", xT)
            dve.wait_ge(s_ss, 1)
            dve.tensor_scalar(var2, var_c, 1.0 / D, RMS_EPS, ALU.mult, ALU.add).then_inc(s_var, 1)
            norms[0] += 1
            dve.wait_ge(s_std, norms[0])
            inv_sqrt(rstd, var2, std2, nwt)
            for t in range(TT):
                link(dve.tensor_scalar(ctxr[:, t, :], ctxr[:, t, :], rstd[:, t:t + 1], None, ALU.mult))
            rows_ready(2)
            mlp(1, lambda t: layer_norm(t, vec[:, 2, :], vec[:, 3, :], s_vecB, 64, turned=False),
                lambda: take_turn_mod("ctx", cT, amod[:, 8:16], modT[:, 0:8, 1]))
            normed()
            for t in range(TT):
                rms_rows(t, t + 2)
            take_turn_mod("rms1", xT, amod[:, 0:8], modT[:, 0:8, 0])
            dve.wait_ge(s_rot, 5)
            link(rope(qk[:, 4:5, :], raw[:, 1], 4, C("cos2"), C("sin2"), 1))
            for g in range(2):
                for o in range(2):
                    i = dve.tensor_copy(qk[o * HD:(o + 1) * HD, 5 + g, :], qk[g * HD:(g + 1) * HD, 4, :])
            i.then_inc(s_roped, 1)
            dve.wait_ge(s_rot, 6)
            dve.wait_ge(s_roped, 5)
            rope(qk[:, 0:4, :], raw[:, 0], 6, C("cos2"), C("sin2"), 4).then_inc(s_roped, 1)
            dve.wait_ge(s_msb, 4)
            link(dve.scalar_tensor_tensor(out=amod[:, 16:24], in0=modT[:, 24:32, 0], scalar=1.0, in1=R("norm2"), op0=ALU.add,
                                          op1=ALU.mult))
            attention("a2", {})
            rows_ready(2)
            take_turn("mix2", xT, 4)
            dve.engine_nop().then_inc(s_xTv, 2)
            for q in range(4):
                t, cols = q // 2, slice((q % 2) * 512, (q % 2 + 1) * 512)
                if q < 3:
                    dve.wait_ge(s_quarter, 6 * (MLP_STEPS + 1) + q + 1)
                else:
                    dve.wait_ge(s_used, FIRST["out_2"] + 4)
                link(dve.tensor_tensor(y[:, t, cols], ps[:, q, :], gaterow[:, 0, cols], ALU.mult))
                i = dve.tensor_tensor(x[:, t, cols], x[:, t, cols], y[:, t, cols], ALU.add)
                if q % 2 == 1:
                    i.then_inc(s_restaken, 1)
                    dve.wait_ge(s_restaken, t + 1)
                if q >= 2:
                    rms_rows(q - 2, q + 2)
            take_turn_mod("rms2", xT, amod[:, 16:24], modT[:, 16:24, 0])
            dve.wait_ge(s_score, 1)
            e3 = [P, TT, NEXP]
            link(dve.tensor_tensor(biased, score, R("rbias").unsqueeze(1).to_broadcast(e3), ALU.add))
            for t in range(TT):
                for g in range(8):
                    link(dve.max(top8[:, t, :], biased[:, t, 8 * g:8 * g + 8]))
                    link(dve.tensor_tensor(gsc[:, t, g:g + 1], top8[:, t, 0:1], top8[:, t, 1:2], ALU.add))
                link(dve.max(top8[:, t, :], gsc[:, t, :]))
                link(dve.max_index(gidx[:, t, :], top8[:, t, :], gsc[:, t, :]))
            link(dve.tensor_copy(gidxf[:], gidx[:]))
            for t in range(TT):
                link(dve.tensor_scalar(gmask[:, t, :], C("iota8"), gidxf[:, t, 0:1], None, ALU.is_equal))
                for r in range(1, 4):
                    link(dve.scalar_tensor_tensor(out=gmask[:, t, :], in0=C("iota8"), scalar=gidxf[:, t, r:r + 1],
                                                  in1=gmask[:, t, :], op0=ALU.is_equal, op1=ALU.add))
                b8 = biased[:, t, :].rearrange("p (g e) -> p g e", g=8)
                m8 = gmask[:, t, :].unsqueeze(2).to_broadcast([P, 8, 8])
                c8 = chosen[:, t, :].rearrange("p (g e) -> p g e", g=8)
                link(dve.tensor_tensor(b8, b8, m8, ALU.mult))
                link(dve.tensor_scalar(c8, m8, -1.0, 1e30, ALU.add, ALU.mult))
                link(dve.tensor_tensor(b8, b8, c8, ALU.add))
                link(dve.max(top8b[:, t, :], biased[:, t, :]))
                link(dve.match_replace(chosen[:, t, :], top8b[:, t, :], biased[:, t, :], 3e30))
            dve.tensor_scalar(chosen, chosen, 2e30, None, ALU.is_ge).then_inc(s_chosen, 1)
            dve.wait_ge(s_chosen, 1)
            link(dve.tensor_tensor(score, score, chosen, ALU.mult))
            link(dve.tensor_reduce(wsum, score, AX, ALU.add))
            link(dve.reciprocal(wsum, wsum))
            for t in range(TT):
                i = dve.tensor_scalar(weight[:, t, :], score[:, t, :], wsum[:, t:t + 1], ROUTED_SCALE, ALU.mult,
                                      ALU.mult)
            link(i)
            dve.wait_ge(s_shsilu, 1)
            dve.tensor_tensor(shactT[:].rearrange("p k c -> p (k c)"), shsg, ps[:, 5, :], ALU.mult).then_inc(s_shact, 1)
            dve.wait_ge(s_rank, 1)
            link(dve.scalar_tensor_tensor(out=rank1, in0=ps[:, 6, P:P + 2 * NEXP].rearrange("p (t e) -> p t e", t=2),
                                          scalar=1.0, in1=chosen, op0=ALU.add, op1=ALU.mult))
            for r in range(ROUNDS):
                cols = slice(r * NEXP, (r + 1) * NEXP)
                dve.tensor_scalar(over[:, cols], ps[:, 6, P + 2 * NEXP:P + 3 * NEXP], float(CAP * (r + 1)), None, ALU.is_gt)
                dve.tensor_scalar(rankr[:, :, cols], rank1, -float(CAP * (r + 1)), None, ALU.add)
                i = dve.tensor_copy(weightr[:, :, cols], weight)
            link(i)
            link(dve.memset(onehot, 1.0))
            link(dve.tensor_tensor_scan(scratch, onehot, over, 0.0, ALU.mult, ALU.add))
            dve.tensor_copy(tot, scratch[:, NOV - 1:NOV])
            link(dve.tensor_tensor(overpos, scratch, over, ALU.mult))
            link(dve.tensor_scalar(onehot, overpos, C("place1"), None, ALU.is_equal))
            link(dve.tensor_tensor(scratch, onehot, C("expert"), ALU.mult))
            link(dve.tensor_reduce(schedf[:, 0:1], scratch, AX, ALU.add))
            link(dve.tensor_scalar(scratch[:, 0:MAX_MORE], C("evens4"), tot, None, ALU.is_lt))
            link(dve.tensor_reduce(schedf[:, 1:2], scratch[:, 0:MAX_MORE], AX, ALU.add))
            link(dve.tensor_scalar(schedf[:, 1:2], schedf[:, 1:2], 1.0, None, ALU.max))
            dve.tensor_copy(schedi[:], schedf).then_inc(s_sched, 1)
            link(dve.memset(kcount, 0.0))
            link(dve.memset(yslot, 0.0))
            link(dve.memset(probT[:, 1, :], 0.0))

            def select_experts(buf, cols):
                for t in range(TT):
                    for a in range(2):
                        r, w = cols(t, a)
                        sl = slice(a * CAP, (a + 1) * CAP)
                        dve.tensor_scalar(select[:, buf, t, sl], C("iota1"), r, None, ALU.is_equal)
                        i = dve.tensor_scalar(selectw[:, buf, t, sl], C("iota1"), r, w, ALU.is_equal, ALU.mult)
                i.then_inc(s_sel, 1)

            def first_round(e):
                return lambda t, a: (rank1[:, t, bass.ds(e + a, 1)], weight[:, t, bass.ds(e + a, 1)])

            def fixed_round(e):
                return lambda t, a: (rank1[:, t, e + a:e + a + 1], weight[:, t, e + a:e + a + 1])

            def pick_again(wait_base, it, per):
                n = [0]

                def step(ins):
                    n[0] += 1
                    ins.then_inc(s_pick, 1)
                    if per:
                        dve.wait_ge(s_pick, it * per + (wait_base + n[0]))
                    else:
                        dve.wait_ge(s_pick, wait_base + n[0])

                for a in range(2):
                    step(dve.tensor_scalar(kcount, kcount, 1.0, None, ALU.add))
                    step(dve.tensor_scalar(onehot, overpos, kcount, None, ALU.is_equal))
                    step(dve.tensor_tensor(picked, again_rows, onehot.unsqueeze(1).to_broadcast([P, 4, NOV]), ALU.mult))
                    step(dve.tensor_reduce(col4[:, :, a], picked, AX, ALU.add))
                return n[0]

            def again(t, a):
                return colr[:, t, a:a + 1], colw[:, t, a:a + 1]

            def take_gathered(n):
                dve.wait_ge(s_gather, n)
                dve.tensor_copy(hg[:, 4:8, :].rearrange("p k c -> p (k c)"), ps[:, 6, :]).then_inc(s_hgv, 1)

            def pair(j, p, used):
                dve.wait_ge(s_silu, p + (j + 1))
                dve.tensor_tensor(act2, sg2, ps[:, 4, 256:512], ALU.mult).then_inc(s_hid2, 1)
                take_gathered(p + (j + 2))
                dve.wait_ge(s_tps, p + (j + 1 + EARLY))
                dve.tensor_copy(probT[:, j, :], ps[:, 7, :]).then_inc(s_tsb, 1)
                dve.wait_ge(s_used, used + (RINGED + 6 * j + 6))
                dve.tensor_copy(yslot[:, 512:1024], ps[:, 6, :]).then_inc(s_yv, 1)

            select_experts(0, fixed_round(0))
            take_gathered(1)
            with dve.Fori(0, STEPS - 1) as it:
                for j in range(2):
                    dve.wait_ge(s_tps, it * 2 + (j + EARLY))
                    select_experts((j + 1) % 2, first_round(it * 4 + (2 * j + 2)))
                    pair(j, it * 2, it * 12)
            last = STEPS - 1
            dve.wait_ge(s_tps, 2 * last + EARLY)
            select_experts(1, fixed_round(NEXP - 2))
            pair(0, 2 * last, 12 * last)
            dve.wait_ge(s_tps, 2 * last + 1 + EARLY)
            picks = pick_again(0, 0, 0)
            select_experts(0, again)
            pair(1, 2 * last, 12 * last)
            dve.wait_ge(s_schedm, 32)
            more = dve.value_load(sched[P:P + 1, :], min_val=1, max_val=MAX_MORE)
            with dve.Fori(0, more) as it:
                for j in range(2):
                    dve.wait_ge(s_tps, it * 2 + (2 * STEPS + j + EARLY))
                    pick_again(picks * (j + 1), it, 2 * picks)
                    select_experts((j + 1) % 2, again)
                    pair(j, it * 2 + 2 * STEPS, it * 12 + 12 * STEPS)
            for q in range(4):
                t, cols = q // 2, slice((q % 2) * 512, (q % 2 + 1) * 512)
                dve.wait_ge(s_moe, q + 1)
                link(dve.tensor_tensor(y[:, t, cols], ps[:, q, :], gaterow[:, 1, cols], ALU.mult))
                i = dve.tensor_tensor(x[:, t, cols], x[:, t, cols], y[:, t, cols], ALU.add)
                if q % 2 == 1:
                    i.then_inc(s_xfin, 1)
            dve.wait_ge(s_xfin, TT)
            dve.wait_ge(s_vecB, 80)
            for t in range(TT):
                inverse_rms(t, t + 6)
                dve.scalar_tensor_tensor(out=x[:, t, :], in0=x[:, t, :], scalar=rstd[:, t:t + 1], in1=vec[:, 2, :],
                                         op0=ALU.mult, op1=ALU.mult).then_inc(s_normed, 1)

        @block.gpsimd
        def _(pool):
            def row(dst, src, s):
                pool.dma_start(dst, src.to_broadcast([P, D])).then_inc(s, 16)

            pool.wait_ge(s_const, 32)
            pool.wait_ge(s_projsb, 1)
            pe3 = R("pe").rearrange("p (j m) -> p j m", j=2)
            for j in range(2):
                for g in range(2):
                    pool.tensor_copy(cmpin[:, j, :, g, :], windows(XS(j), g)).then_inc(s_pool, 1)
                    pool.wait_ge(s_pool, 2 * j + g + 1)
                    pool.tensor_tensor(cmpin[:, j, :, g, :], cmpin[:, j, :, g, :],
                                       pe3[:, j, :].unsqueeze(2).to_broadcast([P, 16, NCMP]), ALU.add).then_inc(s_blk, 1)

            for i in range(2):
                row(vec[:, 2 * i, :], d_gain[0, i:i + 1, :], s_vecB if i else s_vecA)
                row(vec[:, 2 * i + 1, :], d_bias[0, i:i + 1, :], s_vecB if i else s_vecA)

            def start_sums(layer, rows):
                pool.memset(mod_sum, 0.0).then_inc(s_zero, 1)
                pool.wait_ge(s_zero, layer + 1)
                for at, i, n in rows:
                    pool.dma_start(mod_sum[0:1, at * D:(at + n) * D], d_bada[0:1, i * D:(i + n) * D]).then_inc(s_bada, 16)

            def load_modulation(c, n):
                pool.dma_start(mod_slot[c], d_ada[bass.ds(n, 1)].rearrange("o p (k n) -> (o p) k n", k=4)
                               ).then_inc(s_ada[c], 16)

            def load_modulation_later(layer):
                per = MOD_CHUNKS[layer]
                with pool.Fori(1, MLP_STEPS) as it:
                    for c in range(per):
                        pool.wait_ge(s_mod, it * MOD_OPS + (layer * MOD_OPS * MLP_STEPS - MOD_OPS + (c + 1) * MOD_OPS // per))
                        load_modulation(c, it * per + (c + layer * MOD_CHUNKS[0] * MLP_STEPS))

            pool.wait_ge(s_odone, UNITS[INSTANCES["a0"][1] - 1][6] + 1)
            start_sums(0, ((0, 0, 2), (2, 0, 2)))
            for c in range(MOD_CHUNKS[0]):
                pool.dma_start(mod_slot[c], d_ada[c].rearrange("p (k n) -> p k n", k=4)).then_inc(s_ada[c], 16)
            pool.wait_ge(s_normed, 1)
            row(vec[:, 0, :], d_gain[1, 0:1, :], s_vecA)
            row(vec[:, 1, :], d_bias[1, 0:1, :], s_vecA)
            load_modulation_later(0)
            pool.wait_ge(s_normed, 2)
            row(vec[:, 2, :], d_gain[1, 1:2, :], s_vecB)
            row(vec[:, 3, :], d_bias[1, 1:2, :], s_vecB)
            pool.wait_ge(s_fdve, 2)
            pool.dma_start(foxq[65:66, :, :], mix[0:16, 0, 768:1024]).then_inc(s_caug, 16)
            pool.dma_start(foxk[64:65, :, :], mix[0:16, 0, 0:256]).then_inc(s_caug, 16)
            pool.wait_ge(s_odone, UNITS[INSTANCES["a1"][1] - 1][6] + 1)
            pool.dma_start(ctxr, d_ctx.rearrange("(t p) f -> p t f", p=P)).then_inc(s_ctx, 16)
            start_sums(1, ((0, 2, 1), (1, 5, 1), (2, 3, 2)))
            for c in range(MOD_CHUNKS[1]):
                if c == 3:
                    pool.wait_ge(s_ss, 1)
                n = MOD_CHUNKS[0] * MLP_STEPS + c
                pool.dma_start(mod_slot[c], d_ada[n].rearrange("p (k n) -> p k n", k=4)).then_inc(s_ada[c], 16)
            load_modulation_later(1)
            pool.wait_ge(s_normed, 4)
            row(vec[:, 2, :], d_final[0:1, :], s_vecB)
            pool.wait_ge(s_turn, TURN_AT["rms1"] + 4)
            pool.dma_start(poolmat, d_pool).then_inc(s_poolmat, 16)
            pool.wait_ge(s_vecA, 64)
            pool.wait_ge(s_vecB, 80)
            pool.wait_ge(s_sched, 1)
            pool.dma_start(sched[0:P, :], schedi[:, 0:1]).then_inc(s_schedm, 16)
            pool.dma_start(sched[P:P + 1, :], schedi[0:1, 1:2]).then_inc(s_schedm, 16)
            pool.wait_ge(s_schedm, 32)


def rope_tables(positions_and_freqs, rows):
    n = len(positions_and_freqs[0][0])
    cos, sin = np.ones((rows, n)), np.zeros((rows, n))
    for pos, inv, at in positions_and_freqs:
        ang = inv[:, None] * pos[None, :]
        for half in range(2):
            a = at + half * len(inv)
            cos[a:a + len(inv)], sin[a:a + len(inv)] = np.cos(ang), np.sin(ang)
    return cos, sin


def rotation(pairs):
    rot = np.zeros((P, P))
    for at, half in pairs:
        for i in range(half):
            rot[at + i, at + half + i] = -1.0
            rot[at + half + i, at + i] = 1.0
    return rot.T


def shape_constants():
    f = np.float32
    pos = np.arange(T).astype(f)
    inv1 = (f(500000.0) ** (-np.arange(8, dtype=f) / f(8))).astype(f)
    inv2 = (f(10000.0) ** (-np.arange(16, dtype=f) / f(16))).astype(f)
    cpos = (np.arange(NCMP) * 16 + 31).astype(f)
    c1, s1 = rope_tables([(pos, inv1, 0), (pos, inv1, HD)], P)
    cc, sc = rope_tables([(np.tile(cpos, 2), inv1, 0), (np.tile(cpos, 2), inv1, HD)], P)
    row, col = np.arange(T) // 64, np.arange(T) % 64
    c2, s2 = rope_tables([(p.astype(f), inv2, h * HD + o) for h in range(2) for p, o in ((row, 0), (col, 32))], P)
    q = np.arange(T).reshape(TT, P)
    k = np.arange(T)
    causal = np.where(k[None, None] <= q[:, :, None], 0.0, BIG)
    local = np.concatenate([np.where(np.abs(q[:, :, None] - k[None, None]) <= 128, 0.0, BIG), np.zeros((TT, P, T))], 2)
    valid = (np.arange(NCMP) * 16 + 31)[None, None] <= q[:, :, None]
    rows = lambda a: np.moveaxis(a, 0, 1).reshape(P, -1)
    parts = {
        "ident": np.eye(P), "rot1": rotation([(0, 8), (HD, 8)]), "rot2": rotation([(h * 32, 16) for h in range(4)]),
        "cos1": c1, "sin1": s1, "cos2": c2, "sin2": s2, "cosc": cc, "sinc": sc,
        "causal": rows(causal), "local": rows(local), "cmpmask": rows(np.where(valid, 0.0, BIG)),
        "rowvalid": rows(valid.any(2)[:, :, None].astype(f)), "iota8": np.tile(np.arange(8), (P, 1)),
        "iota1": np.tile(np.arange(1, CAP + 1), (P, 1)), "before": np.triu(np.ones((P, P)), 1), "ones": np.ones((P, P)),
        "place1": np.arange(1, P + 1).reshape(P, 1), "expert": np.tile(np.arange(NEXP), (P, ROUNDS)),
        "evens4": np.tile(4 * np.arange(MAX_MORE), (P, 1)),
    }
    consts = np.concatenate([parts[n] for n, _ in CONSTS], 1).astype(f)
    pool = np.zeros((4, T, T))
    for g, w in enumerate(POOL_WINDOWS):
        for t in range(T):
            lo, hi = max(t - w // 2, 0), min(t - w // 2 + w, T)
            pool[g, lo:hi, t] = 1.0 / (hi - lo)
            pool[g, t, t] -= 1.0
    pool = pool.reshape(4, TT, P, T).transpose(2, 0, 1, 3).astype(f)
    return np.ascontiguousarray(consts), np.ascontiguousarray(pool)


def k_major(w):
    return w.reshape(-1, P, w.shape[1]).transpose(1, 0, 2)


def panels(w, width, k_per):
    w = k_major(w)
    return [w[:, k:k + k_per, c:c + width] for c in range(0, w.shape[2], width) for k in range(0, w.shape[1], k_per)]


def lay_out_stream(a):
    chunks = []
    even = a["w_in_even"][0]
    chunks += panels(even[:, 2048:2560], 512, 4) + panels(even[:, 0:1024], 512, 4)
    w1 = [panels(a["nsa_cmp_w1"][0, j], 256, 8) for j in range(2)]
    chunks += [w1[j][c] for c in range(2) for j in range(2)]
    chunks += panels(even[:, 1024:1536], 512, 4) + panels(even[:, 2560:2816], 256, 8) + panels(even[:, 1536:2048], 512, 4)
    for layer in range(2):
        if layer:
            chunks += panels(a["w_in_odd"][0][:, 0:3072], 512, 4)
        chunks += panels(a["w_out_odd" if layer else "w_out_even"][0], 1024, 2)
        up, down = a["mlp_w_up"][layer], a["mlp_w_down"][layer]
        for i in range(MLP_STEPS):
            chunks += panels(up[:, 1024 * i:1024 * (i + 1)], 512, 4) + panels(down[1024 * i:1024 * (i + 1)], 1024, 2)
    w_in = a["w_in_2"][0]
    chunks += panels(w_in[:, 512:768], 256, 8) + panels(w_in[:, 0:512], 512, 4) + panels(w_in[:, 768:1280], 512, 4)
    chunks += panels(a["w_out_2"][0], 1024, 2)
    experts = [(a["ws_gate_2"][0], a["ws_up_2"][0], a["ws_down_2"][0])]
    experts += [(a["w_gate_2"][0, e], a["w_up_2"][0, e], a["w_down_2"][0, e]) for e in range(NEXP)]
    for gate, up, down in experts:
        chunks += panels(np.concatenate([gate, up], 1), 512, 4) + panels(down, 1024, 2)
    stream = np.empty((CHUNKS, P, SLOT), np.float32)
    for n, c in enumerate(chunks):
        stream[n] = c.reshape(P, SLOT)
    return stream


def lay_out_modulation(a):
    w = a["w_ada_2"][0]
    chunks = [c for vectors in MOD_VECTORS for i in vectors for c in panels(w[:, i * D:(i + 1) * D], 512, 4)]
    return np.stack([c.reshape(P, SLOT) for c in chunks])


def lay_out_params(a):
    wide = lambda r: np.tile(r.reshape(1, -1), (P, 1))
    cols = lambda r: r.reshape(-1, P).T
    flat = lambda r: r.reshape(P, -1)
    w2 = a["nsa_cmp_w2"][0]
    fbias = np.zeros((P, 1), np.float32)
    fbias[0:16, 0] = a["fox_f_bias"][0]
    parts = {
        "pe": flat(a["nsa_pe"][0].reshape(2, 16, P).transpose(2, 0, 1)),
        "b1": cols(a["nsa_cmp_b1"][0]),
        "w2k": flat(np.concatenate([k_major(w2[0])] * 2, 2)),
        "w2v": flat(k_major(w2[1])),
        "wgate": flat(k_major(a["w_in_even"][0][:, 2816:2840])),
        "wforget": flat(k_major(a["w_in_odd"][0][:, 3072:3088])),
        "router": flat(k_major(a["w_router_2"][0])),
        "rbias": wide(a["router_bias_2"][0]),
        "poolw": flat(a["pool_w_2"][0].transpose(1, 0, 2)),
        "poolscale": cols(a["pool_scale_2"][0]),
        "cvec": flat(np.stack([cols(a["c_2"][0]), cols(a["c_ctx_2"])], 2)),
        "norm1": cols(a["norm1_g_2"][0]), "norm2": cols(a["norm2_g_2"][0]),
        "sink": wide(a["attn_sink_2"][0]), "lam": wide(a["diff_lambda"][0]), "subln": wide(a["diff_subln"][0]),
        "fbias": fbias,
    }
    return np.ascontiguousarray(np.concatenate([parts[n] for n, _ in PARAMS], 1))


def kernel(**inputs):
    import concourse.bacc as bacc
    from concourse.bass_utils import run_bass_kernel_spmd

    a = {name: np.asarray(value) for name, value in inputs.items()}
    consts, pool = shape_constants()
    arrays = {
        "stream": lay_out_stream(a), "params": lay_out_params(a), "consts": consts, "poolmat": pool,
        "x": np.ascontiguousarray(a["x"][0]), "ctx": np.ascontiguousarray(a["ctx_2"][0]),
        "gain": np.ascontiguousarray(a["ln_gain"]), "bias": np.ascontiguousarray(a["ln_bias"]),
        "ada": lay_out_modulation(a), "bada": np.ascontiguousarray(a["b_ada_2"]),
        "final": np.ascontiguousarray(a["final_g_2"].reshape(1, -1)),
    }
    nc = bacc.Bacc("TRN2", target_bir_lowering=False, num_devices=1)
    aps = [nc.dram_tensor(f"in_{n}", v.shape, F32, kind="ExternalInput").ap() for n, v in arrays.items()]
    out = nc.dram_tensor("out_0", (T, D), F32, kind="ExternalOutput").ap()
    build(nc, *aps, out)
    r = run_bass_kernel_spmd(nc, [{f"in_{n}": v for n, v in arrays.items()}], core_ids=[0])
    return r.results[0]["out_0"].reshape(1, T, D)
```
